# Optimizing a Trainium2 kernel written in Bass

```python
import math, functools
import jax, jax.numpy as jnp
from jax import lax
import numpy as np

D_MODEL = 1024
BATCH = 1
SEQ = 1024
DEPTH = 2

N_MEM = 256
D_MAIN = D_MODEL
N_POOL_GROUPS = 4
POOL_WINDOWS = (2, 4, 8, 16)
POOL_GROUP = D_MAIN // N_POOL_GROUPS
FOX_HEADS = 16
FOX_HEAD_DIM = D_MAIN // FOX_HEADS
MEM_HEADS = 4
MEM_HEAD_DIM = 128
D_MEM = MEM_HEADS * MEM_HEAD_DIM
D_MIX = D_MAIN + D_MEM
D_IN = 2 * D_MIX
N_A = DEPTH // 2
N_B = DEPTH - N_A
Q_BLOCK = 128
ALPHA = (2 * DEPTH) ** 0.25
BETA = (8 * DEPTH) ** -0.25
LN_EPS = 1e-5


def layer_norm(x, g, b):
    xf = x.astype(jnp.float32)
    mu = jnp.mean(xf, axis=-1, keepdims=True)
    var = jnp.mean(jnp.square(xf - mu), axis=-1, keepdims=True)
    y = (xf - mu) * lax.rsqrt(var + LN_EPS) * g.astype(jnp.float32) + b.astype(jnp.float32)
    return y.astype(x.dtype)

def causal_multiscale_pool(u, pool_w, pool_scale):
    B, S, _ = u.shape
    ug = u.reshape(B, S, N_POOL_GROUPS, POOL_GROUP)
    cs = jnp.cumsum(ug.astype(jnp.float32), axis=1)
    cs = jnp.pad(cs, ((0, 0), (1, 0), (0, 0), (0, 0)))
    t = jnp.arange(S)
    outs = []
    for gi, w in enumerate(POOL_WINDOWS):
        c = cs[:, :, gi]
        upper = c[:, 1:]
        lower = jnp.concatenate(
            [jnp.zeros((B, w - 1, POOL_GROUP), jnp.float32), c[:, :S + 1 - w]], axis=1)
        count = jnp.minimum(t + 1, w).astype(jnp.float32)[None, :, None]
        outs.append((upper - lower) / count - ug[:, :, gi].astype(jnp.float32))
    pm = jnp.stack(outs, axis=2).astype(u.dtype)
    mixed = jnp.einsum('bsgc,gcd->bsgd', pm, pool_w)
    return mixed.reshape(B, S, D_MAIN) * pool_scale

def shared_kv(x, w_kv_shared, b_forget):
    B, S, _ = x.shape
    h = x @ w_kv_shared
    k = h[..., :D_MAIN].reshape(B, S, FOX_HEADS, FOX_HEAD_DIM)
    v = h[..., D_MAIN:2 * D_MAIN].reshape(B, S, FOX_HEADS, FOX_HEAD_DIM)
    f_logit = h[..., 2 * D_MAIN:].astype(jnp.float32) + b_forget.astype(jnp.float32)
    log_f = jax.nn.log_sigmoid(f_logit)
    cum = jnp.cumsum(log_f, axis=1)
    return k, v, cum

def forgetting_attention(u, k, v, cum):
    B, S, _ = u.shape
    q = u.reshape(B, S, FOX_HEADS, FOX_HEAD_DIM)
    nb = S // Q_BLOCK
    qb = q.reshape(B, nb, Q_BLOCK, FOX_HEADS, FOX_HEAD_DIM).transpose(1, 0, 2, 3, 4)
    cb = cum.reshape(B, nb, Q_BLOCK, FOX_HEADS).transpose(1, 0, 3, 2)
    cum_k = cum.transpose(0, 2, 1)
    starts = jnp.arange(nb) * Q_BLOCK
    kpos = jnp.arange(S)
    scale = FOX_HEAD_DIM ** -0.5

    def block(args):
        qi, ci, s0 = args
        logits = jnp.einsum('bqhd,bkhd->bhqk', qi, k,
                            preferred_element_type=jnp.float32) * scale
        logits = logits + (ci[..., :, None] - cum_k[:, :, None, :])
        qpos = s0 + jnp.arange(Q_BLOCK)
        mask = kpos[None, :] <= qpos[:, None]
        logits = jnp.where(mask[None, None], logits, -jnp.inf)
        p = jax.nn.softmax(logits, axis=-1)
        return jnp.einsum('bhqk,bkhd->bqhd', p.astype(v.dtype), v)

    out = lax.map(block, (qb, cb, starts))
    return out.transpose(1, 0, 2, 3, 4).reshape(B, S, D_MAIN)

def memory_attention(q_mem, mem, w_mem_kv):
    B, S, _ = q_mem.shape
    M = mem.shape[1]
    mkv = mem @ w_mem_kv
    mk = mkv[..., :D_MEM].reshape(B, M, MEM_HEADS, MEM_HEAD_DIM)
    mv = mkv[..., D_MEM:].reshape(B, M, MEM_HEADS, MEM_HEAD_DIM)
    q = q_mem.reshape(B, S, MEM_HEADS, MEM_HEAD_DIM)
    logits = jnp.einsum('bshd,bmhd->bhsm', q, mk,
                        preferred_element_type=jnp.float32) * (MEM_HEAD_DIM ** -0.5)
    p = jax.nn.softmax(logits, axis=-1)
    return jnp.einsum('bhsm,bmhd->bshd', p.astype(mv.dtype), mv).reshape(B, S, D_MEM)

def mixer_sublayer(x, mem, w_in, w_mem_kv, w_out, main_fn):
    h = x @ w_in
    u_main = h[..., :D_MAIN]
    q_mem = h[..., D_MAIN:D_MIX]
    g_main = h[..., D_MIX:D_MIX + D_MAIN]
    g_mem = h[..., D_MIX + D_MAIN:]
    y_main = main_fn(u_main)
    y_mem = memory_attention(q_mem, mem, w_mem_kv)
    y = jnp.concatenate([y_main * jax.nn.silu(g_main), y_mem * jax.nn.silu(g_mem)], axis=-1)
    return y @ w_out

def first_inputs(seed: int = 0) -> dict:
    key = jax.random.key(seed)
    ks = jax.random.split(key, 12)
    x = jax.random.normal(ks[0], (BATCH, SEQ, D_MODEL), jnp.float32)
    mem = jax.random.normal(ks[1], (BATCH, N_MEM, D_MODEL), jnp.float32)
    w_in = jax.random.normal(ks[2], (DEPTH, D_MODEL, D_IN), jnp.float32) * D_MODEL ** -0.5
    w_mem_kv = jax.random.normal(ks[3], (DEPTH, D_MODEL, 2 * D_MEM), jnp.float32) * D_MODEL ** -0.5
    w_out = jax.random.normal(ks[4], (DEPTH, D_MIX, D_MODEL), jnp.float32) * (D_MIX ** -0.5 * BETA)
    ln_g = 1.0 + 0.02 * jax.random.normal(ks[5], (DEPTH, D_MODEL), jnp.float32)
    ln_b = 0.02 * jax.random.normal(ks[6], (DEPTH, D_MODEL), jnp.float32)
    pool_w = jax.random.normal(ks[7], (N_A, N_POOL_GROUPS, POOL_GROUP, POOL_GROUP), jnp.float32) * POOL_GROUP ** -0.5
    pool_scale = 1.0 + 0.1 * jax.random.normal(ks[8], (N_A, D_MAIN), jnp.float32)
    w_kv_shared = jax.random.normal(ks[9], (D_MODEL, 2 * D_MAIN + FOX_HEADS), jnp.float32) * D_MODEL ** -0.5
    b_forget = jax.random.uniform(ks[10], (FOX_HEADS,), jnp.float32, 1.0, 5.0)
    return {"x": x, "mem": mem, "w_in": w_in, "w_mem_kv": w_mem_kv, "w_out": w_out,
            "ln_g": ln_g, "ln_b": ln_b, "pool_w": pool_w, "pool_scale": pool_scale,
            "w_kv_shared": w_kv_shared, "b_forget": b_forget}

def first_block(x, mem, w_in, w_mem_kv, w_out, ln_g, ln_b, pool_w, pool_scale,
              w_kv_shared, b_forget):
    k_sh = v_sh = cum_sh = None
    for layer in range(DEPTH):
        if layer < N_A:
            main_fn = functools.partial(causal_multiscale_pool,
                                        pool_w=pool_w[layer], pool_scale=pool_scale[layer])
        else:
            if layer == N_A:
                k_sh, v_sh, cum_sh = shared_kv(x, w_kv_shared, b_forget)
            main_fn = functools.partial(forgetting_attention, k=k_sh, v=v_sh, cum=cum_sh)
        y = mixer_sublayer(x, mem, w_in[layer], w_mem_kv[layer], w_out[layer], main_fn)
        x = layer_norm(ALPHA * x + y, ln_g[layer], ln_b[layer])
    return x


DEPTH_2 = 1

MIX_WIDTH = D_MODEL
GMLP_WIDTH = MIX_WIDTH // 2
RWKV_WIDTH = MIX_WIDTH - GMLP_WIDTH
HEAD_DIM = 64
GMLP_HEADS = GMLP_WIDTH // HEAD_DIM
RWKV_HEADS = RWKV_WIDTH // HEAD_DIM
CHUNK = 128
DECAY_LORA = 32
ICLR_LORA = 32
GATE_LORA = 96
RWKV_PROJ = 3 * RWKV_WIDTH + DECAY_LORA + ICLR_LORA + GATE_LORA
IN_WIDTH = 2 * GMLP_WIDTH + RWKV_PROJ
N_GROUPS = 4
EXPERTS_PER_GROUP = 8
N_EXPERTS = N_GROUPS * EXPERTS_PER_GROUP
TOP_K = 2
EXPERT_HIDDEN = 512
MOE_BLOCK = 128
RMS_EPS = 1e-6
GN_EPS = 64e-5


def _rmsnorm(x, g):
    x32 = x.astype(jnp.float32)
    y = x32 * lax.rsqrt(jnp.mean(x32 * x32, axis=-1, keepdims=True) + RMS_EPS)
    return y.astype(x.dtype) * g

def _modulate(h, shift, scale):
    return h * (1 + scale[:, None, :]) + shift[:, None, :]

def _token_shift(z):
    return jnp.pad(z, ((0, 0), (1, 0), (0, 0)))[:, :-1]

def _gmlp_mixer(zu, zv, ln_w, ln_b, ws, bs):
    B, S, _ = zu.shape
    u = jax.nn.gelu(zu)
    v = jax.nn.gelu(zv)
    v32 = v.astype(jnp.float32)
    m = jnp.mean(v32, axis=-1, keepdims=True)
    var = jnp.mean(jnp.square(v32 - m), axis=-1, keepdims=True)
    v = ((v32 - m) * lax.rsqrt(var + LN_EPS)).astype(zu.dtype) * ln_w + ln_b
    vc = v.reshape(B, S // CHUNK, CHUNK, GMLP_HEADS, HEAD_DIM)
    w_causal = jnp.tril(ws)
    mixed = jnp.einsum('hts,bcshd->bcthd', w_causal, vc) + bs.T[None, None, :, :, None]
    return u * mixed.reshape(B, S, GMLP_WIDTH)

def _wkv7_scan(r, w, k, v, a, b):
    Bn, S, H, N = r.shape
    seq = tuple(jnp.moveaxis(t, 1, 0) for t in (r, w, k, v, a, b))

    def step(state, inp):
        r_t, w_t, k_t, v_t, a_t, b_t = inp
        sa = jnp.einsum('bhvk,bhk->bhv', state, a_t)
        state = (state * w_t[:, :, None, :] + sa[..., None] * b_t[:, :, None, :]
                 + v_t[..., None] * k_t[:, :, None, :])
        return state, jnp.einsum('bhvk,bhk->bhv', state, r_t)

    s0 = jnp.zeros((Bn, H, N, N), jnp.float32)
    _, y = lax.scan(step, s0, seq)
    return jnp.moveaxis(y, 0, 1)

def _rwkv7_mixer(z, mu, w0, w2, a0, a2, g2, k_k, k_a, r_k, gn_w, gn_b):
    B, S, _ = z.shape
    f32 = jnp.float32
    z = z + (_token_shift(z) - z) * mu
    W = RWKV_WIDTH
    r, k, v, xw, xa, xg = jnp.split(
        z, [W, 2 * W, 3 * W, 3 * W + DECAY_LORA, 3 * W + DECAY_LORA + ICLR_LORA], axis=-1)
    w_log = -jax.nn.softplus(-(w0 + jnp.tanh(xw) @ w2).astype(f32)) - 0.5
    decay = jnp.exp(-jnp.exp(w_log))
    a = jax.nn.sigmoid(a0 + xa @ a2)
    g = jax.nn.sigmoid(xg) @ g2
    hv = lambda t: t.reshape(B, S, RWKV_HEADS, HEAD_DIM)
    kk = hv(k * k_k).astype(f32)
    kk = kk / jnp.maximum(jnp.sqrt(jnp.sum(kk * kk, axis=-1, keepdims=True)), 1e-12)
    k = k * (1 + (a - 1) * k_a)
    r4, k4, v4, a4 = hv(r), hv(k), hv(v), hv(a)
    y = _wkv7_scan(r4.astype(f32), hv(decay), k4.astype(f32), v4.astype(f32),
                   -kk, kk * a4.astype(f32))
    m = jnp.mean(y, axis=-1, keepdims=True)
    var = jnp.mean(jnp.square(y - m), axis=-1, keepdims=True)
    y = ((y - m) * lax.rsqrt(var + GN_EPS)).reshape(B, S, W).astype(z.dtype) * gn_w + gn_b
    bonus = jnp.sum(r4 * k4 * r_k, axis=-1, keepdims=True) * v4
    return (y + bonus.reshape(B, S, W)) * g

def _hier_moe(h, rg_w, rg_b, re_w, re_b, w_gate, w_up, w_down):
    B, S, D = h.shape
    N = B * S
    f32 = jnp.float32
    ht = h.reshape(N, D)
    group_prob = jax.nn.softmax((ht @ rg_w + rg_b).astype(f32), axis=-1)
    g_p, g_idx = lax.top_k(group_prob, 1)
    exp_logits = (ht @ re_w + re_b).astype(f32).reshape(N, N_GROUPS, EXPERTS_PER_GROUP)
    sel = jnp.take_along_axis(exp_logits, g_idx[:, :, None], axis=1)[:, 0]
    e_p, e_idx = lax.top_k(jax.nn.softmax(sel, axis=-1), TOP_K)
    e_p = e_p / jnp.sum(e_p, axis=-1, keepdims=True)
    weights = g_p * e_p
    expert = g_idx * EXPERTS_PER_GROUP + e_idx
    A = N * TOP_K
    flat_e = expert.reshape(A)
    flat_w = weights.reshape(A)
    flat_tok = jnp.repeat(jnp.arange(N, dtype=jnp.int32), TOP_K)
    order = jnp.argsort(flat_e)
    se, stok, sw = flat_e[order], flat_tok[order], flat_w[order]
    counts = jnp.bincount(flat_e, length=N_EXPERTS)
    padded = (counts + MOE_BLOCK - 1) // MOE_BLOCK * MOE_BLOCK
    pad_end = jnp.cumsum(padded)
    pad_start = pad_end - padded
    start = jnp.cumsum(counts) - counts
    dest = pad_start[se] + jnp.arange(A) - start[se]
    n_blocks = -(-A // MOE_BLOCK) + N_EXPERTS
    P = n_blocks * MOE_BLOCK
    tok_buf = jnp.full((P,), N, jnp.int32).at[dest].set(stok)
    w_buf = jnp.zeros((P,), f32).at[dest].set(sw)
    block_e = jnp.minimum(
        jnp.searchsorted(pad_end, jnp.arange(n_blocks) * MOE_BLOCK, side='right'), N_EXPERTS - 1)
    x_pad = jnp.concatenate([ht, jnp.zeros((1, D), ht.dtype)], axis=0)
    xb = x_pad[tok_buf].reshape(n_blocks, MOE_BLOCK, D)

    def expert_block(args):
        xbk, e = args
        return (jax.nn.silu(xbk @ w_gate[e]) * (xbk @ w_up[e])) @ w_down[e]

    yb = lax.map(expert_block, (xb, block_e)).reshape(P, D)
    y = jnp.zeros((N + 1, D), yb.dtype).at[tok_buf].add(yb * w_buf[:, None].astype(yb.dtype))
    return y[:N].reshape(B, S, D)

def second_inputs(seed: int = 0) -> dict:
    key = jax.random.key(seed)
    ks = jax.random.split(key, 40)
    L, D = DEPTH_2, D_MODEL
    nrm = lambda k, shape, s: jax.random.normal(k, shape, jnp.float32) * s
    uni = lambda k, shape, lo, hi: jax.random.uniform(k, shape, jnp.float32, lo, hi)
    return {
        "x": nrm(ks[0], (BATCH, SEQ, D), 1.0),
        "c": nrm(ks[1], (BATCH, D), 1.0),
        "ada_w": nrm(ks[2], (L, D, 6 * D), 0.3 * D ** -0.5),
        "ada_b": nrm(ks[3], (L, 6 * D), 0.01),
        "norm1_g": 1.0 + nrm(ks[4], (L, D), 0.05),
        "w_in": nrm(ks[5], (L, D, IN_WIDTH), D ** -0.5),
        "gmlp_ln_w": 1.0 + nrm(ks[6], (L, GMLP_WIDTH), 0.05),
        "gmlp_ln_b": nrm(ks[7], (L, GMLP_WIDTH), 0.02),
        "gmlp_ws": nrm(ks[8], (L, GMLP_HEADS, CHUNK, CHUNK), CHUNK ** -0.5),
        "gmlp_bs": 1.0 + nrm(ks[9], (L, GMLP_HEADS, CHUNK), 0.1),
        "rwkv_mu": uni(ks[10], (L, RWKV_PROJ), 0.0, 1.0),
        "rwkv_w0": uni(ks[11], (L, RWKV_WIDTH), -6.0, 0.0),
        "rwkv_w2": nrm(ks[12], (L, DECAY_LORA, RWKV_WIDTH), 0.1),
        "rwkv_a0": nrm(ks[13], (L, RWKV_WIDTH), 0.5),
        "rwkv_a2": nrm(ks[14], (L, ICLR_LORA, RWKV_WIDTH), ICLR_LORA ** -0.5),
        "rwkv_g2": nrm(ks[15], (L, GATE_LORA, RWKV_WIDTH), GATE_LORA ** -0.5),
        "rwkv_k_k": 0.85 + nrm(ks[16], (L, RWKV_WIDTH), 0.05),
        "rwkv_k_a": 1.0 + nrm(ks[17], (L, RWKV_WIDTH), 0.05),
        "rwkv_r_k": nrm(ks[18], (L, RWKV_HEADS, HEAD_DIM), 0.1),
        "rwkv_gn_w": 1.0 + nrm(ks[19], (L, RWKV_WIDTH), 0.05),
        "rwkv_gn_b": nrm(ks[20], (L, RWKV_WIDTH), 0.02),
        "w_out": nrm(ks[21], (L, MIX_WIDTH, D), MIX_WIDTH ** -0.5),
        "norm2_g": 1.0 + nrm(ks[22], (L, D), 0.05),
        "router_group_w": nrm(ks[23], (L, D, N_GROUPS), D ** -0.5),
        "router_group_b": nrm(ks[24], (L, N_GROUPS), 0.01),
        "router_expert_w": nrm(ks[25], (L, D, N_EXPERTS), D ** -0.5),
        "router_expert_b": nrm(ks[26], (L, N_EXPERTS), 0.01),
        "moe_w_gate": nrm(ks[27], (L, N_EXPERTS, D, EXPERT_HIDDEN), D ** -0.5),
        "moe_w_up": nrm(ks[28], (L, N_EXPERTS, D, EXPERT_HIDDEN), D ** -0.5),
        "moe_w_down": nrm(ks[29], (L, N_EXPERTS, EXPERT_HIDDEN, D), EXPERT_HIDDEN ** -0.5),
        "final_norm_g": 1.0 + nrm(ks[30], (D,), 0.05),
    }

def second_block(x, c, ada_w, ada_b, norm1_g, w_in, gmlp_ln_w, gmlp_ln_b, gmlp_ws, gmlp_bs,
              rwkv_mu, rwkv_w0, rwkv_w2, rwkv_a0, rwkv_a2, rwkv_g2, rwkv_k_k, rwkv_k_a,
              rwkv_r_k, rwkv_gn_w, rwkv_gn_b, w_out, norm2_g, router_group_w, router_group_b,
              router_expert_w, router_expert_b, moe_w_gate, moe_w_up, moe_w_down,
              final_norm_g):
    for l in range(DEPTH_2):
        mod = c @ ada_w[l] + ada_b[l]
        shift1, scale1, gate1, shift2, scale2, gate2 = jnp.split(mod, 6, axis=-1)
        h = _modulate(_rmsnorm(x, norm1_g[l]), shift1, scale1)
        z = h @ w_in[l]
        zu, zv, zr = jnp.split(z, [GMLP_WIDTH, 2 * GMLP_WIDTH], axis=-1)
        y_a = _gmlp_mixer(zu, zv, gmlp_ln_w[l], gmlp_ln_b[l], gmlp_ws[l], gmlp_bs[l])
        y_b = _rwkv7_mixer(zr, rwkv_mu[l], rwkv_w0[l], rwkv_w2[l], rwkv_a0[l], rwkv_a2[l],
                           rwkv_g2[l], rwkv_k_k[l], rwkv_k_a[l], rwkv_r_k[l],
                           rwkv_gn_w[l], rwkv_gn_b[l])
        y = jnp.concatenate([y_a, y_b], axis=-1) @ w_out[l]
        x = x + gate1[:, None, :] * y
        h = _modulate(_rmsnorm(x, norm2_g[l]), shift2, scale2)
        y = _hier_moe(h, router_group_w[l], router_group_b[l], router_expert_w[l],
                      router_expert_b[l], moe_w_gate[l], moe_w_up[l], moe_w_down[l])
        x = x + gate2[:, None, :] * y
    return _rmsnorm(x, final_norm_g)


def setup_inputs(seed=0):
    out = dict(first_inputs(seed))
    for name, value in second_inputs(seed + 1).items():
        if name != "x":
            out[name + "_2"] = value
    return out


def reference(
    x, mem, w_in, w_mem_kv, w_out, ln_g, ln_b, pool_w, pool_scale, w_kv_shared, b_forget, c_2,
    ada_w_2, ada_b_2, norm1_g_2, w_in_2, gmlp_ln_w_2, gmlp_ln_b_2, gmlp_ws_2, gmlp_bs_2,
    rwkv_mu_2, rwkv_w0_2, rwkv_w2_2, rwkv_a0_2, rwkv_a2_2, rwkv_g2_2, rwkv_k_k_2, rwkv_k_a_2,
    rwkv_r_k_2, rwkv_gn_w_2, rwkv_gn_b_2, w_out_2, norm2_g_2, router_group_w_2,
    router_group_b_2, router_expert_w_2, router_expert_b_2, moe_w_gate_2, moe_w_up_2,
    moe_w_down_2, final_norm_g_2,
):
    x = first_block(
        x, mem, w_in, w_mem_kv, w_out, ln_g, ln_b, pool_w, pool_scale, w_kv_shared, b_forget,
    )
    return second_block(
        x, c_2, ada_w_2, ada_b_2, norm1_g_2, w_in_2, gmlp_ln_w_2, gmlp_ln_b_2, gmlp_ws_2,
        gmlp_bs_2, rwkv_mu_2, rwkv_w0_2, rwkv_w2_2, rwkv_a0_2, rwkv_a2_2, rwkv_g2_2, rwkv_k_k_2,
        rwkv_k_a_2, rwkv_r_k_2, rwkv_gn_w_2, rwkv_gn_b_2, w_out_2, norm2_g_2, router_group_w_2,
        router_group_b_2, router_expert_w_2, router_expert_b_2, moe_w_gate_2, moe_w_up_2,
        moe_w_down_2, final_norm_g_2,
    )


_drawn_inputs = setup_inputs


def setup_inputs(seed=0):
    import zlib

    import numpy as np

    out = dict(_drawn_inputs(seed))
    spreads = {}
    factors = {'mem': 2.888,
     'w_mem_kv': 2.747,
     'pool_scale': 3.359,
     'ada_b_2': 4.137,
     'norm1_g_2': 3.245,
     'gmlp_ln_w_2': 8.0,
     'gmlp_ln_b_2': 8.0,
     'gmlp_bs_2': 3.234,
     'rwkv_w2_2': 8.0,
     'rwkv_k_k_2': 21.809,
     'rwkv_k_a_2': 4.827,
     'rwkv_gn_w_2': 8.0,
     'rwkv_gn_b_2': 39.903,
     'norm2_g_2': 3.248,
     'router_group_b_2': 8.0,
     'router_expert_b_2': 25.15}
    for name, (base, spread) in spreads.items():
        noise = np.random.default_rng([zlib.crc32(name.encode()), seed]).standard_normal(out[name].shape)
        drawn = base * np.exp(spread * noise) if base else spread * noise
        out[name] = __import__('jax').numpy.asarray(drawn.astype(out[name].dtype))
    for name, factor in factors.items():
        out[name] = (out[name] * factor).astype(out[name].dtype)
    return out
```

```python
import math
from contextlib import ExitStack

import concourse.bass as bass
from concourse import mybir

F32 = mybir.dt.float32
F32R = mybir.dt.float32r
I32 = mybir.dt.int32
U32 = mybir.dt.uint32
ALU = mybir.AluOpType
ACT = mybir.ActivationFunctionType
X = mybir.AxisListType.X

P = 128
D = 1024
S = 1024
NT = S // P
ND = D // P
HALF = 512
NH = S // HALF
DEPTH = 2
ALPHA = (2 * DEPTH) ** 0.25
LN_EPS = 1e-5
RMS_EPS = 1e-6
GN_EPS = 64e-5
N_MEM = 256
NM = N_MEM // P
MEM_HEADS = 4
MEM_SCALE = 128.0 ** -0.5
NY = ND + MEM_HEADS
GATE0 = NY
POOL_WINDOWS = (2, 4, 8, 16)
PAD = 16
FOX_HEADS = 16
FOX_SCALE = 64.0 ** -0.5
MASKED = -1.0e30


class Ring:

    def __init__(self, banks, full, free):
        self.banks, self.full, self.free = banks, full, free
        self.n, self.at = 0, {}

    def take(self, key):
        self.at[key] = self.n
        self.n += 1
        before = self.n - len(self.banks)
        return self.banks[self.at[key] % len(self.banks)], (before if before > 0 else None)

    def nth(self, key):
        return self.at[key] + 1

    def bank(self, key):
        return self.banks[self.at[key] % len(self.banks)]


class Slots:

    def __init__(self, slots, landed):
        self.slots, self.landed, self.at = slots, landed, {}

    def load(self, key):
        n = len(self.at)
        self.at[key] = n
        return self.slots[n % len(self.slots)], self.landed[n % len(self.slots)], n

    def get(self, key):
        n = self.at[key]
        k = len(self.slots)
        return self.slots[n % k], self.landed[n % k], 16 * (n // k + 1)


class Chain:

    def __init__(self, sem):
        self.sem, self.n = sem, 0

    def __call__(self, eng, ins):
        ins.then_inc(self.sem, 1)
        self.n += 1
        eng.wait_ge(self.sem, self.n)


class Env:

    def __init__(self, nc, ctx):
        self.nc, self.ctx = nc, ctx
        self.of_stage = None

    def sem(self, name):
        if self.of_stage is None:
            return self.ctx.enter_context(self.nc.semaphore(name))
        self.of_stage.append(self.nc.alloc_semaphore(name=name))
        return self.of_stage[-1]

    def run(self, stage, *args, **options):
        self.of_stage = []
        stage(self.nc, self, *args, **options)
        self.nc.clear_and_free_semaphores(self.of_stage)
        self.nc.all_engine_barrier()
        self.of_stage = None

    def sb(self, name, shape, dt=F32, ctx=None, **options):
        return (ctx or self.ctx).enter_context(self.nc.sbuf_tensor(name, shape, dt, **options))


def wait(eng, sem, value):
    if value is not None and value > 0:
        eng.wait_ge(sem, value)


class SplitX:

    def __init__(self, nc, E, name):
        self.nc, self.E = nc, E
        self.hi_set = E.sem(name + "_x_hi_set")

    def round(self, act):
        for d in range(ND):
            self.nc.scalar.copy(self.E.x_hi[:, d, :], self.E.xT[:, d, :]).then_inc(self.hi_set, 1)

    def rest(self, dve):
        E = self.E
        for d in range(ND):
            dve.wait_ge(self.hi_set, d + 1)
            self.nc.vector.tensor_tensor(E.x_lo[:, d, :], E.xT[:, d, :], E.x_hi[:, d, :].bitcast(F32), ALU.subtract)


class SplitProducts:

    def __init__(self, nc, E, name, st, used):
        self.nc, self.E, self.used = nc, E, used
        self.slots = [E.sb(f"{name}_{i}", [P, ND, P], ctx=st) for i in range(2)]
        self.landed = [E.sem(f"{name}_landed{i}") for i in range(2)]
        self.hi, self.lo = ([E.sb(f"{name}_{x}{i}", [P, ND, P], F32R, ctx=st) for i in range(2)] for x in ("hi", "lo"))
        self.hi_set, self.split = E.sem(name + "_hi_set"), E.sem(name + "_split")

    def load(self, sp, n, src):
        if n >= 2:
            sp.wait_ge(self.split, n - 1)
        sp.dma_start(self.slots[n % 2][:], src).then_inc(self.landed[n % 2], 16)

    def split_weights(self, pool, count):
        for n in range(count):
            b = n % 2
            if n >= 2:
                self.used(pool, n - 2)
            pool.wait_ge(self.landed[b], 16 * (n // 2 + 1))
            self.nc.gpsimd.tensor_copy(self.hi[b][:], self.slots[b][:]).then_inc(self.hi_set, 1)
            pool.wait_ge(self.hi_set, n + 1)
            self.nc.gpsimd.tensor_tensor(self.lo[b][:], self.slots[b][:], self.hi[b][:].bitcast(F32), ALU.subtract).then_inc(self.split, 1)

    def project(self, pe, bank, n, hf):
        E, cols = self.E, slice(hf * HALF, (hf + 1) * HALF)
        pe.wait_ge(self.split, n + 1)
        hi, lo = self.hi[n % 2], self.lo[n % 2]
        for d in range(ND):
            self.nc.tensor.matmul(bank[:], hi[:, d, :], E.x_hi[:, d, cols], start=(d == 0), stop=False)
            self.nc.tensor.matmul(bank[:], hi[:, d, :], E.x_lo[:, d, cols], start=False, stop=False)
            last = self.nc.tensor.matmul(bank[:], lo[:, d, :], E.x_hi[:, d, cols], start=False, stop=(d == ND - 1))
        return last


def stage_constants(nc, E, A):
    with ExitStack() as st:
        mem_rows = E.sb("mem_rows", [P, NM, D], ctx=st)
        x_rows = E.sb("x_rows", [P, NT, D], ctx=st)
        x_landed = E.sem("x_landed")
        x_landed2 = E.sem("x_landed2")
        mem_landed = E.sem("mem_landed")
        id_set = E.sem("id_set")
        turned = Ring(E.banks[0:4], E.sem("turn_full"), E.sem("turn_free"))
        turned2 = Ring(E.banks[4:8], E.sem("turn2_full"), E.sem("turn2_free"))
        small_landed = E.sem("small_landed")
        const_set = E.sem("const_set")
        groups = [("mem", m, h) for m in range(NM) for h in range(2)]
        groups += [("x", t, h) for t in range(NT) for h in range(2)]

        with nc.Block() as block:

            @block.sync
            def _(sp):
                sp.dma_start(mem_rows[:], A["mem"].rearrange("o (m p) d -> p (o m) d", p=P)).then_inc(mem_landed, 16)
                xv = A["x"].rearrange("o (t p) d -> p (o t) d", p=P)
                sp.dma_start(x_rows[:, 0:4, :], xv[:, 0:4, :]).then_inc(x_landed, 16)
                sp.dma_start(x_rows[:, 4:8, :], xv[:, 4:8, :]).then_inc(x_landed2, 16)
                sp.dma_start(E.pool_scale[:], A["pool_scale_cols"]).then_inc(small_landed, 16)
                sp.dma_start(E.b_forget[:], A["b_forget"].rearrange("(h o) -> h o", o=1)).then_inc(small_landed, 16)
                sp.wait_ge(small_landed, 32)

            @block.gpsimd
            def _(pool):
                nc.gpsimd.memset(E.ident[:], 0.0).then_inc(id_set, 1)
                nc.gpsimd.memset(E.causal[:], 0.0).then_inc(id_set, 1)
                pool.wait_ge(id_set, 2)
                nc.gpsimd.affine_select(out=E.ident[:], in_=E.ident[:], compare_op=ALU.not_equal, fill=1.0, base=0,
                                        pattern=[[-1, P]], channel_multiplier=1).then_inc(id_set, 1)
                nc.gpsimd.affine_select(out=E.causal[:], in_=E.causal[:], compare_op=ALU.is_ge, fill=MASKED, base=0,
                                        pattern=[[-1, P]], channel_multiplier=1).then_inc(id_set, 1)
                for g, w in enumerate(POOL_WINDOWS):
                    nc.gpsimd.iota(E.icount[:, g, :], pattern=[[1, PAD]], base=1, channel_multiplier=0,
                                   allow_small_or_imprecise_dtypes=True).then_inc(const_set, 1)

            @block.tensor
            def _(pe):
                pe.wait_ge(id_set, 4)
                for n, (what, t, h) in enumerate(groups):
                    if what == "mem" and n == 0:
                        pe.wait_ge(mem_landed, 16)
                    if what == "x" and h == 0 and t == 0:
                        pe.wait_ge(x_landed, 16)
                    if what == "x" and h == 0 and t == 4:
                        pe.wait_ge(x_landed2, 16)
                    ring = turned if n % 2 == 0 else turned2
                    bank, free = ring.take(n)
                    wait(pe, ring.free, free)
                    rows = mem_rows if what == "mem" else x_rows
                    for c in range(4):
                        last = nc.tensor.transpose(bank[:, c * P:(c + 1) * P], rows[:, t, (4 * h + c) * P:(4 * h + c + 1) * P], E.ident[:])
                    last.then_inc(ring.full, 1)

            def evacuate(eng, copy, ring, parity):
                for n, (what, t, h) in enumerate(groups):
                    if n % 2 != parity:
                        continue
                    eng.wait_ge(ring.full, ring.nth(n))
                    to = E.memT if what == "mem" else E.xT
                    copy(to[:, 4 * h:4 * h + 4, t * P:(t + 1) * P],
                         ring.bank(n).rearrange("p (c n) -> p c n", c=4)).then_inc(ring.free, 1)

            @block.scalar
            def _(act):
                evacuate(act, nc.scalar.copy, turned, 0)

            @block.vector
            def _(dve):
                link = Chain(E.dve_chain)
                link.n = E.chain_n
                dve.wait_ge(const_set, len(POOL_WINDOWS))
                for g, w in enumerate(POOL_WINDOWS):
                    link(dve, nc.vector.tensor_scalar(E.icount[:, g, :], E.icount[:, g, :], float(w), None, ALU.min))
                link(dve, nc.vector.reciprocal(E.icount[:], E.icount[:]))
                link(dve, nc.vector.memset(E.ones[:], 1.0))
                link(dve, nc.vector.memset(E.eps_ln[:], LN_EPS))
                link(dve, nc.vector.memset(E.eps_rms[:], RMS_EPS))
                link(dve, nc.vector.memset(E.eps_gn[:], GN_EPS))
                evacuate(dve, nc.vector.tensor_copy, turned2, 1)
                E.chain_n = link.n


def stage_memory_kv(nc, E, A, layer, split_x=False):
    with ExitStack() as st:
        halves = [E.sb(f"mkv_w{layer}_{i}", [P, ND, HALF], ctx=st) for i in range(2)]
        landed = [E.sem(f"mkv_landed{layer}_{i}") for i in range(2)]
        ring = Ring(E.banks, E.sem(f"mkv_full{layer}"), E.sem(f"mkv_free{layer}"))
        wv = A["w_mem_kv"][layer].rearrange("(c p) n -> p c n", p=P)
        split = SplitX(nc, E, "kv") if split_x else None
        with nc.Block() as block:

            @block.sync
            def _(sp):
                for i in range(2):
                    sp.dma_start(halves[i][:], wv[:, :, i * HALF:(i + 1) * HALF]).then_inc(landed[i], 16)

            @block.tensor
            def _(pe):
                pe.wait_ge(landed[0], 16)
                for h in range(MEM_HEADS):
                    bank, _ = ring.take(("k", h))
                    for c in range(ND):
                        last = nc.tensor.matmul(bank[:, 0:N_MEM], halves[0][:, c, h * P:(h + 1) * P], E.memT[:, c, :],
                                                start=(c == 0), stop=(c == ND - 1))
                    last.then_inc(ring.full, 1)
                pe.wait_ge(landed[1], 16)
                for m in range(NM):
                    bank, _ = ring.take(("v", m))
                    for c in range(ND):
                        last = nc.tensor.matmul(bank[:], E.memT[:, c, m * P:(m + 1) * P], halves[1][:, c, :],
                                                start=(c == 0), stop=(c == ND - 1))
                    last.then_inc(ring.full, 1)

            @block.scalar
            def _(act):
                if split:
                    split.round(act)
                for h in range(MEM_HEADS):
                    act.wait_ge(ring.full, ring.nth(("k", h)))
                    nc.scalar.copy(E.mkT[:, h, :], ring.bank(("k", h))[:, 0:N_MEM])
                for m in range(NM):
                    act.wait_ge(ring.full, ring.nth(("v", m)))
                    nc.scalar.copy(E.mv[:, m, :], ring.bank(("v", m))[:])

            @block.vector
            def _(dve):
                if split:
                    split.rest(dve)


def stage_split_x(nc, E, A):
    split = SplitX(nc, E, "x")
    with nc.Block() as block:

        @block.scalar
        def _(act):
            split.round(act)

        @block.vector
        def _(dve):
            split.rest(dve)


class MemoryAttention:

    def __init__(self, nc, E, layer, ringA, ringD, st):
        self.nc, self.E, self.ringA, self.ringD = nc, E, ringA, ringD
        n = f"{layer}"
        self.probs = E.sb("mem_probs" + n, [P, NT, N_MEM], ctx=st)
        self.probsT = E.sb("mem_probsT" + n, [P, NM, S], ctx=st)
        self.top = E.sb("mem_top" + n, [P, NT], ctx=st)
        self.bias = E.sb("mem_bias" + n, [P, NT], ctx=st)
        self.total = E.sb("mem_total" + n, [P, NT], ctx=st)
        self.inv = E.sb("mem_inv" + n, [P, NT], ctx=st)
        self.bias_set = E.sem("mem_bias_set" + n)
        self.scaled = E.sem("mem_scaled" + n)

    def scores(self, pe, h, qT):
        nc, ring = self.nc, self.ringA
        for tp in range(NT // 2):
            bank, free = ring.take(("s", h, tp))
            wait(pe, ring.free, free)
            for j in range(2):
                t = 2 * tp + j
                last = nc.tensor.matmul(bank[:, j * N_MEM:(j + 1) * N_MEM], qT[:, t * P:(t + 1) * P], self.E.mkT[:, h, :],
                                        start=True, stop=True)
            last.then_inc(ring.full, 1)

    def turn(self, pe, h):
        nc, ring = self.nc, self.ringA
        for tp in range(NT // 2):
            bank, free = ring.take(("t", h, tp))
            wait(pe, ring.free, free)
            pe.wait_ge(self.scaled, h * (NT // 2) + tp + 1)
            for m in range(NM):
                for j in range(2):
                    last = nc.tensor.transpose(bank[:, (2 * m + j) * P:(2 * m + j + 1) * P],
                                               self.probs[:, 2 * tp + j, m * P:(m + 1) * P], self.E.ident[:])
            last.then_inc(ring.full, 1)

    def values(self, pe, h):
        nc, ring = self.nc, self.ringD
        pe.wait_ge(self.ringA.free, self.ringA.nth(("t", h, NT // 2 - 1)))
        for hf in range(NH):
            bank, free = ring.take(("o", h, hf))
            wait(pe, ring.free, free)
            for m in range(NM):
                last = nc.tensor.matmul(bank[:], self.E.mv[:, m, h * P:(h + 1) * P], self.probsT[:, m, hf * HALF:(hf + 1) * HALF],
                                        start=(m == 0), stop=(m == NM - 1))
            last.then_inc(ring.full, 1)

    def maxima(self, dve, link, h):
        nc, ring = self.nc, self.ringA
        for tp in range(NT // 2):
            dve.wait_ge(ring.full, ring.nth(("s", h, tp)))
            tt = slice(2 * tp, 2 * tp + 2)
            if h > 0:
                dve.wait_ge(ring.free, ring.nth(("s", h - 1, tp)))
            link(dve, nc.vector.tensor_reduce(self.top[:, tt], ring.bank(("s", h, tp)).rearrange("p (j n) -> p j n", j=2), X, ALU.max))
            nc.vector.tensor_scalar(self.bias[:, tt], self.top[:, tt], -MEM_SCALE, None, ALU.mult).then_inc(self.bias_set, 1)

    def normalise(self, dve, link, h):
        nc = self.nc
        for tp in range(NT // 2):
            dve.wait_ge(self.ringA.free, self.ringA.nth(("s", h, tp)))
            tt = slice(2 * tp, 2 * tp + 2)
            link(dve, nc.vector.reciprocal(self.inv[:, tt], self.total[:, tt]))
            nc.vector.tensor_scalar(self.probs[:, 2 * tp, :], self.probs[:, 2 * tp, :], self.inv[:, 2 * tp:2 * tp + 1], None, ALU.mult)
            nc.vector.tensor_scalar(self.probs[:, 2 * tp + 1, :], self.probs[:, 2 * tp + 1, :], self.inv[:, 2 * tp + 1:2 * tp + 2], None,
                                    ALU.mult).then_inc(self.scaled, 1)

    def gate(self, dve, h):
        nc, ring = self.nc, self.ringD
        for hf in range(NH):
            dve.wait_ge(ring.full, ring.nth(("o", h, hf)))
            cols = slice(hf * HALF, (hf + 1) * HALF)
            nc.vector.tensor_tensor(self.E.yT[:, ND + h, cols], ring.bank(("o", h, hf))[:], self.E.yT[:, ND + h, cols], ALU.mult).then_inc(ring.free, 1)

    def exps(self, act, h):
        nc, ring = self.nc, self.ringA
        for tp in range(NT // 2):
            act.wait_ge(self.bias_set, h * (NT // 2) + tp + 1)
            if h > 0:
                act.wait_ge(ring.full, ring.nth(("t", h - 1, tp)))
            for j in range(2):
                t = 2 * tp + j
                last = nc.scalar.activation(self.probs[:, t, :], ring.bank(("s", h, tp))[:, j * N_MEM:(j + 1) * N_MEM], ACT.Exp,
                                            bias=self.bias[:, t:t + 1], scale=MEM_SCALE, accum_out=self.total[:, t:t + 1])
            last.then_inc(ring.free, 1)

    def evacuate(self, act, h):
        nc, ring = self.nc, self.ringA
        for tp in range(NT // 2):
            act.wait_ge(ring.full, ring.nth(("t", h, tp)))
            if h > 0 and tp == 0:
                act.wait_ge(self.ringD.full, self.ringD.nth(("o", h - 1, NH - 1)))
            nc.scalar.copy(self.probsT[:, :, tp * 2 * P:(tp + 1) * 2 * P],
                           ring.bank(("t", h, tp)).rearrange("p (m n) -> p m n", m=NM)).then_inc(ring.free, 1)


def stage_layer0(nc, E, A):
    with ExitStack() as st:
        pool_w = [E.sb(f"pool_w{i}", [P, 2, 256], ctx=st) for i in range(2)]
        pool_w_landed = [E.sem(f"pool_w_landed{i}") for i in range(2)]
        uT = [E.sb(f"uT{c}", [P, PAD + S], ctx=st) for c in range(2)]
        qT = E.sb("qT0", [P, S], ctx=st)
        sums = [E.sb(f"sums{c}", [P, PAD + S], ctx=st) for c in range(2)]
        pm = [E.sb(f"pm{c}", [P, S], ctx=st) for c in range(2)]
        edge = E.sb("edge", [P, PAD], ctx=st)
        ringA = Ring(E.banks[0:4], E.sem("l0A_full"), E.sem("l0A_free"))
        ringD = Ring(E.banks[4:8], E.sem("l0D_full"), E.sem("l0D_free"))
        pm_set = E.sem("pm_set")
        attn = MemoryAttention(nc, E, 0, ringA, ringD, st)
        win = A["w_in"][0].rearrange("(c p) n -> p c n", p=P)
        G = len(POOL_WINDOWS)
        order = []
        for g in range(G):
            order += [("u", 0, 2 * g), ("u", 1, 2 * g + 1), ("g", 0, GATE0 + 2 * g), ("g", 1, GATE0 + 2 * g + 1),
                      ("q", 0, ND + g), ("m", 0, GATE0 + ND + g)]

        def used(eng, n):
            kind, c, _ = order[n]
            ring = ringD if kind in "uq" else ringA
            eng.wait_ge(ring.full, ring.nth((kind, n // 6, c, NH - 1)))

        split = SplitProducts(nc, E, "w0", st, used)

        def evacuate_dve(dve, g):
            for kind, c in (("u", 0), ("u", 1), ("q", 0)):
                for hf in range(NH):
                    key = (kind, g, c, hf)
                    dve.wait_ge(ringD.full, ringD.nth(key))
                    if kind == "u":
                        to = uT[c][:, PAD + hf * HALF:PAD + (hf + 1) * HALF]
                    else:
                        if g > 0 and hf == 0:
                            dve.wait_ge(ringA.full, ringA.nth(("s", g - 1, NT // 2 - 1)))
                        to = qT[:, hf * HALF:(hf + 1) * HALF]
                    nc.vector.tensor_copy(to, ringD.bank(key)[:]).then_inc(ringD.free, 1)

        with nc.Block() as block:

            @block.tensor
            def _(pe):
                def project(g):
                    for kind, c, col in order[6 * g:6 * g + 6]:
                        n = 6 * g + (("u", "u", "g", "g", "q", "m").index(kind) + (c if kind in "ug" else 0))
                        ring = ringD if kind in "uq" else ringA
                        for hf in range(NH):
                            bank, free = ring.take((kind, g, c, hf))
                            wait(pe, ring.free, free)
                            split.project(pe, bank, n, hf).then_inc(ring.full, 1)

                project(0)
                for g in range(G):
                    pe.wait_ge(ringD.free, ringD.nth(("q", g, 0, 1)))
                    attn.scores(pe, g, qT)
                    if g + 1 < G:
                        project(g + 1)
                    pe.wait_ge(pm_set, 2 * (g + 1))
                    pe.wait_ge(pool_w_landed[g % 2], 16 * (g // 2 + 1))
                    for c in range(2):
                        for hf in range(NH):
                            bank, free = ringD.take(("mix", g, c, hf))
                            wait(pe, ringD.free, free)
                            for k in range(2):
                                last = nc.tensor.matmul(bank[:], pool_w[g % 2][:, k, c * P:(c + 1) * P], pm[k][:, hf * HALF:(hf + 1) * HALF],
                                                        start=(k == 0), stop=(k == 1))
                            last.then_inc(ringD.full, 1)
                    attn.turn(pe, g)
                    attn.values(pe, g)

            @block.sync
            def _(sp):
                for n, (kind, c, col) in enumerate(order):
                    split.load(sp, n, win[:, :, col * P:(col + 1) * P])
                    if n % 6 == 1:
                        g = n // 6
                        if g > 1:
                            sp.wait_ge(ringD.full, ringD.nth(("mix", g - 2, 1, NH - 1)))
                        sp.dma_start(pool_w[g % 2][:], A["pool_w"][0, g].rearrange("(k p) d -> p k d", p=P)).then_inc(pool_w_landed[g % 2], 16)

            @block.gpsimd
            def _(pool):
                split.split_weights(pool, len(order))

            @block.scalar
            def _(act):
                def gates(g):
                    for kind, c in (("g", 0), ("g", 1), ("m", 0)):
                        for hf in range(NH):
                            key = (kind, g, c, hf)
                            act.wait_ge(ringA.full, ringA.nth(key))
                            to = E.yT[:, 2 * g + c if kind == "g" else ND + g, :]
                            nc.scalar.activation(to[:, hf * HALF:(hf + 1) * HALF], ringA.bank(key)[:], ACT.Silu).then_inc(ringA.free, 1)

                gates(0)
                for g in range(G):
                    attn.exps(act, g)
                    if g + 1 < G:
                        gates(g + 1)
                    attn.evacuate(act, g)

            @block.vector
            def _(dve):
                link = Chain(E.dve_chain)
                link.n = E.chain_n
                for c in range(2):
                    link(dve, nc.vector.memset(uT[c][:, 0:PAD], 0.0))
                    link(dve, nc.vector.memset(sums[c][:, 0:PAD], 0.0))

                def pool_mean(g, c):
                    u = uT[c]
                    before, at = u, 0
                    step = 1
                    while step < POOL_WINDOWS[g]:
                        to = sums[at]
                        link(dve, nc.vector.tensor_tensor(to[:, PAD:PAD + S], before[:, PAD:PAD + S], before[:, PAD - step:PAD + S - step], ALU.add))
                        before, at, step = to, 1 - at, 2 * step
                    if g > 0 and c == 0:
                        dve.wait_ge(ringD.full, ringD.nth(("mix", g - 1, 1, NH - 1)))
                    nc.vector.scalar_tensor_tensor(pm[c][:, PAD:S], before[:, 2 * PAD:PAD + S], 1.0 / POOL_WINDOWS[g], u[:, 2 * PAD:PAD + S],
                                                   ALU.mult, ALU.subtract)
                    link(dve, nc.vector.tensor_tensor(edge[:], before[:, PAD:2 * PAD], E.icount[:, g, :], ALU.mult))
                    link(dve, nc.vector.tensor_tensor(pm[c][:, 0:PAD], edge[:], u[:, PAD:2 * PAD], ALU.subtract))
                    dve.sem_inc(pm_set, 1)

                evacuate_dve(dve, 0)
                for g in range(G):
                    attn.maxima(dve, link, g)
                    attn.normalise(dve, link, g)
                    dve.wait_ge(ringD.free, ringD.nth(("u", g, 1, NH - 1)))
                    pool_mean(g, 0)
                    pool_mean(g, 1)
                    if g + 1 < G:
                        evacuate_dve(dve, g + 1)
                    for c in range(2):
                        for hf in range(NH):
                            key = ("mix", g, c, hf)
                            cols = slice(hf * HALF, (hf + 1) * HALF)
                            dve.wait_ge(ringD.full, ringD.nth(key))
                            dve.wait_ge(ringA.free, ringA.nth(("g", g, c, hf)))
                            nc.vector.scalar_tensor_tensor(E.yT[:, 2 * g + c, cols], ringD.bank(key)[:], E.pool_scale[:, 2 * g + c:2 * g + c + 1],
                                                           E.yT[:, 2 * g + c, cols], ALU.mult, ALU.mult).then_inc(ringD.free, 1)
                    dve.wait_ge(ringA.free, ringA.nth(("m", g, 0, NH - 1)))
                    attn.gate(dve, g)
                E.chain_n = link.n


class NormTurn:

    def __init__(self, nc, E, name, ring, st, rows_set, to, scale, shift):
        self.nc, self.E, self.ring, self.rows_set, self.to, self.scale, self.shift = nc, E, ring, rows_set, to, scale, shift
        self.rows = [E.sb(f"{name}_rows{i}", [P, D], ctx=st) for i in range(2)]
        self.ssq, self.dev, self.inv = (E.sb(f"{name}_{x}", [P, 2], ctx=st) for x in ("ssq", "dev", "inv"))
        self.sq_set, self.dev_set, self.xn_set = (E.sem(f"{name}_{x}") for x in ("sq_set", "dev_set", "xn_set"))
        self.stored = None

    def square(self, act, x, t):
        nc, b = self.nc, slice(t % 2, t % 2 + 1)
        act.wait_ge(self.rows_set, t + 1)
        if t >= 2:
            act.wait_ge(self.ring.full, self.ring.nth(("t", t - 2, 1)))
            if self.stored is not None:
                act.wait_ge(self.stored[t % 2], 16 * (t // 2))
        nc.scalar.activation(self.rows[t % 2][:], x, ACT.Square, accum_out=self.ssq[:, b]).then_inc(self.sq_set, 1)
        act.wait_ge(self.sq_set, t + 1)
        nc.scalar.activation(self.dev[:, b], self.ssq[:, b], ACT.Sqrt, bias=self.E.eps_rms[:], scale=1.0 / D).then_inc(self.dev_set, 1)

    def normalise(self, dve, link, x, t):
        nc, b = self.nc, slice(t % 2, t % 2 + 1)
        dve.wait_ge(self.dev_set, t + 1)
        link(dve, nc.vector.reciprocal(self.inv[:, b], self.dev[:, b]))
        nc.vector.tensor_scalar(self.rows[t % 2][:], x, self.inv[:, b], None, ALU.mult).then_inc(self.xn_set, 1)

    def turn(self, pe, t):
        nc, ring = self.nc, self.ring
        pe.wait_ge(self.xn_set, t + 1)
        for h in range(2):
            bank, free = ring.take(("t", t, h))
            wait(pe, ring.free, free)
            for c in range(4):
                last = nc.tensor.transpose(bank[:, c * P:(c + 1) * P], self.rows[t % 2][:, (4 * h + c) * P:(4 * h + c + 1) * P], self.E.ident[:])
            last.then_inc(ring.full, 1)

    def evacuate(self, act, t):
        nc, ring = self.nc, self.ring
        for h in range(2):
            act.wait_ge(ring.full, ring.nth(("t", t, h)))
            for k in range(4):
                c = 4 * h + k
                last = nc.scalar.activation(self.to[:, c, t * P:(t + 1) * P], ring.bank(("t", t, h))[:, k * P:(k + 1) * P], ACT.Identity,
                                            bias=self.shift[:, c:c + 1], scale=self.scale[:, c:c + 1])
            last.then_inc(ring.free, 1)


def stage_out(nc, E, A, layer, rows_in, rows_out, modulate=False):
    n = f"{layer}"
    with ExitStack() as st:
        wo = E.sb("wo" + n, [P, NY, D], ctx=st)
        gain = E.sb("ln_gain" + n, [P, D], ctx=st)
        shift = E.sb("ln_shift" + n, [P, D], ctx=st)
        stats = E.sb("ln_stats" + n, [P, 2, 6], ctx=st)
        mv = E.sb("ln_mv" + n, [P, 2], ctx=st)
        dev = E.sb("ln_dev" + n, [P, 1], ctx=st)
        rstd = E.sb("ln_rstd" + n, [P, 1], ctx=st)
        NX = 3
        xs = [E.sb(f"x_tile{n}_{i}", [P, D], ctx=st) for i in range(NX)]
        x_landed = [E.sem(f"x_tile_landed{n}_{i}") for i in range(NX)]
        stored = [E.sem(f"x_stored{n}_{i}") for i in range(NX)]
        wo_landed = [E.sem(f"wo_landed{n}_{i}") for i in range(3)]
        ln_landed = E.sem("ln_landed" + n)
        var_set, dev_set, rows_set = E.sem("var_set" + n), E.sem("dev_set" + n), E.sem("rows_set" + n)
        ringD = Ring(E.banks[0:4], E.sem("outD_full" + n), E.sem("outD_free" + n))
        ringA = Ring(E.banks[4:8], E.sem("outA_full" + n), E.sem("outA_free" + n))
        norm = NormTurn(nc, E, "n1", ringA, st, rows_set, E.xT, E.mod[:, ND:2 * ND], E.mod[:, 0:ND]) if modulate else None
        with nc.Block() as block:

            @block.tensor
            def _(pe):
                def turn(t):
                    if modulate:
                        norm.turn(pe, t)
                        return
                    pe.wait_ge(rows_set, t + 1)
                    for h in range(2):
                        bank, free = ringA.take(("t", t, h))
                        wait(pe, ringA.free, free)
                        for c in range(4):
                            last = nc.tensor.transpose(bank[:, c * P:(c + 1) * P], xs[t % NX][:, (4 * h + c) * P:(4 * h + c + 1) * P], E.ident[:])
                        last.then_inc(ringA.full, 1)

                for t in range(NT):
                    for hf in range(2):
                        bank, free = ringD.take(("y", t, hf))
                        wait(pe, ringD.free, free)
                        for c in range(NY):
                            if t == 0 and hf == 0 and c % 4 == 0:
                                pe.wait_ge(wo_landed[c // 4], 16)
                            last = nc.tensor.matmul(bank[:], E.yT[:, c, t * P:(t + 1) * P], wo[:, c, hf * HALF:(hf + 1) * HALF],
                                                    start=(c == 0), stop=(c == NY - 1))
                        last.then_inc(ringD.full, 1)
                    if t > 0:
                        turn(t - 1)
                turn(NT - 1)

            @block.sync
            def _(sp):
                def load_x(t):
                    if t >= NX:
                        sp.wait_ge(stored[t % NX], 16 * (t // NX))
                        sp.wait_ge(ringA.full, ringA.nth(("t", t - NX, 1)))
                    sp.dma_start(xs[t % NX][:], rows_in[t * P:(t + 1) * P, :]).then_inc(x_landed[t % NX], 16)

                wv = A["w_out"][layer].rearrange("(c p) n -> p c n", p=P)
                for i in range(3):
                    sp.dma_start(wo[:, 4 * i:4 * i + 4, :], wv[:, 4 * i:4 * i + 4, :]).then_inc(wo_landed[i], 16)
                sp.dma_start(gain[:], A["ln_g"][layer:layer + 1, :].broadcast_to([P, D])).then_inc(ln_landed, 16)
                sp.dma_start(shift[:], A["ln_b"][layer:layer + 1, :].broadcast_to([P, D])).then_inc(ln_landed, 16)
                for t in range(NX):
                    load_x(t)
                for t in range(NT):
                    sp.wait_ge(rows_set, t + 1)
                    sp.dma_start(rows_out[t * P:(t + 1) * P, :], xs[t % NX][:]).then_inc(stored[t % NX], 16)
                    if t >= 1 and t - 1 + NX < NT:
                        load_x(t - 1 + NX)
                for i in range(NX):
                    sp.wait_ge(stored[i], 16 * ((NT - 1 - i) // NX + 1))

            @block.scalar
            def _(act):
                def evacuate(t):
                    if modulate:
                        norm.evacuate(act, t)
                        return
                    for h in range(2):
                        act.wait_ge(ringA.full, ringA.nth(("t", t, h)))
                        nc.scalar.copy(E.xT[:, 4 * h:4 * h + 4, t * P:(t + 1) * P],
                                       ringA.bank(("t", t, h)).rearrange("p (c n) -> p c n", c=4)).then_inc(ringA.free, 1)

                for t in range(NT):
                    act.wait_ge(var_set, t + 1)
                    nc.scalar.activation(dev[:], mv[:, 1:2], ACT.Sqrt, bias=E.eps_ln[:]).then_inc(dev_set, 1)
                    if modulate:
                        norm.square(act, xs[t % NX][:], t)
                    if t > 0:
                        evacuate(t - 1)
                evacuate(NT - 1)

            @block.vector
            def _(dve):
                link = Chain(E.dve_chain)
                link.n = E.chain_n
                dve.wait_ge(ln_landed, 32)
                for t in range(NT):
                    xt = xs[t % NX]
                    dve.wait_ge(x_landed[t % NX], 16 * (t // NX + 1))
                    for hf in range(2):
                        cols = slice(hf * HALF, (hf + 1) * HALF)
                        dve.wait_ge(ringD.full, ringD.nth(("y", t, hf)))
                        nc.vector.scalar_tensor_tensor(xt[:, cols], xt[:, cols], ALPHA, ringD.bank(("y", t, hf))[:],
                                                       ALU.mult, ALU.add).then_inc(ringD.free, 1)
                        dve.wait_ge(ringD.free, ringD.nth(("y", t, hf)))
                        link(dve, nc.vector.bn_stats(stats[:, hf, :], xt[:, cols]))
                    nc.vector.bn_aggr(mv[:], stats[:].rearrange("p a b -> p (a b)")).then_inc(var_set, 1)
                    dve.wait_ge(dev_set, t + 1)
                    link(dve, nc.vector.reciprocal(rstd[:], dev[:]))
                    link(dve, nc.vector.tensor_scalar(xt[:], xt[:], mv[:, 0:1], rstd[:], ALU.subtract, ALU.mult))
                    link(dve, nc.vector.tensor_tensor(xt[:], xt[:], gain[:], ALU.mult))
                    nc.vector.tensor_tensor(xt[:], xt[:], shift[:], ALU.add).then_inc(rows_set, 1)
                    if modulate:
                        norm.normalise(dve, link, xt[:], t)
                E.chain_n = link.n


def stage_forget(nc, E, A):
    with ExitStack() as st:
        wf = E.sb("wf", [P, ND, FOX_HEADS], ctx=st)
        z = E.sb("f_z", [FOX_HEADS, S], ctx=st)
        e = E.sb("f_exp", [FOX_HEADS, S], ctx=st)
        low = E.sb("f_low", [FOX_HEADS, S], ctx=st)
        one = E.sb("f_one", [FOX_HEADS, S], ctx=st)
        wf_landed, cum_stored = E.sem("wf_landed"), E.sem("cum_stored")
        ring = Ring(E.banks[0:2], E.sem("f_full"), E.sem("f_free"))
        logit_set, abs_set, log_set, ncum_set, exp_set = E.sem("f_logit_set"), E.sem("f_abs_set"), E.sem("f_log_set"), E.sem("ncum_set"), E.sem("f_exp_set")
        with nc.Block() as block:

            @block.tensor
            def _(pe):
                pe.wait_ge(wf_landed, 16)
                for hf in range(NH):
                    bank, _ = ring.take(hf)
                    for d in range(ND):
                        last = nc.tensor.matmul(bank[0:FOX_HEADS, :], wf[:, d, :], E.xT[:, d, hf * HALF:(hf + 1) * HALF],
                                                start=(d == 0), stop=(d == ND - 1))
                    last.then_inc(ring.full, 1)

            @block.sync
            def _(sp):
                sp.dma_start(wf[:], A["w_kv_shared"].rearrange("(c p) n -> p c n", p=P)[:, :, 2 * D:2 * D + FOX_HEADS]).then_inc(wf_landed, 16)
                sp.wait_ge(ncum_set, 1)
                sp.dma_start(E.ncum_rows, z[:]).then_inc(cum_stored, 16)
                sp.wait_ge(cum_stored, 16)

            @block.scalar
            def _(act):
                act.wait_ge(logit_set, 1)
                nc.scalar.activation(e[:], z[:], ACT.Abs).then_inc(abs_set, 1)
                act.wait_ge(abs_set, 1)
                nc.scalar.activation(e[:], e[:], ACT.Exp, scale=-1.0).then_inc(exp_set, 1)
                act.wait_ge(exp_set, 1)
                nc.scalar.activation(e[:], e[:], ACT.Ln, bias=E.ones[0:FOX_HEADS, 0:1]).then_inc(log_set, 1)

            @block.vector
            def _(dve):
                link = Chain(E.dve_chain)
                link.n = E.chain_n
                link(dve, nc.vector.memset(one[:], 1.0))
                for hf in range(NH):
                    dve.wait_ge(ring.full, ring.nth(hf))
                    link(dve, nc.vector.tensor_scalar(z[:, hf * HALF:(hf + 1) * HALF], ring.bank(hf)[0:FOX_HEADS, :], E.b_forget[:], None, ALU.add))
                nc.vector.tensor_scalar(low[:], z[:], 0.0, None, ALU.min).then_inc(logit_set, 1)
                dve.wait_ge(logit_set, 1)
                dve.wait_ge(log_set, 1)
                link(dve, nc.vector.tensor_tensor(e[:], e[:], low[:], ALU.subtract))
                nc.vector.tensor_tensor_scan(z[:], one[:], e[:], 0.0, ALU.mult, ALU.add).then_inc(ncum_set, 1)
                E.chain_n = link.n


def stage_fox(nc, E, A):
    NP = FOX_HEADS // 2
    STEPS = FOX_HEADS * NT
    with ExitStack() as st:
        vT = E.sb("fox_vT", [P, S], ctx=st)
        qT = [E.sb(f"fox_qT{b}", [P, S], ctx=st) for b in range(2)]
        kT = [E.sb(f"fox_kT{b}", [P, S], ctx=st) for b in range(2)]
        v = [E.sb(f"fox_v{b}", [P, NT, P], ctx=st) for b in range(2)]
        ncum = [E.sb(f"ncum{b}", [P, S], ctx=st) for b in range(2)]
        ncum_landed = [E.sem(f"ncum_landed{b}") for b in range(2)]
        probs = [E.sb(f"fox_p{b}", [P, S], ctx=st) for b in range(3)]
        probsT = [E.sb(f"fox_pT{b}", [P, S], ctx=st) for b in range(2)]
        y = [E.sb(f"fox_y{b}", [P, NT, P], ctx=st) for b in range(2)]
        NB = 4
        top = E.sb("fox_top", [P, NB], ctx=st)
        bias = E.sb("fox_bias", [P, NB], ctx=st)
        total = E.sb("fox_total", [P, NB], ctx=st)
        inv = E.sb("fox_inv", [P, NB], ctx=st)
        score = Ring([E.psum[:, 0:S], E.psum[:, S:2 * S]], E.sem("score_full"), E.sem("score_free"))
        ringA = Ring(E.banks[4:6], E.sem("foxA_full"), E.sem("foxA_free"))
        ringY = Ring(E.banks[6:8], E.sem("foxY_full"), E.sem("foxY_free"))
        bias_set, exp_done = E.sem("fox_bias_set"), E.sem("fox_exp_done")
        win = A["w_in"][1].rearrange("(c p) n -> p c n", p=P)
        wkv = A["w_kv_shared"].rearrange("(c p) n -> p c n", p=P)
        KINDS = ("q", "k", "v", "g")

        split = SplitProducts(nc, E, "w1", st, lambda eng, n: eng.wait_ge(ringA.full, ringA.nth((KINDS[n % 4], n // 4, 1))))

        def columns(c, kind):
            if kind == "q":
                return win[:, :, c * P:(c + 1) * P]
            if kind == "g":
                return win[:, :, (GATE0 + c) * P:(GATE0 + c + 1) * P]
            return wkv[:, :, c * P + (D if kind == "v" else 0):(c + 1) * P + (D if kind == "v" else 0)]

        def tile_of(n):
            return n % NT

        def groups(i):
            return [(s, min(s + 4, i + 1)) for s in range(0, i + 1, 4)]

        with nc.Block() as block:

            @block.tensor
            def _(pe):
                def project(c, piece):
                    kind, hf = KINDS[piece // 2], piece % 2
                    n = 4 * c + piece // 2
                    if kind == "g":
                        bank, free = ringA.take(("tv", c, hf))
                        wait(pe, ringA.free, free)
                        pe.wait_ge(ringA.free, ringA.nth(("v", c, hf)))
                        for j in range(4):
                            last = nc.tensor.transpose(bank[:, j * P:(j + 1) * P], vT[:, (4 * hf + j) * P:(4 * hf + j + 1) * P], E.ident[:])
                        last.then_inc(ringA.full, 1)
                    bank, free = ringA.take((kind, c, hf))
                    wait(pe, ringA.free, free)
                    split.project(pe, bank, n, hf).then_inc(ringA.full, 1)

                def scores(n):
                    hd, i = n // NT, tile_of(n)
                    c, r = hd // 2, slice((hd % 2) * 64, (hd % 2) * 64 + 64)
                    bank, free = score.take(n)
                    wait(pe, score.free, free)
                    if n % (2 * NT) == 0:
                        pe.wait_ge(ringA.free, ringA.nth(("k", c, 1)))
                    keys = (i + 1) * P
                    for k0 in range(0, keys, HALF):
                        k1 = min(k0 + HALF, keys)
                        nc.tensor.matmul(bank[:, k0:k1], qT[c % 2][r, i * P:(i + 1) * P], kT[c % 2][r, k0:k1],
                                         start=True, stop=True)
                    nc.tensor.matmul(bank[:, keys - P:keys], E.ident[:], E.causal[:], start=False, stop=True,
                                     skip_group_check=True).then_inc(score.full, 1)

                def turn(n):
                    i = tile_of(n)
                    pe.wait_ge(exp_done, n + 1)
                    for s0, s1 in groups(i):
                        bank, free = ringA.take(("t", n, s0))
                        wait(pe, ringA.free, free)
                        for s in range(s0, s1):
                            last = nc.tensor.transpose(bank[:, (s - s0) * P:(s - s0 + 1) * P], probs[n % 3][:, s * P:(s + 1) * P], E.ident[:])
                        last.then_inc(ringA.full, 1)

                def values(n):
                    hd, i = n // NT, tile_of(n)
                    c, j = hd // 2, hd % 2
                    bank, free = ringY.take(n)
                    wait(pe, ringY.free, free)
                    pe.wait_ge(ringA.free, ringA.nth(("t", n, groups(i)[-1][0])))
                    pe.wait_ge(ringA.free, ringA.nth(("tv", c, 1)))
                    for s in range(i + 1):
                        last = nc.tensor.matmul(bank[:, 0:64], probsT[n % 2][:, s * P:(s + 1) * P], v[c % 2][:, s, j * 64:(j + 1) * 64],
                                                start=(s == 0), stop=(s == i))
                    last.then_inc(ringY.full, 1)

                def turn_y(c):
                    pe.wait_ge(ringY.free, ringY.nth(2 * NT * (c + 1) - 1))
                    for hf in range(NH):
                        bank, free = ringY.take(("y", c, hf))
                        wait(pe, ringY.free, free)
                        for k in range(4):
                            last = nc.tensor.transpose(bank[:, k * P:(k + 1) * P], y[c % 2][:, 4 * hf + k, :], E.ident[:])
                        last.then_inc(ringY.full, 1)

                for piece in range(8):
                    project(0, piece)
                for n in range(STEPS + 5):
                    if n < STEPS:
                        scores(n)
                    if 2 <= n < STEPS + 2:
                        turn(n - 2)
                    if 3 <= n < STEPS + 3:
                        values(n - 3)
                    if n >= 2 * NT + 4 and (n - 4) % (2 * NT) == 0:
                        turn_y((n - 4) // (2 * NT) - 1)
                    if n % 2 == 1 and n // (2 * NT) + 1 < NP:
                        project(n // (2 * NT) + 1, (n % (2 * NT)) // 2)

            @block.sync
            def _(sp):
                def load_w(n):
                    split.load(sp, n, columns(n // 4, KINDS[n % 4]))

                def load_ncum(hd):
                    if hd >= 2:
                        sp.wait_ge(score.free, score.nth((hd - 1) * NT - 1))
                    sp.dma_start(ncum[hd % 2][:], E.ncum_rows[hd:hd + 1, :].broadcast_to([P, S])).then_inc(ncum_landed[hd % 2], 16)

                for n in range(4):
                    load_w(n)
                load_ncum(0)
                load_ncum(1)
                hd = 2
                for n in range(4, 4 * NP):
                    load_w(n)
                    while hd < FOX_HEADS and 2 * n >= 4 * hd + 4:
                        load_ncum(hd)
                        hd += 1
                while hd < FOX_HEADS:
                    load_ncum(hd)
                    hd += 1

            @block.gpsimd
            def _(pool):
                split.split_weights(pool, 4 * NP)

            @block.scalar
            def _(act):
                def evacuate_piece(c, piece):
                    kind, hf = KINDS[piece // 2], piece % 2
                    key = (kind, c, hf)
                    if kind == "g":
                        act.wait_ge(ringA.full, ringA.nth(("tv", c, hf)))
                        if c >= 2 and hf == 0:
                            act.wait_ge(ringY.full, ringY.nth(2 * NT * (c - 1) - 1))
                        nc.scalar.copy(v[c % 2][:, 4 * hf:4 * hf + 4, :], ringA.bank(("tv", c, hf)).rearrange("p (t n) -> p t n", t=4)).then_inc(ringA.free, 1)
                    act.wait_ge(ringA.full, ringA.nth(key))
                    cols = slice(hf * HALF, (hf + 1) * HALF)
                    if c >= 2 and hf == 0 and kind in "qk":
                        act.wait_ge(score.full, score.nth(2 * NT * (c - 1) - 1))
                    bank = ringA.bank(key)
                    if kind == "q":
                        ins = nc.scalar.activation(qT[c % 2][:, cols], bank[:], ACT.Copy, scale=FOX_SCALE)
                    elif kind == "k":
                        ins = nc.scalar.copy(kT[c % 2][:, cols], bank[:])
                    elif kind == "v":
                        ins = nc.scalar.copy(vT[:, cols], bank[:])
                    else:
                        ins = nc.scalar.activation(E.yT[:, c, cols], bank[:], ACT.Silu)
                    ins.then_inc(ringA.free, 1)

                for piece in range(8):
                    evacuate_piece(0, piece)
                for n in range(STEPS + 5):
                    if n < STEPS:
                        keys = (tile_of(n) + 1) * P
                        act.wait_ge(bias_set, n + 1)
                        if n >= NB:
                            act.wait_ge(ringY.free, ringY.nth(n - NB))
                        nc.scalar.activation(probs[n % 3][:, 0:keys], probs[n % 3][:, 0:keys], ACT.Exp, bias=bias[:, n % NB:n % NB + 1],
                                             accum_out=total[:, n % NB:n % NB + 1]).then_inc(exp_done, 1)
                    if 2 <= n < STEPS + 2:
                        m = n - 2
                        for s0, s1 in groups(tile_of(m)):
                            key = ("t", m, s0)
                            act.wait_ge(ringA.full, ringA.nth(key))
                            if m >= 2 and s0 == 0:
                                act.wait_ge(ringY.full, ringY.nth(m - 2))
                            nc.scalar.copy(probsT[m % 2][:, s0 * P:s1 * P], ringA.bank(key)[:, 0:(s1 - s0) * P]).then_inc(ringA.free, 1)
                    if n % 2 == 1 and n // (2 * NT) + 1 < NP:
                        evacuate_piece(n // (2 * NT) + 1, (n % (2 * NT)) // 2)

            @block.vector
            def _(dve):
                link = Chain(E.dve_chain)
                link.n = E.chain_n
                for n in range(STEPS + 5):
                    if n < STEPS:
                        hd, i = n // NT, tile_of(n)
                        keys = (i + 1) * P
                        if n % NT == 0:
                            dve.wait_ge(ncum_landed[hd % 2], 16 * (hd // 2 + 1))
                        if n >= 3:
                            dve.wait_ge(ringA.full, ringA.nth(("t", n - 3, groups(tile_of(n - 3))[-1][0])))
                        if n >= NB:
                            dve.wait_ge(exp_done, n - NB + 1)
                        dve.wait_ge(score.full, score.nth(n))
                        b = slice(n % NB, n % NB + 1)
                        nc.vector.tensor_tensor_reduce(probs[n % 3][:, 0:keys], score.bank(n)[:, 0:keys], ncum[hd % 2][:, 0:keys], 1.0, -3.0e38,
                                                       ALU.add, ALU.max, top[:, b]).then_inc(score.free, 1)
                        dve.wait_ge(score.free, score.nth(n))
                        nc.vector.tensor_scalar(bias[:, b], top[:, b], -1.0, None, ALU.mult).then_inc(bias_set, 1)
                    if 3 <= n < STEPS + 3:
                        m = n - 3
                        hd, i = m // NT, tile_of(m)
                        b = slice(m % NB, m % NB + 1)
                        dve.wait_ge(exp_done, m + 1)
                        link(dve, nc.vector.reciprocal(inv[:, b], total[:, b]))
                        dve.wait_ge(ringY.full, ringY.nth(m))
                        nc.vector.tensor_scalar(y[(hd // 2) % 2][:, i, (hd % 2) * 64:(hd % 2) * 64 + 64], ringY.bank(m)[:, 0:64], inv[:, b], None,
                                                ALU.mult).then_inc(ringY.free, 1)
                    if n >= 2 * NT + 4 and (n - 4) % (2 * NT) == 0:
                        c = (n - 4) // (2 * NT) - 1
                        for hf in range(NH):
                            cols = slice(hf * HALF, (hf + 1) * HALF)
                            dve.wait_ge(ringY.full, ringY.nth(("y", c, hf)))
                            dve.wait_ge(ringA.free, ringA.nth(("g", c, hf)))
                            nc.vector.tensor_tensor(E.yT[:, c, cols], ringY.bank(("y", c, hf))[:], E.yT[:, c, cols], ALU.mult).then_inc(ringY.free, 1)
                E.chain_n = link.n


def stage_memory_heads(nc, E, A, layer):
    n = f"{layer}"
    with ExitStack() as st:
        NW = 6
        w = [E.sb(f"wm_{i}", [P, ND, P], ctx=st) for i in range(NW)]
        landed = [E.sem(f"wm_landed{i}") for i in range(NW)]
        qT = [E.sb(f"mem_qT{i}", [P, S], ctx=st) for i in range(2)]
        ringA = Ring(E.banks[0:4], E.sem("mA_full"), E.sem("mA_free"))
        ringD = Ring(E.banks[4:8], E.sem("mD_full"), E.sem("mD_free"))
        attn = MemoryAttention(nc, E, layer, ringA, ringD, st)
        mod = Modulation(nc, E, A, st)
        per_head = mod.LOADS // MEM_HEADS
        mod_banks = (E.banks[0], E.banks[4:8])
        win = A["w_in"][layer].rearrange("(c p) n -> p c n", p=P)
        with nc.Block() as block:

            @block.tensor
            def _(pe):
                def project(h):
                    for k, kind in enumerate("qm"):
                        m = 2 * h + k
                        pe.wait_ge(landed[m % NW], 16 * (m // NW + 1))
                        ring = ringD if kind == "q" else ringA
                        for hf in range(NH):
                            bank, free = ring.take((kind, h, hf))
                            wait(pe, ring.free, free)
                            for d in range(ND):
                                last = nc.tensor.matmul(bank[:], w[m % NW][:, d, :], E.xT[:, d, hf * HALF:(hf + 1) * HALF],
                                                        start=(d == 0), stop=(d == ND - 1))
                            last.then_inc(ring.full, 1)

                project(0)
                for h in range(MEM_HEADS):
                    pe.wait_ge(ringD.free, ringD.nth(("q", h, NH - 1)))
                    attn.scores(pe, h, qT[h % 2])
                    if h + 1 < MEM_HEADS:
                        project(h + 1)
                    attn.turn(pe, h)
                    attn.values(pe, h)
                pe.wait_ge(ringA.free, ringA.nth(("t", MEM_HEADS - 1, NT // 2 - 1)))
                pe.wait_ge(ringD.free, ringD.nth(("o", MEM_HEADS - 1, NH - 1)))
                mod.total(pe, mod_banks)

            @block.sync
            def _(sp):
                mod.load_small(sp)
                done = 0
                for m in range(2 * MEM_HEADS):
                    h, kind = m // 2, "qm"[m % 2]
                    col = (ND if kind == "q" else GATE0 + ND) + h
                    if m >= NW:
                        k0, h0 = "qm"[(m - NW) % 2], (m - NW) // 2
                        ring = ringD if k0 == "q" else ringA
                        sp.wait_ge(ring.full, ring.nth((k0, h0, NH - 1)))
                    sp.dma_start(w[m % NW][:], win[:, :, col * P:(col + 1) * P]).then_inc(landed[m % NW], 16)
                    while m >= NW - 1 and done < (m - NW + 2) * per_head:
                        mod.load(sp, done)
                        done += 1
                for m in range(done, mod.LOADS):
                    mod.load(sp, m)
                mod.store(sp)

            @block.scalar
            def _(act):
                def gate(h):
                    for hf in range(NH):
                        act.wait_ge(ringA.full, ringA.nth(("m", h, hf)))
                        nc.scalar.activation(E.yT[:, ND + h, hf * HALF:(hf + 1) * HALF], ringA.bank(("m", h, hf))[:], ACT.Silu).then_inc(ringA.free, 1)

                gate(0)
                for h in range(MEM_HEADS):
                    attn.exps(act, h)
                    if h + 1 < MEM_HEADS:
                        gate(h + 1)
                    attn.evacuate(act, h)

            @block.vector
            def _(dve):
                link = Chain(E.dve_chain)
                link.n = E.chain_n

                def queries(h):
                    for hf in range(NH):
                        dve.wait_ge(ringD.full, ringD.nth(("q", h, hf)))
                        if h >= 2 and hf == 0:
                            dve.wait_ge(ringA.full, ringA.nth(("s", h - 2, NT // 2 - 1)))
                        nc.vector.tensor_copy(qT[h % 2][:, hf * HALF:(hf + 1) * HALF], ringD.bank(("q", h, hf))[:]).then_inc(ringD.free, 1)

                queries(0)
                for h in range(MEM_HEADS):
                    attn.maxima(dve, link, h)
                    attn.normalise(dve, link, h)
                    for m in range(h * per_head, (h + 1) * per_head):
                        mod.accumulate(dve, link, m)
                    if h + 1 < MEM_HEADS:
                        queries(h + 1)
                    dve.wait_ge(ringA.free, ringA.nth(("m", h, NH - 1)))
                    attn.gate(dve, h)
                mod.finish(dve, link, mod_banks)
                E.chain_n = link.n


GW = 512
RW = 512
HD = 64
NPAIR = RW // P
C = 64
NC = S // C
LORA, GATE_LORA = 32, 96
DECAY = math.exp(-0.5)
LEVELS = 5
UNITS = 4


class Modulation:
    NG = 6 * D // HALF
    GATES = (4, 5, 10, 11)
    HD_ = ND // 2
    LOADS = 2 * (6 * D // HALF)

    def __init__(self, nc, E, A, st):
        self.nc, self.E, self.A = nc, E, A
        self.w = [E.sb(f"ada_{i}", [P, self.HD_, HALF], ctx=st) for i in range(2)]
        self.landed = [E.sem(f"ada_landed{i}") for i in range(2)]
        self.sum = E.sb("ada_sum", [P, 6 * D], ctx=st)
        self.c_cols = E.sb("c_cols", [P, ND], ctx=st)
        self.b = E.sb("ada_b", [P, 6 * ND], ctx=st)
        self.gain = E.sb("norm_gains", [P, 2 * ND], ctx=st)
        self.gate_b = E.sb("gate_b", [P, 2, D], ctx=st)
        self.small, self.stored = E.sem("ada_small"), E.sem("gates_stored")
        self.summed, self.full, self.rows_set = E.sem("ada_summed"), E.sem("ada_full"), E.sem("gate_rows_set")

    def load_small(self, sp):
        A, gain = self.A, self.gain
        for to, src in ((self.c_cols[:], A["c_2_cols"]), (self.b[:], A["ada_b_2_cols"]),
                        (gain[:, 0:ND], A["norm1_g_2_cols"]), (gain[:, ND:2 * ND], A["norm2_g_2_cols"])):
            sp.dma_start(to, src).then_inc(self.small, 16)
        for i in range(2):
            g0 = (2 + 3 * i) * D
            sp.dma_start(self.gate_b[:, i, :], A["ada_b_2"][0:1, g0:g0 + D].broadcast_to([P, D])).then_inc(self.small, 16)

    def load(self, sp, m):
        g, half = m // 2, m % 2
        if m >= 2:
            sp.wait_ge(self.summed, m - 1)
        wv = self.A["ada_w_2"][0].rearrange("(c p) n -> p c n", p=P)
        sp.dma_start(self.w[half][:], wv[:, half * self.HD_:(half + 1) * self.HD_, g * HALF:(g + 1) * HALF]).then_inc(self.landed[half], 16)

    def store(self, sp):
        sp.wait_ge(self.rows_set, 1)
        for i in range(2):
            g0 = (2 + 3 * i) * D
            sp.dma_start(self.E.gates[:, i * D:(i + 1) * D], self.sum[:, g0:g0 + D]).then_inc(self.stored, 16)
        sp.wait_ge(self.stored, 32)

    def accumulate(self, dve, link, m):
        V, g, half = self.nc.vector, m // 2, m % 2
        to = self.sum[:, g * HALF:(g + 1) * HALF]
        if m == 0:
            dve.wait_ge(self.small, 16 * 6)
        dve.wait_ge(self.landed[half], 16 * (g + 1))
        for k in range(self.HD_):
            d = half * self.HD_ + k
            c = self.c_cols[:, d:d + 1]
            if d == 0:
                ins = V.tensor_scalar(to, self.w[half][:, k, :], c, None, ALU.mult)
            else:
                ins = V.scalar_tensor_tensor(to, self.w[half][:, k, :], c, to, ALU.mult, ALU.add)
            if k < self.HD_ - 1:
                link(dve, ins)
        ins.then_inc(self.summed, 1)
        dve.wait_ge(self.summed, m + 1)

    def finish(self, dve, link, banks):
        V, E = self.nc.vector, self.E
        cols_bank, gate_banks = banks
        dve.wait_ge(self.full, 1)
        for g in range(self.NG):
            if g not in self.GATES:
                link(dve, V.tensor_tensor(E.mod[:, 4 * g:4 * g + 4], cols_bank[:, 4 * g:4 * g + 4], self.b[:, 4 * g:4 * g + 4], ALU.add))
        for k, g in enumerate(self.GATES):
            i, hf = k // 2, g % 2
            ins = V.tensor_tensor(self.sum[:, g * HALF:(g + 1) * HALF], gate_banks[k][:], self.gate_b[:, i, hf * HALF:(hf + 1) * HALF], ALU.add)
        ins.then_inc(self.rows_set, 1)
        for i in range(2):
            m = E.mod[:, (1 + 3 * i) * ND:(2 + 3 * i) * ND]
            link(dve, V.scalar_tensor_tensor(m, m, 1.0, self.gain[:, i * ND:(i + 1) * ND], ALU.add, ALU.mult))

    def total(self, pe, banks):
        nc, E = self.nc, self.E
        cols_bank, gate_banks = banks
        pe.wait_ge(self.summed, self.LOADS)
        for g in range(self.NG):
            if g in self.GATES:
                bank = gate_banks[self.GATES.index(g)]
                last = nc.tensor.matmul(bank[:], E.ones[:], self.sum[:, g * HALF:(g + 1) * HALF], start=True, stop=True)
            else:
                for k in range(4 * g, 4 * g + 4):
                    last = nc.tensor.matmul(cols_bank[:, k:k + 1], self.sum[:, k * P:(k + 1) * P], E.ones[:, 0:1], start=True, stop=True)
        last.then_inc(self.full, 1)


def stage_rwkv_pairs(nc, E, A):
    n0 = 3 * RW
    with ExitStack() as st:
        NW = 3
        w = [E.sb(f"wr_{i}", [P, ND, P], ctx=st) for i in range(NW)]
        w_landed = [E.sem(f"wr_landed{i}") for i in range(NW)]
        wl = E.sb("w_lora", [P, ND, 2 * LORA + GATE_LORA], ctx=st)
        w2 = E.sb("w2", [LORA, RW], ctx=st)
        a2 = E.sb("a2", [LORA, RW], ctx=st)
        small = E.sem("rwkv_small")
        cols = E.sb("rwkv_cols", [P, 12 + 4 * 6], ctx=st)
        mu, w0c, a0c, kkc, kac, rkc = (cols[:, 0:12], *(cols[:, 12 + 4 * i:16 + 4 * i] for i in range(5)))
        ka1 = cols[:, 32:36]
        mu_x = [E.sb(f"mu_x{i}", [n, 1], ctx=st) for i, n in enumerate((LORA, LORA, GATE_LORA))]
        xw = E.sb("xw", [LORA, S], ctx=st)
        xa = E.sb("xa", [LORA, S], ctx=st)
        blocksum = E.sb("blocksum", [P, P], ctx=st)
        headsel = E.sb("headsel", [P, 2], ctx=st)
        restart = E.sb("restart", [P, S], ctx=st)
        m_up = E.sb("m_up", [P, P], ctx=st)
        m_upeq = E.sb("m_upeq", [P, P], ctx=st)
        m_low0 = E.sb("m_low0", [P, P], ctx=st)
        m_level = E.sb("m_level", [P, LEVELS + 1, P], ctx=st)
        masks_set = E.sem("masks_set")
        z = E.sb("z", [P, 1 + S], ctx=st)
        r = [E.sb(f"r{i}", [P, S], ctx=st) for i in range(2)]
        k, v, at, bt = (E.sb(x, [P, S], ctx=st) for x in ("k", "v", "at", "bt"))
        lw = E.sb("lw", [P, S], ctx=st)
        cl = E.sb("cl", [P, S], ctx=st)
        e2 = E.sb("e2", [P, S], ctx=st)
        tmp = E.sb("tmp", [P, S], ctx=st)
        rate = E.sb("rate", [P, S], ctx=st)
        ctr = E.sb("ctr", [P, NC], ctx=st)
        tok = {x: E.sb("tok_" + x, [P, NT, P], ctx=st) for x in "abkv"}
        abT, akT, rbT, rkT, Xm, XT, L = (E.sb(x, [P, 4, UNITS * P], ctx=st) for x in ("abT", "akT", "rbT", "rkT", "Xm", "XT", "L"))
        AV = E.sb("AV", [P, 4, UNITS * HD], ctx=st)
        T1, GH = akT, Xm
        spare, spare2 = abT[:].rearrange("p g n -> p (g n)"), L[:].rearrange("p g n -> p (g n)")
        MTs, Ns, QTs = spare[:, 0:S], spare[:, S:2 * S], spare2[:, 0:S]
        Yi = spare2[:, S:2 * S].rearrange("p (t n) -> p t n", t=NT)
        ringA = Ring(E.banks[0:4], E.sem("rwA_full"), E.sem("rwA_free"))
        ringD = Ring(E.banks[4:8], E.sem("rwD_full"), E.sem("rwD_free"))
        S_ = {x: E.sem("rw_" + x) for x in ("shift", "sq", "cc", "front", "level", "exp1", "exp2", "exp3", "lora", "stored", "tanh", "rstore")}
        win = A["w_in_2"][0].rearrange("(c p) n -> p c n", p=P)[:, :, 2 * GW:]
        KIND = "rkv"

        script = [("lora",)]
        front = [("proj", "r"), ("proj", "k"), ("proj", "v"), ("small",), ("sums",)]
        script += [(f[0], 0, *f[1:]) for f in front]
        for c in range(NPAIR):
            script.append(("turn", c))
            script.append(("A", c))
            script.append(("AV", c))
            for m in range(1, LEVELS + 1):
                script.append(("level", c, m))
                if c + 1 < NPAIR:
                    f = front[m - 1]
                    script.append((f[0], c + 1, *f[1:]))
            script.append(("tail", c))

        def units(g):
            return g // 2, g % 2

        with nc.Block() as block:

            @block.tensor
            def _(pe):
                def take(ring, key):
                    bank, free = ring.take(key)
                    wait(pe, ring.free, free)
                    return bank

                def lora():
                    pe.wait_ge(small, 16 * E.n_small)
                    for i, (lo, n) in enumerate(((0, LORA), (LORA, LORA), (2 * LORA, GATE_LORA))):
                        for hf in range(NH):
                            bank = take(ringA, ("lora", i, hf))
                            for d in range(ND):
                                last = nc.tensor.matmul(bank[0:n, :], wl[:, d, lo:lo + n], E.hT[:, d, hf * HALF:(hf + 1) * HALF],
                                                        start=(d == 0), stop=(d == ND - 1))
                            last.then_inc(ringA.full, 1)

                def proj(c, kind):
                    m = 3 * c + KIND.index(kind)
                    pe.wait_ge(w_landed[m % NW], 16 * (m // NW + 1))
                    for hf in range(NH):
                        bank = take(ringA, (kind, c, hf))
                        for d in range(ND):
                            last = nc.tensor.matmul(bank[:], w[m % NW][:, d, :], E.hT[:, d, hf * HALF:(hf + 1) * HALF],
                                                    start=(d == 0), stop=(d == ND - 1))
                        last.then_inc(ringA.full, 1)

                def small_(c):
                    pe.wait_ge(S_["lora"], 2)
                    pe.wait_ge(S_["tanh"], 1)
                    for name, m, x in (("w", w2, xw), ("a", a2, xa)):
                        for hf in range(NH):
                            bank = take(ringA, (name, c, hf))
                            nc.tensor.matmul(bank[:], m[:, c * P:(c + 1) * P], x[:, hf * HALF:(hf + 1) * HALF],
                                             start=True, stop=True).then_inc(ringA.full, 1)

                def sums(c):
                    pe.wait_ge(S_["sq"], c + 1)
                    for hf in range(NH):
                        bank = take(ringA, ("n", c, hf))
                        nc.tensor.matmul(bank[:], blocksum[:], tmp[:, hf * HALF:(hf + 1) * HALF], start=True, stop=True).then_inc(ringA.full, 1)

                def turn(c):
                    for x, src in (("v", v), ("k", k), ("b", bt), ("a", at)):
                        if x == "v":
                            pe.wait_ge(S_["shift"], 3 * c + 3)
                        if x == "k":
                            pe.wait_ge(S_["front"], c + 1)
                        for hf in range(NH):
                            bank = take(ringA, ("t" + x, c, hf))
                            for j in range(4):
                                t = 4 * hf + j
                                last = nc.tensor.transpose(bank[:, j * P:(j + 1) * P], src[:, t * P:(t + 1) * P], E.ident[:])
                            last.then_inc(ringA.full, 1)
                    bank = take(ringA, ("bonus", c))
                    for t in range(NT):
                        last = nc.tensor.matmul(bank[:, 2 * t:2 * t + 2], rate[:, t * P:(t + 1) * P], headsel[:], start=True, stop=True)
                    last.then_inc(ringA.full, 1)

                def a_part(c):
                    aT, bT, kT, rT = at, bt, k, r[c % 2]
                    for g in range(4):
                        j, th = units(g)
                        rows = slice(j * HD, (j + 1) * HD)
                        for name, left, right in (("ab", bT, aT), ("X", aT, bT), ("ak", kT, aT), ("rb", bT, rT), ("rk", kT, rT)):
                            bank = take(ringD, (name, c, g))
                            for u in range(UNITS):
                                t = slice((4 * th + u) * P, (4 * th + u + 1) * P)
                                last = nc.tensor.matmul(bank[:, u * P:(u + 1) * P], left[rows, t], right[rows, t], start=True, stop=True)
                            last.then_inc(ringD.full, 1)

                def level(c, m):
                    for g in range(4):
                        pe.wait_ge(S_["level"], 4 * (LEVELS * c + m - 1) + g + 1)
                        pe.wait_ge(ringD.free, ringD.nth(("X", c, g) if m == 1 else ("dXT", c, m - 1, g)))
                        bank = take(ringA, ("T1", c, m, g))
                        for u in range(UNITS):
                            cu = slice(u * P, (u + 1) * P)
                            last = nc.tensor.matmul(bank[:, cu], L[:, g, cu], Xm[:, g, cu], start=True, stop=True)
                        last.then_inc(ringA.full, 1)
                    for g in range(4):
                        pe.wait_ge(ringA.free, ringA.nth(("T1", c, m, g)))
                        if m < LEVELS:
                            bank = take(ringD, ("dX", c, m, g))
                            for u in range(UNITS):
                                cu = slice(u * P, (u + 1) * P)
                                last = nc.tensor.matmul(bank[:, cu], XT[:, g, cu], T1[:, g, cu], start=True, stop=True)
                            last.then_inc(ringD.full, 1)
                        bank = take(ringD, ("dXT", c, m, g))
                        for u in range(UNITS):
                            cu = slice(u * P, (u + 1) * P)
                            last = nc.tensor.matmul(bank[:, cu], T1[:, g, cu], XT[:, g, cu], start=True, stop=True)
                        last.then_inc(ringD.full, 1)

                def av(c):
                    pe.wait_ge(ringA.free, ringA.nth(("ta", c, NH - 1)))
                    for g in range(4):
                        j, th = units(g)
                        hcols = slice(j * HD, (j + 1) * HD)
                        bank = take(ringA, ("AV", c, g))
                        pe.wait_ge(ringD.free, ringD.nth(("ak", c, g)))
                        for u in range(UNITS):
                            last = nc.tensor.matmul(bank[:, u * HD:(u + 1) * HD], akT[:, g, u * P:(u + 1) * P], tok["v"][:, 4 * th + u, hcols],
                                                    start=True, stop=True)
                        last.then_inc(ringA.full, 1)

                def tail(c):
                    for g in range(4):
                        j, th = units(g)
                        hcols = slice(j * HD, (j + 1) * HD)
                        bank = take(ringA, ("GH", c, g))
                        pe.wait_ge(ringA.free, ringA.nth(("AV", c, g)))
                        pe.wait_ge(ringD.free, ringD.nth(("dXT", c, LEVELS, g)))
                        for u in range(UNITS):
                            wT = XT[:, g, u * P:(u + 1) * P]
                            nc.tensor.matmul(bank[:, u * P:u * P + HD], wT, tok["a"][:, 4 * th + u, hcols], start=True, stop=True)
                            last = nc.tensor.matmul(bank[:, u * P + HD:(u + 1) * P], wT, AV[:, g, u * HD:(u + 1) * HD], start=True, stop=True)
                        last.then_inc(ringA.full, 1)
                    pe.wait_ge(ringA.free, ringA.nth(("GH", c, 3)))
                    for q in range(2):
                        rows = slice(q * C, (q + 1) * C)
                        bank = take(ringD, ("MT", c, q))
                        for t in range(NT):
                            for j in range(2):
                                g, u, o = 2 * j + t // 4, t % 4, slice(j * HD, (j + 1) * HD)
                                last = nc.tensor.matmul(bank[o, t * HD:(t + 1) * HD], GH[rows, g, u * P:u * P + HD], tok["b"][rows, t, o],
                                                        start=True, stop=True)
                        last.then_inc(ringD.full, 1)
                    for q in range(2):
                        rows = slice(q * C, (q + 1) * C)
                        bank = take(ringD, ("N", c, q))
                        for t in range(NT):
                            for j in range(2):
                                g, u, o = 2 * j + t // 4, t % 4, slice(j * HD, (j + 1) * HD)
                                to = bank[o, t * HD:(t + 1) * HD]
                                nc.tensor.matmul(to, tok["b"][rows, t, o], GH[rows, g, u * P + HD:(u + 1) * P], start=True, stop=False)
                                last = nc.tensor.matmul(to, tok["k"][rows, t, o], tok["v"][rows, t, o], start=False, stop=True)
                        last.then_inc(ringD.full, 1)
                    for th in range(2):
                        bank = take(ringD, ("Q", c, th))
                        for u in range(UNITS):
                            for j in range(2):
                                g = 2 * j + th
                                last = nc.tensor.matmul(bank[j * HD:(j + 1) * HD, u * P:(u + 1) * P], GH[:, g, u * P:u * P + HD],
                                                        rbT[:, g, u * P:(u + 1) * P], start=True, stop=True)
                        last.then_inc(ringD.full, 1)
                    for th in range(2):
                        bank = take(ringA, ("Yi", c, th))
                        for u in range(UNITS):
                            t = 4 * th + u
                            for j in range(2):
                                g = 2 * j + th
                                to = bank[:, u * P + j * HD:u * P + (j + 1) * HD]
                                nc.tensor.matmul(to, rbT[:, g, u * P:(u + 1) * P], GH[:, g, u * P + HD:(u + 1) * P], start=True, stop=False)
                                last = nc.tensor.matmul(to, rkT[:, g, u * P:(u + 1) * P], tok["v"][:, t, j * HD:(j + 1) * HD], start=False, stop=True)
                        last.then_inc(ringA.full, 1)

                pe.wait_ge(masks_set, E.n_masks)
                steps = {"lora": lora, "proj": proj, "small": small_, "sums": sums, "turn": turn, "A": a_part, "AV": av, "level": level, "tail": tail}
                for name, *args in script:
                    steps[name](*args)

            @block.sync
            def _(sp):
                n = 0
                for to, src in ((wl[:], win[:, :, n0:n0 + 2 * LORA + GATE_LORA]), (w2[:], A["rwkv_w2_2"][0]), (a2[:], A["rwkv_a2_2"][0]),
                                (mu, A["mu_main_cols"]), (mu_x[0][:], A["mu_w_col"]), (mu_x[1][:], A["mu_a_col"]), (mu_x[2][:], A["mu_g_col"]),
                                (w0c, A["rwkv_w0_2_cols"]), (a0c, A["rwkv_a0_2_cols"]), (kkc, A["rwkv_k_k_2_cols"]),
                                (kac, A["rwkv_k_a_2_cols"]), (rkc, A["rwkv_r_k_2_cols"])):
                    sp.dma_start(to, src).then_inc(small, 16)
                    n += 1
                assert n == E.n_small

                def load(m):
                    if m >= NW:
                        sp.wait_ge(ringA.full, ringA.nth((KIND[(m - NW) % 3], (m - NW) // 3, 1)))
                    col = (m % 3) * RW + (m // 3) * P
                    sp.dma_start(w[m % NW][:], win[:, :, col:col + P]).then_inc(w_landed[m % NW], 16)

                for m in range(NW):
                    load(m)
                for c in range(NPAIR):
                    sp.wait_ge(ringA.free, ringA.nth(("tv", c, 1)))
                    sp.dma_start(E.v_dram[:, :, c * P:(c + 1) * P], tok["v"][:]).then_inc(S_["rstore"], 16)
                    for m in range(NW + 3 * c, min(NW + 3 * c + 3, 3 * NPAIR)):
                        load(m)
                    sp.wait_ge(ringD.free, ringD.nth(("Q", c, 1)))
                    sp.wait_ge(ringA.free, ringA.nth(("Yi", c, 1)))
                    for to, src in ((E.mt_dram, MTs), (E.n_dram, Ns), (E.qt_dram, QTs)):
                        sp.dma_start(to[:, c * S:(c + 1) * S], src).then_inc(S_["stored"], 16)
                    sp.dma_start(E.yi_dram[:, :, c * P:(c + 1) * P], Yi).then_inc(S_["stored"], 16)
                sp.wait_ge(S_["stored"], 64 * NPAIR)
                sp.wait_ge(S_["rstore"], 16 * NPAIR)

            @block.gpsimd
            def _(pool):
                ready = E.sem("pool_masks")
                count = 0

                def done(ins):
                    nonlocal count
                    ins.then_inc(ready, 1)
                    count += 1
                    pool.wait_ge(ready, count)

                def keep(ap, pattern, op, base, mult):
                    done(nc.gpsimd.affine_select(out=ap, in_=ap, compare_op=op, fill=0.0, base=base, pattern=pattern, channel_multiplier=mult))

                def blocks(ap, size):
                    v3 = ap.rearrange("p (b n) -> p b n", n=size)
                    keep(v3, [[-size, P // size], [0, size]], ALU.is_ge, 0, 1)
                    keep(v3, [[size, P // size], [0, size]], ALU.is_ge, size - 1, -1)

                for ap in (blocksum[:], m_up[:], m_upeq[:], m_low0[:], m_level[:]):
                    done(nc.gpsimd.memset(ap, 1.0))
                blocks(blocksum[:], HD)
                blocks(m_up[:], C)
                keep(m_up[:], [[1, P]], ALU.is_gt, 0, -1)
                blocks(m_upeq[:], C)
                keep(m_upeq[:], [[1, P]], ALU.is_ge, 0, -1)
                blocks(m_low0[:], 2)
                keep(m_low0[:], [[-1, P]], ALU.is_gt, 0, 1)
                for m in range(0, LEVELS + 1):
                    half = 2 ** m
                    ap = m_level[:, m, :]
                    blocks(ap, 2 * half)
                    v3 = ap.rearrange("p (b n) -> p b n", n=2 * half)
                    keep(v3, [[0, P // (2 * half)], [1, 2 * half]], ALU.is_ge, -half, 0)
                    keep(v3, [[2 * half, P // (2 * half)], [0, 2 * half]], ALU.is_ge, half - 1, -1)
                done(nc.gpsimd.memset(restart[:], 1.0))
                keep(restart[:].rearrange("p (b n) -> p b n", n=C), [[0, NC], [1, C]], ALU.is_gt, 0, 0)
                done(nc.gpsimd.memset(headsel[:], 1.0))
                keep(headsel[:, 0:1], [[0, 1]], ALU.is_ge, HD - 1, -1)
                keep(headsel[:, 1:2], [[0, 1]], ALU.is_ge, -HD, 1)
                pool.sem_inc(masks_set, E.n_masks)
                for c in range(NPAIR):
                    for m in range(1, LEVELS + 1):
                        for g in range(4):
                            if m == 1:
                                pool.wait_ge(ringD.free, ringD.nth(("ab", c, g)))
                                if c > 0:
                                    pool.wait_ge(S_["stored"], 64 * c)
                            else:
                                pool.wait_ge(ringA.full, ringA.nth(("T1", c, m - 1, g)))
                            nc.gpsimd.tensor_tensor(L[:, g, :].rearrange("p (u n) -> p u n", u=UNITS), abT[:, g, :].rearrange("p (u n) -> p u n", u=UNITS),
                                                    m_level[:, m:m + 1, :].broadcast_to([P, UNITS, P]), ALU.mult).then_inc(S_["level"], 1)

            @block.scalar
            def _(act):
                def got(key):
                    act.wait_ge(ringA.full, ringA.nth(key))
                    return ringA.bank(key)

                def lora():
                    for i, n in enumerate((LORA, LORA, GATE_LORA)):
                        for hf in range(NH):
                            bank = got(("lora", i, hf))
                            if i > 0 and hf == 0:
                                act.wait_ge(S_["lora"], i)
                            nc.scalar.copy(z[0:n, 1 + hf * HALF:1 + (hf + 1) * HALF], bank[0:n, :]).then_inc(ringA.free, 1)
                    act.wait_ge(S_["lora"], 1)
                    nc.scalar.activation(xw[:], xw[:], ACT.Tanh).then_inc(S_["tanh"], 1)
                    act.wait_ge(S_["lora"], 3)
                    nc.scalar.activation(E.xg[:], E.xg[:], ACT.Sigmoid)

                def proj(c, kind):
                    m = 3 * c + KIND.index(kind)
                    for hf in range(NH):
                        bank = got((kind, c, hf))
                        if hf == 0 and m > 0:
                            act.wait_ge(S_["shift"], m)
                        nc.scalar.copy(z[:, 1 + hf * HALF:1 + (hf + 1) * HALF], bank[:]).then_inc(ringA.free, 1)

                def small_(c):
                    for name, to, bias in (("w", lw, w0c), ("a", rate, a0c)):
                        for hf in range(NH):
                            bank = got((name, c, hf))
                            if c > 0 and hf == 0:
                                if name == "w":
                                    act.wait_ge(S_["front"], c)
                                else:
                                    act.wait_ge(ringA.full, ringA.nth(("bonus", c - 1)))
                            nc.scalar.activation(to[:, hf * HALF:(hf + 1) * HALF], bank[:], ACT.Sigmoid, bias=bias[:, c:c + 1]).then_inc(ringA.free, 1)
                    act.wait_ge(S_["shift"], 3 * c + 2)
                    if c > 0:
                        act.wait_ge(S_["front"], c)
                    nc.scalar.activation(tmp[:], k[:], ACT.Square, scale=kkc[:, c:c + 1]).then_inc(S_["sq"], 1)

                def sums(c):
                    for hf in range(NH):
                        bank = got(("n", c, hf))
                        if hf == 0:
                            act.wait_ge(ringA.full, ringA.nth(("n", c, 1)))
                        nc.scalar.activation(tmp[:, hf * HALF:(hf + 1) * HALF], bank[:], ACT.Sqrt).then_inc(ringA.free, 1)
                    act.wait_ge(S_["cc"], c + 1)
                    nc.scalar.activation(e2[:], cl[:], ACT.Exp, scale=-1.0).then_inc(S_["exp1"], 1)
                    nc.scalar.activation(cl[:], cl[:], ACT.Exp).then_inc(S_["exp2"], 1)
                    nc.scalar.activation(E.carry[:, c, :], E.carry[:, c, :], ACT.Exp)
                    nc.scalar.activation(lw[:], lw[:], ACT.Exp).then_inc(S_["exp3"], 1)

                def turn(c):
                    for x in "vkba":
                        for hf in range(NH):
                            bank = got(("t" + x, c, hf))
                            if x == "v" and hf == 0 and c > 0:
                                act.wait_ge(S_["rstore"], 16 * c)
                            nc.scalar.copy(tok[x][:, 4 * hf:4 * hf + 4, :], bank.rearrange("p (t n) -> p t n", t=4)).then_inc(ringA.free, 1)
                    bank = got(("bonus", c))
                    nc.scalar.copy(E.bonus[:, :, 2 * c:2 * c + 2], bank[:, 0:2 * NT].rearrange("p (t j) -> p t j", t=NT)).then_inc(ringA.free, 1)

                def a_part(c):
                    pass

                def av(c):
                    for g in range(4):
                        bank = got(("AV", c, g))
                        nc.scalar.copy(AV[:, g, :], bank[:, 0:UNITS * HD]).then_inc(ringA.free, 1)

                def level(c, m):
                    for g in range(4):
                        bank = got(("T1", c, m, g))
                        if not (c == 0 and m == 1):
                            before = (c, m - 1) if m > 1 else (c - 1, LEVELS)
                            act.wait_ge(ringD.full, ringD.nth(("dXT", before[0], before[1], g)))
                        nc.scalar.copy(T1[:, g, :], bank[:]).then_inc(ringA.free, 1)

                def tail(c):
                    for g in range(4):
                        bank = got(("GH", c, g))
                        nc.scalar.copy(GH[:, g, :], bank[:]).then_inc(ringA.free, 1)
                    for th in range(2):
                        bank = got(("Yi", c, th))
                        nc.scalar.copy(Yi[:, 4 * th:4 * th + 4, :], bank.rearrange("p (t n) -> p t n", t=4)).then_inc(ringA.free, 1)

                steps = {"lora": lora, "proj": proj, "small": small_, "sums": sums, "turn": turn, "A": a_part, "AV": av, "level": level, "tail": tail}
                for name, *args in script:
                    steps[name](*args)

            @block.vector
            def _(dve):
                link = Chain(E.dve_chain)
                link.n = E.chain_n
                def mixed(dst, n, m, free_sem):
                    link(dve, nc.vector.tensor_tensor(dst, z[0:n, 0:S], z[0:n, 1:1 + S], ALU.subtract))
                    nc.vector.scalar_tensor_tensor(dst, dst, m, z[0:n, 1:1 + S], ALU.mult, ALU.add).then_inc(free_sem, 1)

                def lora():
                    for i, (n, dst) in enumerate(((LORA, xw[:]), (LORA, xa[:]), (GATE_LORA, E.xg[:]))):
                        dve.wait_ge(ringA.free, ringA.nth(("lora", i, 1)))
                        mixed(dst, n, mu_x[i][:], S_["lora"])

                def proj(c, kind):
                    i = KIND.index(kind)
                    dve.wait_ge(ringA.free, ringA.nth((kind, c, 1)))
                    dst = {"r": r[c % 2], "k": k, "v": v}[kind]
                    if kind == "v" and c > 0:
                        dve.wait_ge(ringA.full, ringA.nth(("tv", c - 1, 1)))
                    if c >= 2 and kind == "r":
                        dve.wait_ge(ringD.free, ringD.nth(("Q", c - 2, 1)))
                    if c >= 1 and kind == "k":
                        dve.wait_ge(ringD.full, ringD.nth(("rk", c - 1, 3)))
                        dve.wait_ge(ringA.full, ringA.nth(("tk", c - 1, 1)))
                    mixed(dst[:], P, mu[:, i * 4 + c:i * 4 + c + 1], S_["shift"])

                def small_(c):
                    V = nc.vector
                    dve.wait_ge(S_["shift"], 3 * c + 3)
                    dve.wait_ge(ringA.free, ringA.nth(("w", c, 1)))
                    link(dve, V.tensor_scalar(lw[:], lw[:], -DECAY, None, ALU.mult))
                    link(dve, V.tensor_tensor_scan(cl[:], restart[:], lw[:], 0.0, ALU.mult, ALU.add))
                    cl3 = cl[:].rearrange("p (c n) -> p c n", n=C)
                    link(dve, V.tensor_copy(ctr[:].rearrange("p (c o) -> p c o", o=1), cl3[:, :, C // 2 - 1:C // 2]))
                    carry = E.carry[:, c, :]
                    link(dve, V.tensor_tensor(carry.rearrange("p (c o) -> p c o", o=1), cl3[:, :, C - 1:C], ctr[:].rearrange("p (c o) -> p c o", o=1), ALU.subtract))
                    link(dve, V.tensor_tensor(carry[:, 0:NC - 1], carry[:, 0:NC - 1], ctr[:, 1:NC], ALU.add))
                    link(dve, V.tensor_tensor(cl3, cl3, ctr[:].rearrange("p (c o) -> p c o", o=1).broadcast_to([P, NC, C]), ALU.subtract))
                    V.tensor_tensor(lw[:], cl[:], lw[:], ALU.subtract).then_inc(S_["cc"], 1)

                def sums(c):
                    V = nc.vector
                    K, R = k, r[c % 2]
                    if c >= 1:
                        dve.wait_ge(ringD.full, ringD.nth(("rk", c - 1, 3)))
                        dve.wait_ge(ringA.full, ringA.nth(("ta", c - 1, 1)))
                    dve.wait_ge(ringA.free, ringA.nth(("n", c, 1)))
                    link(dve, V.tensor_scalar(tmp[:], tmp[:], 1e-12, None, ALU.max))
                    link(dve, V.reciprocal(tmp[:], tmp[:]))
                    link(dve, V.scalar_tensor_tensor(at[:], K[:], kkc[:, c:c + 1], tmp[:], ALU.mult, ALU.mult))
                    link(dve, V.tensor_tensor(bt[:], at[:], rate[:], ALU.mult))
                    link(dve, V.tensor_scalar(rate[:], rate[:], kac[:, c:c + 1], ka1[:, c:c + 1], ALU.mult, ALU.add))
                    link(dve, V.tensor_tensor(K[:], K[:], rate[:], ALU.mult))
                    link(dve, V.scalar_tensor_tensor(rate[:], R[:], rkc[:, c:c + 1], K[:], ALU.mult, ALU.mult))
                    dve.wait_ge(S_["exp1"], c + 1)
                    link(dve, V.tensor_tensor(K[:], K[:], e2[:], ALU.mult))
                    link(dve, V.tensor_tensor(bt[:], bt[:], e2[:], ALU.mult))
                    dve.wait_ge(S_["exp2"], c + 1)
                    link(dve, V.tensor_tensor(R[:], R[:], cl[:], ALU.mult))
                    dve.wait_ge(S_["exp3"], c + 1)
                    V.scalar_tensor_tensor(at[:], at[:], -1.0, lw[:], ALU.mult, ALU.mult).then_inc(S_["front"], 1)

                def turn(c):
                    pass

                def av(c):
                    pass

                def a_part(c):
                    V = nc.vector
                    if c > 0:
                        dve.wait_ge(ringA.full, ringA.nth(("Yi", c - 1, 1)))
                        dve.wait_ge(S_["stored"], 64 * c)
                    wide = lambda m: m.rearrange("p (o n) -> p o n", o=1).broadcast_to([P, UNITS, P])
                    u3 = lambda x: x.rearrange("p (u n) -> p u n", u=UNITS)
                    for g in range(4):
                        for name, to, m in (("ab", abT, m_up), ("X", Xm, m_low0), ("ak", akT, m_up), ("rb", rbT, m_upeq), ("rk", rkT, m_upeq)):
                            key = (name, c, g)
                            dve.wait_ge(ringD.full, ringD.nth(key))
                            if name != "X":
                                V.tensor_tensor(u3(to[:, g, :]), u3(ringD.bank(key)), wide(m[:]), ALU.mult).then_inc(ringD.free, 1)
                                if name == "ab":
                                    dve.wait_ge(ringD.free, ringD.nth(key))
                                    link(dve, V.tensor_tensor(u3(XT[:, g, :]), u3(abT[:, g, :]), m_level[:, 0:1, :].broadcast_to([P, UNITS, P]), ALU.mult))
                                    link(dve, V.tensor_tensor(u3(XT[:, g, :]), u3(XT[:, g, :]), wide(E.ident[:]), ALU.add))
                            else:
                                link(dve, V.tensor_tensor(u3(Xm[:, g, :]), u3(ringD.bank(key)), wide(m[:]), ALU.mult))
                                V.tensor_tensor(u3(Xm[:, g, :]), u3(Xm[:, g, :]), wide(E.ident[:]), ALU.add).then_inc(ringD.free, 1)

                def level(c, m):
                    V = nc.vector
                    for g in range(4):
                        if m < LEVELS:
                            key = ("dX", c, m, g)
                            dve.wait_ge(ringD.full, ringD.nth(key))
                            V.tensor_tensor(Xm[:, g, :], Xm[:, g, :], ringD.bank(key)[:], ALU.add).then_inc(ringD.free, 1)
                        key = ("dXT", c, m, g)
                        dve.wait_ge(ringD.full, ringD.nth(key))
                        V.tensor_tensor(XT[:, g, :], XT[:, g, :], ringD.bank(key)[:], ALU.add).then_inc(ringD.free, 1)

                def tail(c):
                    V = nc.vector
                    dve.wait_ge(S_["level"], 4 * LEVELS * (c + 1))
                    chunk = lambda to, q: to.rearrange("p (t q n) -> p t q n", q=2, n=HD)[:, :, q, :]
                    for q in range(2):
                        dve.wait_ge(ringD.full, ringD.nth(("MT", c, q)))
                        V.tensor_tensor(chunk(MTs, q), ringD.bank(("MT", c, q)).rearrange("p (t n) -> p t n", n=HD),
                                        E.ident2[:].rearrange("p (o n) -> p o n", o=1).broadcast_to([P, NT, HD]), ALU.add).then_inc(ringD.free, 1)
                    for q in range(2):
                        dve.wait_ge(ringD.full, ringD.nth(("N", c, q)))
                        V.tensor_copy(chunk(Ns, q), ringD.bank(("N", c, q)).rearrange("p (t n) -> p t n", n=HD)).then_inc(ringD.free, 1)
                    for th in range(2):
                        cols4 = slice(th * HALF, (th + 1) * HALF)
                        dve.wait_ge(ringD.full, ringD.nth(("Q", c, th)))
                        V.tensor_tensor(QTs[:, cols4], ringD.bank(("Q", c, th))[:], r[c % 2][:, cols4], ALU.add).then_inc(ringD.free, 1)

                link(dve, nc.vector.memset(z[:, 0:1], 0.0))
                dve.wait_ge(masks_set, E.n_masks)
                dve.wait_ge(small, 16 * E.n_small)
                link(dve, nc.vector.tensor_scalar(ka1, kac, -1.0, 1.0, ALU.mult, ALU.add))
                link(dve, nc.vector.tensor_copy(E.ident2[0:HD, :], E.ident[0:HD, 0:HD]))
                link(dve, nc.vector.tensor_copy(E.ident2[HD:P, :], E.ident[HD:P, HD:P]))
                steps = {"lora": lora, "proj": proj, "small": small_, "sums": sums, "turn": turn, "A": a_part, "AV": av, "level": level, "tail": tail}
                for name, *args in script:
                    steps[name](*args)
                E.chain_n = link.n


N_GROUPS, PER_GROUP = 4, 8
EXPERTS = N_GROUPS * PER_GROUP
TOP_K = 2
EH = 512


def stage_mix(nc, E, A, rows_in, rows_out, normed_out):
    H = GW // HD
    NR = N_GROUPS + EXPERTS
    with ExitStack() as st:
        sb = lambda name, shape, dt=F32: E.sb(name, shape, dt, ctx=st)
        w_uv, w_o = sb("w_uv", [P, ND, 2 * GW]), sb("w_o", [P, ND, D])
        ws, wsT = sb("ws", [P, H, P]), sb("wsT", [P, H, P])
        bs = sb("bs", [P, H])
        ln_w, ln_b, gn_w, gn_b = (sb(x, [P, 512]) for x in ("gln_w", "gln_b", "gn_w", "gn_b"))
        g2 = sb("g2", [GATE_LORA, RW])
        gate = sb("gate1", [P, D])
        rw, rb = sb("rw", [P, ND, NR]), sb("rb", [P, NR])
        STREAMS = ("mt", "n", "qt", "yi", "v")
        stream = {x: [sb(f"s_{x}{i}", [P, 512]) for i in range(2)] for x in STREAMS}
        landed = {x: [E.sem(f"s_{x}_landed{i}") for i in range(2)] for x in STREAMS}
        T = [sb(f"T{i}", [P, NPAIR * HD]) for i in range(5)]
        u = [sb(f"gu{i}", [P, GW]) for i in range(2)]
        vg = sb("vg", [P, GW])
        vn = [sb(f"vn{i}", [P, GW]) for i in range(2)]
        y = [sb(f"y{i}", [P, D]) for i in range(2)]
        sq = sb("gn_sq", [P, RW])
        yT = [sb(f"y2T{i}", [P, ND, P]) for i in range(2)]
        NX = 2
        xs = [sb(f"x2_{i}", [P, D]) for i in range(NX)]
        h2T = [sb(f"h2T{i}", [P, ND, P]) for i in range(2)]
        stats, mv_ = sb("g_stats", [P, 6]), sb("g_mv", [P, 2])
        gdev, grstd = sb("g_dev", [P, 1]), sb("g_rstd", [P, 1])
        s1, s2, dev8, inv8 = (sb(x, [P, H]) for x in ("gn_s1", "gn_s2", "gn_dev", "gn_inv"))
        small = E.sem("mix_small")
        w_landed = {x: E.sem("mix_" + x) for x in ("uv", "o", "ws", "row")}
        x_landed = [E.sem(f"x2_landed{i}") for i in range(NX)]
        x_stored = [E.sem(f"x2_stored{i}") for i in range(NX)]
        n_stored = [E.sem(f"n2_stored{i}") for i in range(2)]
        sems = {x: E.sem("mix_" + x) for x in ("tril", "var", "dev", "vn", "T", "ya", "yb", "s2", "sq", "yc", "dev8", "rows")}
        ringA = Ring(E.banks[0:4], E.sem("mixA_full"), E.sem("mixA_free"))
        ringD = Ring(E.banks[4:8], E.sem("mixD_full"), E.sem("mixD_free"))

        class Slot:
            def __getitem__(self, at):
                _, c, cols = at
                t = cols.start // P
                return h2T[t % 2][:, c, :]

        norm = NormTurn(nc, E, "n2", ringA, st, sems["rows"], Slot(), E.mod[:, 4 * ND:5 * ND], E.mod[:, 3 * ND:4 * ND])
        norm.stored = n_stored
        win = A["w_in_2"][0].rearrange("(c p) n -> p c n", p=P)

        with nc.Block() as block:

            @block.tensor
            def _(pe):
                def take(ring, key):
                    bank, free = ring.take(key)
                    wait(pe, ring.free, free)
                    return bank

                def uv(t, i):
                    bank = take(ringA, ("u" if i == 0 else "v", t))
                    for d in range(ND):
                        last = nc.tensor.matmul(bank[:], E.hT[:, d, t * P:(t + 1) * P], w_uv[:, d, i * GW:(i + 1) * GW],
                                                start=(d == 0), stop=(d == ND - 1))
                    last.then_inc(ringA.full, 1)

                def chain(c):
                    if c == 0 or c >= NC - 1:
                        return
                    t, q = c // 2, c % 2
                    if q == 0 or c == 1:
                        pe.wait_ge(landed["mt"][t % 2], 16 * (t // 2 + 1))
                    pe.wait_ge(sems["T"], c + 1)
                    bank = take(ringD, ("T", c))
                    for p in range(NPAIR):
                        for j in range(2):
                            rows = slice(j * HD, (j + 1) * HD)
                            last = nc.tensor.matmul(bank[rows, p * HD:(p + 1) * HD], stream["mt"][t % 2][rows, p * P + q * HD:p * P + (q + 1) * HD],
                                                    T[c % 5][rows, p * HD:(p + 1) * HD], start=True, stop=True)
                    last.then_inc(ringD.full, 1)

                def mix(t):
                    pe.wait_ge(sems["vn"], t + 1)
                    bank = take(ringD, ("mix", t))
                    for h in range(H):
                        last = nc.tensor.matmul(bank[:, h * HD:(h + 1) * HD], wsT[:, h, :], vn[t % 2][:, h * HD:(h + 1) * HD], start=True, stop=True)
                    last.then_inc(ringD.full, 1)

                def rwkv_rows(t):
                    pe.wait_ge(landed["qt"][t % 2], 16 * (t // 2 + 1))
                    pe.wait_ge(sems["T"], min(2 * t + 2, NC))
                    for j in range(2):
                        bank = take(ringD, ("y", t, j))
                        rows = slice(j * HD, (j + 1) * HD)
                        for q in range(2):
                            for p in range(NPAIR):
                                last = nc.tensor.matmul(bank[q * C:(q + 1) * C, p * HD:(p + 1) * HD],
                                                        stream["qt"][t % 2][rows, p * P + q * C:p * P + (q + 1) * C],
                                                        T[(2 * t + q) % 5][rows, p * HD:(p + 1) * HD], start=True, stop=True)
                        last.then_inc(ringD.full, 1)
                    bank = take(ringD, ("g", t))
                    nc.tensor.matmul(bank[:], E.xg[:, t * P:(t + 1) * P], g2[:], start=True, stop=True).then_inc(ringD.full, 1)

                def turn(t):
                    pe.wait_ge(sems["ya"], t + 1)
                    pe.wait_ge(sems["yb"], t + 1)
                    for h in range(2):
                        bank = take(ringA, ("yT", t, h))
                        for k in range(4):
                            last = nc.tensor.transpose(bank[:, k * P:(k + 1) * P], y[t % 2][:, (4 * h + k) * P:(4 * h + k + 1) * P], E.ident[:])
                        last.then_inc(ringA.full, 1)

                def out(t):
                    pe.wait_ge(ringA.free, ringA.nth(("yT", t, 1)))
                    for hf in range(2):
                        bank = take(ringD, ("o", t, hf))
                        for d in range(ND):
                            last = nc.tensor.matmul(bank[:], yT[t % 2][:, d, :], w_o[:, d, hf * HALF:(hf + 1) * HALF],
                                                    start=(d == 0), stop=(d == ND - 1))
                        last.then_inc(ringD.full, 1)

                def router(t):
                    pe.wait_ge(ringA.free, ringA.nth(("t", t, 1)))
                    bank = take(ringD, ("r", t))
                    for d in range(ND):
                        last = nc.tensor.matmul(bank[:, 0:NR], h2T[t % 2][:, d, :], rw[:, d, :], start=(d == 0), stop=(d == ND - 1))
                    last.then_inc(ringD.full, 1)

                pe.wait_ge(sems["tril"], 1)
                for h in range(2):
                    bank = take(ringA, ("ws", h))
                    for k in range(4):
                        last = nc.tensor.transpose(bank[:, k * P:(k + 1) * P], ws[:, 4 * h + k, :], E.ident[:])
                    last.then_inc(ringA.full, 1)
                pe.wait_ge(small, 16 * 6)
                for t in range(NT + 5):
                    if t < NT:
                        if t == 0:
                            pe.wait_ge(w_landed["uv"], 16)
                        uv(t, 0)
                        chain(2 * t)
                        uv(t, 1)
                        chain(2 * t + 1)
                    if 1 <= t <= NT:
                        mix(t - 1)
                        rwkv_rows(t - 1)
                    if 2 <= t <= NT + 1:
                        turn(t - 2)
                    if 3 <= t <= NT + 2:
                        if t == 3:
                            pe.wait_ge(w_landed["o"], 16)
                        out(t - 3)
                    if 4 <= t <= NT + 3:
                        norm.turn(pe, t - 4)
                    if 5 <= t:
                        router(t - 5)

            @block.sync
            def _(sp):
                sp.dma_start(ws[:], A["gmlp_ws_2"][0].rearrange("h t s -> t h s")).then_inc(w_landed["ws"], 16)
                sp.dma_start(w_uv[:], win[:, :, 0:2 * GW]).then_inc(w_landed["uv"], 16)
                sp.dma_start(bs[:], A["gmlp_bs_cols"]).then_inc(small, 16)
                sp.dma_start(g2[:], A["rwkv_g2_2"][0]).then_inc(small, 16)
                sp.dma_start(rw[:, :, 0:N_GROUPS], A["router_group_w_2"][0].rearrange("(c p) n -> p c n", p=P)).then_inc(small, 16)
                sp.dma_start(rw[:, :, N_GROUPS:NR], A["router_expert_w_2"][0].rearrange("(c p) n -> p c n", p=P)).then_inc(small, 16)
                sp.dma_start(rb[:, 0:N_GROUPS], A["router_group_b_2"].broadcast_to([P, N_GROUPS])).then_inc(small, 16)
                sp.dma_start(rb[:, N_GROUPS:NR], A["router_expert_b_2"].broadcast_to([P, EXPERTS])).then_inc(small, 16)
                for to, name in ((ln_w, "gmlp_ln_w_2"), (ln_b, "gmlp_ln_b_2"), (gn_w, "rwkv_gn_w_2"), (gn_b, "rwkv_gn_b_2")):
                    sp.dma_start(to[:], A[name].broadcast_to([P, 512])).then_inc(w_landed["row"], 16)
                sp.dma_start(gate[:], E.gates[:, 0:D]).then_inc(w_landed["row"], 16)

                def load(x, t):
                    to = stream[x][t % 2]
                    if t >= 2:
                        if x == "mt":
                            sp.wait_ge(ringD.full, ringD.nth(("T", 2 * t - 3)))
                        elif x == "n":
                            sp.wait_ge(sems["T"], 2 * t - 1)
                        elif x == "qt":
                            sp.wait_ge(ringD.full, ringD.nth(("y", t - 2, 1)))
                        else:
                            sp.wait_ge(sems["yb"], t - 1)
                    if x in ("yi", "v"):
                        src = {"yi": E.yi_dram, "v": E.v_dram}[x][:, t, :]
                        sp.dma_start(to[:], src).then_inc(landed[x][t % 2], 16)
                    else:
                        src = {"mt": E.mt_dram, "n": E.n_dram, "qt": E.qt_dram}[x].rearrange("p (c n) -> p c n", c=NPAIR)[:, :, t * P:(t + 1) * P]
                        sp.dma_start(to[:].rearrange("p (c n) -> p c n", c=NPAIR), src).then_inc(landed[x][t % 2], 16)

                def load_x(t):
                    if t >= NX:
                        sp.wait_ge(x_stored[t % NX], 16 * (t // NX))
                        sp.wait_ge(norm.xn_set, t - NX + 1)
                    sp.dma_start(xs[t % NX][:], rows_in[t * P:(t + 1) * P, :]).then_inc(x_landed[t % NX], 16)

                def store(t):
                    sp.wait_ge(sems["rows"], t + 1)
                    sp.dma_start(rows_out[t * P:(t + 1) * P, :], xs[t % NX][:]).then_inc(x_stored[t % NX], 16)
                    sp.wait_ge(norm.xn_set, t + 1)
                    sp.dma_start(normed_out[t * P:(t + 1) * P, :], norm.rows[t % 2][:]).then_inc(n_stored[t % 2], 16)

                for t in range(2):
                    for x in STREAMS:
                        load(x, t)
                    load_x(t)
                sp.dma_start(w_o[:], A["w_out_2"][0].rearrange("(c p) n -> p c n", p=P)).then_inc(w_landed["o"], 16)
                for t in range(1, NT + 5):
                    if t + 1 < NT and t >= 1:
                        for x in STREAMS:
                            load(x, t + 1)
                    if 4 <= t < NT + 4:
                        store(t - 4)
                        if t - 4 + NX < NT:
                            load_x(t - 4 + NX)
                for i in range(2):
                    sp.wait_ge(x_stored[i], 16 * (NT // 2))
                    sp.wait_ge(n_stored[i], 16 * (NT // 2))

            @block.gpsimd
            def _(pool):
                pool.wait_ge(w_landed["ws"], 16)
                nc.gpsimd.affine_select(out=ws[:], in_=ws[:], compare_op=ALU.is_ge, fill=0.0, base=0,
                                        pattern=[[0, H], [-1, P]], channel_multiplier=1).then_inc(sems["tril"], 1)

            @block.scalar
            def _(act):
                def got(key):
                    act.wait_ge(ringA.full, ringA.nth(key))
                    return ringA.bank(key)

                for h in range(2):
                    nc.scalar.copy(wsT[:, 4 * h:4 * h + 4, :], got(("ws", h)).rearrange("p (h n) -> p h n", h=4)).then_inc(ringA.free, 1)
                for t in range(NT + 5):
                    if t < NT:
                        if t >= 2:
                            act.wait_ge(sems["ya"], t - 1)
                        nc.scalar.activation(u[t % 2][:], got(("u", t))[:], ACT.Gelu_apprx_tanh).then_inc(ringA.free, 1)
                        if t >= 1:
                            act.wait_ge(sems["vn"], t)
                        nc.scalar.activation(vg[:], got(("v", t))[:], ACT.Gelu_apprx_tanh).then_inc(ringA.free, 1)
                        act.wait_ge(sems["var"], t + 1)
                        nc.scalar.activation(gdev[:], mv_[:, 1:2], ACT.Sqrt, bias=E.eps_ln[:]).then_inc(sems["dev"], 1)
                    if 1 <= t <= NT:
                        act.wait_ge(sems["yc"], t)
                        nc.scalar.activation(sq[:], y[(t - 1) % 2][:, GW:D], ACT.Square).then_inc(sems["sq"], 1)
                        act.wait_ge(sems["s2"], t)
                        nc.scalar.activation(dev8[:], s2[:], ACT.Sqrt, bias=E.eps_gn[:], scale=1.0 / HD).then_inc(sems["dev8"], 1)
                    if 2 <= t <= NT + 1:
                        for h in range(2):
                            bank = got(("yT", t - 2, h))
                            if t >= 4 and h == 0:
                                act.wait_ge(ringD.full, ringD.nth(("o", t - 4, 1)))
                            nc.scalar.copy(yT[(t - 2) % 2][:, 4 * h:4 * h + 4, :], bank.rearrange("p (c n) -> p c n", c=4)).then_inc(ringA.free, 1)
                    if 4 <= t <= NT + 3:
                        norm.square(act, xs[(t - 4) % NX][:], t - 4)
                        if t >= 6:
                            act.wait_ge(ringD.full, ringD.nth(("r", t - 6)))
                        norm.evacuate(act, t - 4)

            @block.vector
            def _(dve):
                link = Chain(E.dve_chain)
                link.n = E.chain_n
                V = nc.vector
                heads = lambda ap: ap.rearrange("p (h n) -> p h n", n=HD)
                each = lambda ap, n: ap.rearrange("p (h o) -> p h o", o=1).broadcast_to([P, n, HD])

                def got(key):
                    dve.wait_ge(ringD.full, ringD.nth(key))
                    return ringD.bank(key)

                def step(c):
                    if c >= NC - 1:
                        return
                    t, q = c // 2, c % 2
                    if q == 0:
                        dve.wait_ge(landed["n"][t % 2], 16 * (t // 2 + 1))
                    part = stream["n"][t % 2][:].rearrange("p (c n) -> p c n", c=NPAIR)[:, :, q * HD:(q + 1) * HD]
                    to = heads(T[(c + 1) % 5][:])
                    F = E.carry[:, :, c:c + 1].broadcast_to([P, NPAIR, HD])
                    if c >= 4:
                        dve.wait_ge(ringD.full, ringD.nth(("y", (c - 4) // 2, 1)))
                    if c == 0:
                        V.tensor_tensor(to, part, F, ALU.mult).then_inc(sems["T"], 1)
                        return
                    link(dve, V.tensor_tensor(to, heads(got(("T", c))[:, 0:NPAIR * HD]), part, ALU.add))
                    dve.sem_inc(ringD.free, 1)
                    V.tensor_tensor(to, to, F, ALU.mult).then_inc(sems["T"], 1)

                def gmlp_norm(t):
                    dve.wait_ge(ringA.free, ringA.nth(("v", t)))
                    link(dve, V.bn_stats(stats[:], vg[:]))
                    V.bn_aggr(mv_[:], stats[:]).then_inc(sems["var"], 1)
                    dve.wait_ge(sems["dev"], t + 1)
                    link(dve, V.reciprocal(grstd[:], gdev[:]))
                    if t >= 2:
                        dve.wait_ge(ringD.full, ringD.nth(("mix", t - 2)))
                    to = vn[t % 2]
                    link(dve, V.tensor_scalar(to[:], vg[:], mv_[:, 0:1], grstd[:], ALU.subtract, ALU.mult))
                    link(dve, V.tensor_tensor(to[:], to[:], ln_w[:], ALU.mult))
                    V.tensor_tensor(to[:], to[:], ln_b[:], ALU.add).then_inc(sems["vn"], 1)

                def gmlp_rows(t):
                    if t >= 2:
                        dve.wait_ge(ringA.full, ringA.nth(("yT", t - 2, 1)))
                    to = y[t % 2][:, 0:GW]
                    V.tensor_tensor(heads(to), heads(got(("mix", t))), each(bs[:], H), ALU.add).then_inc(ringD.free, 1)
                    dve.wait_ge(ringD.free, ringD.nth(("mix", t)))
                    V.tensor_tensor(to, to, u[t % 2][:], ALU.mult).then_inc(sems["ya"], 1)

                def rwkv_rows(t):
                    yr = y[t % 2][:, GW:D]
                    dve.wait_ge(landed["yi"][t % 2], 16 * (t // 2 + 1))
                    dve.wait_ge(landed["v"][t % 2], 16 * (t // 2 + 1))
                    for j in range(2):
                        head = lambda ap: ap.rearrange("p (c j n) -> p c j n", j=2, n=HD)[:, :, j, :]
                        V.tensor_tensor(head(yr), heads(got(("y", t, j))[:, 0:NPAIR * HD]), head(stream["yi"][t % 2][:]), ALU.add).then_inc(ringD.free, 1)
                    dve.wait_ge(ringD.free, ringD.nth(("y", t, 1)))
                    link(dve, V.tensor_reduce(s1[:], heads(yr), X, ALU.add))
                    link(dve, V.tensor_scalar(s1[:], s1[:], 1.0 / HD, None, ALU.mult))
                    V.tensor_tensor(heads(yr), heads(yr), each(s1[:], H), ALU.subtract).then_inc(sems["yc"], 1)
                    dve.wait_ge(sems["sq"], t + 1)
                    V.tensor_reduce(s2[:], heads(sq[:]), X, ALU.add).then_inc(sems["s2"], 1)
                    vr = stream["v"][t % 2][:]
                    link(dve, V.tensor_tensor(heads(vr), heads(vr), each(E.bonus[:, t, :], H), ALU.mult))
                    dve.wait_ge(sems["dev8"], t + 1)
                    link(dve, V.reciprocal(inv8[:], dev8[:]))
                    link(dve, V.tensor_tensor(heads(yr), heads(yr), each(inv8[:], H), ALU.mult))
                    link(dve, V.tensor_tensor(yr, yr, gn_w[:], ALU.mult))
                    link(dve, V.tensor_tensor(vr, vr, gn_b[:], ALU.add))
                    link(dve, V.tensor_tensor(yr, yr, vr, ALU.add))
                    V.tensor_tensor(yr, yr, got(("g", t))[:], ALU.mult).then_inc(ringD.free, 1)
                    dve.wait_ge(ringD.free, ringD.nth(("g", t)))
                    dve.sem_inc(sems["yb"], 1)

                def residual(t):
                    x = xs[t % NX]
                    dve.wait_ge(x_landed[t % NX], 16 * (t // NX + 1))
                    for hf in range(2):
                        cols = slice(hf * HALF, (hf + 1) * HALF)
                        bank = got(("o", t, hf))
                        link(dve, V.tensor_tensor(sq2[:], bank[:], gate[:, cols], ALU.mult))
                        dve.sem_inc(ringD.free, 1)
                        ins = V.tensor_tensor(x[:, cols], x[:, cols], sq2[:], ALU.add)
                        if hf == 0:
                            link(dve, ins)
                    ins.then_inc(sems["rows"], 1)

                sq2 = sb("res_tmp", [P, HALF])
                dve.wait_ge(w_landed["row"], 16 * 5)
                dve.wait_ge(small, 16 * 6)
                V.memset(T[0][:], 0.0).then_inc(sems["T"], 1)
                for t in range(NT + 5):
                    if t < NT:
                        step(2 * t)
                        gmlp_norm(t)
                        step(2 * t + 1)
                    if 1 <= t <= NT:
                        gmlp_rows(t - 1)
                        rwkv_rows(t - 1)
                    if 3 <= t <= NT + 2:
                        residual(t - 3)
                    if 4 <= t <= NT + 3:
                        norm.normalise(dve, link, xs[(t - 4) % NX][:], t - 4)
                    if 5 <= t:
                        V.tensor_tensor(E.logits[:, t - 5, :], got(("r", t - 5))[:, 0:NR], rb[:], ALU.add).then_inc(ringD.free, 1)
                link(dve, V.memset(s1[:], 0.0))
                E.chain_n = link.n


ASSIGNED = S * TOP_K
OVER = (ASSIGNED - 1) // P
BLOCKS = EXPERTS + OVER
SLOTS = BLOCKS * P
NHC = EH // P


def stage_experts(nc, E, A, normed, token_of_slot, y_slots):
    NR = N_GROUPS + EXPERTS
    with ExitStack() as st:
        sb = lambda name, shape, dt=F32: E.sb(name, shape, dt, ctx=st)
        routes = ("gexp", "geq", "gone")
        gexp, geq, gone = (sb(x, [P, NT, N_GROUPS]) for x in routes)
        sel, sexp, seq, one1, one2 = (sb(x, [P, NT, PER_GROUP]) for x in ("sel", "sexp", "seq", "one1", "one2"))
        best, gprob, first, top1, top2, over, at, den = (sb(x, [P, NT]) for x in ("best", "gprob", "first", "top1", "top2", "over", "at_", "den"))
        both, pick, one32a, one32b, place = (sb(x, [P, NT, EXPERTS]) for x in ("both", "pick", "one32a", "one32b", "place"))
        base = sb("rank_base", [P, NT + 1, EXPERTS])
        nover, upto, over_at, e128 = (sb(x, [P, EXPERTS]) for x in ("nover", "upto", "over_at", "e128"))
        ovcmp, ovexp = sb("ovcmp", [P, OVER, EXPERTS]), sb("ovexp", [P, OVER])
        iota_j = sb("iota_j", [P, EXPERTS])
        before = sb("before", [P, P])
        token_id = sb("token_id", [P, NT], I32)
        zero_i = sb("zero_i", [P, BLOCKS], I32)
        zeros = sb("zeros", [P, D])
        slot_rows_i, slot_rows = sb("slot_rows_i", [BLOCKS, P], I32), sb("slot_rows", [BLOCKS, P])
        idx = sb("idx", [P, BLOCKS], I32)
        ovexp_i, n_over = sb("ovexp_i", [P, OVER], I32), sb("n_over", [P, 1], I32)
        wg, wu = ([sb(f"{x}{i}", [P, ND, EH]) for i in range(2)] for x in ("wgate", "wup"))
        wd = [sb(f"wdown{i}", [P, NHC, D]) for i in range(2)]
        xg = [sb(f"xg{i}", [P, D]) for i in range(2)]
        xT = [sb(f"exT{i}", [P, ND, P]) for i in range(2)]
        act_, hid = sb("e_act", [P, EH]), sb("e_hid", [P, EH])
        hT = sb("e_hT", [P, NHC, P])
        yb = [sb(f"yb{i}", [P, D]) for i in range(2)]

        R = {x: E.sem("route_" + x) for x in ("consts", "gsub", "gexp", "ssub", "sexp", "both", "ranks", "slots", "cleared", "zeroed", "scattered",
                                              "rows", "rowsf", "turned", "idx", "over")}
        two = lambda name: [E.sem(f"{name}{i}") for i in range(2)]
        wg_in, wu_in, wd_in, xg_in, y_out = (two(x) for x in ("wgate_landed", "wup_landed", "wdown_landed", "xg_landed", "y_stored"))
        M = {x: E.sem("moe_" + x) for x in ("xT_full", "xT_set", "gate_full", "up_full", "act_set", "hid_set", "hT_full", "hT_set",
                                            "down_full", "y0_set", "y1_set")}
        O = {x: E.sem("over_" + x) for x in ("w_landed", "xg_landed", "xT_full", "xT_set", "gate_full", "up_full", "act_set", "hid_set",
                                             "hT_full", "hT_set", "down_full", "y0_set", "y1_set", "y_stored", "through")}
        gate_b, up_b, xT_b, hT_b, down_b, rank_b = E.banks[0], E.banks[1], E.banks[2:4], E.banks[4], E.banks[5:7], E.banks[7]
        scale, shift = E.mod[:, 4 * ND:5 * ND], E.mod[:, 3 * ND:4 * ND]
        wgv, wuv = (A[x][0].rearrange("e (c p) n -> e p c n", p=P) for x in ("moe_w_gate_2", "moe_w_up_2"))
        wdv = A["moe_w_down_2"][0].rearrange("e (c p) n -> e p c n", p=P)
        yv = y_slots.rearrange("(b p) d -> b p d", p=P)
        one_of = lambda v, b: v[bass.ds(b, 1)].rearrange("o p c n -> p (o c) n")
        y_of = lambda b: yv[bass.ds(b, 1)].rearrange("o p d -> p (o d)")

        def need(eng, sem, value):
            if not isinstance(value, int) or value > 0:
                eng.wait_ge(sem, value)

        def blocks_in_turn(eng, step):
            for b in range(4):
                step(b, b % 2, b // 2)
            with eng.Fori(2, EXPERTS // 2 - 1) as i:
                for s in range(2):
                    step(i * 2 + s, s, i)
            for s in range(2):
                step(EXPERTS - 2 + s, s, EXPERTS // 2 - 1)

        def further_blocks(eng, step):
            eng.wait_ge(R["over"], 1)
            filled = eng.value_load(n_over[0:1, 0:1], min_val=0, max_val=OVER)
            with eng.Fori(0, OVER) as j:
                with eng.If(filled > j):
                    step(j)

        with nc.Block() as block:

            @block.sync
            def _(sp):
                def load(b, s, what):
                    if what in "gb":
                        sp.dma_start(wg[s][:], one_of(wgv, b)).then_inc(wg_in[s], 16)
                    if what in "ub":
                        sp.dma_start(wu[s][:], one_of(wuv, b)).then_inc(wu_in[s], 16)
                    if what in "db":
                        sp.dma_start(wd[s][:], one_of(wdv, b)).then_inc(wd_in[s], 16)

                sp.wait_ge(R["consts"], 1)
                sp.dma_start(token_of_slot.rearrange("(p b) o -> p (b o)", p=P), zero_i[:]).then_inc(R["cleared"], 16)
                load(0, 0, "b")
                load(1, 1, "g")
                load(1, 1, "u")
                sp.dma_start(yv[EXPERTS:BLOCKS].rearrange("b p d -> p b d"), zeros[:].rearrange("p (o d) -> p o d", o=1).broadcast_to([P, OVER, D])).then_inc(R["zeroed"], 16)
                sp.wait_ge(R["scattered"], 16 * TOP_K * NT)
                sp.dma_start(slot_rows_i[:], token_of_slot.rearrange("(b p) o -> b (p o)", p=P)).then_inc(R["rows"], 16)

                def step(b, s, i):
                    last = isinstance(b, int) and b >= EXPERTS - 2
                    if not last:
                        sp.wait_ge(M["gate_full"], b + 1)
                        load(b + 2, s, "g")
                        sp.wait_ge(M["up_full"], b + 1)
                        load(b + 2, s, "u")
                    if not (isinstance(b, int) and b + 1 >= EXPERTS):
                        need(sp, M["down_full"], 2 * b)
                        load(b + 1, 1 - s, "d")
                    if not (isinstance(b, int) and b == 0):
                        sp.wait_ge(M["y0_set"], b)
                        sp.wait_ge(M["y1_set"], b)
                        sp.dma_start(y_of(b - 1), yb[1 - s][:]).then_inc(y_out[1 - s], 16)

                blocks_in_turn(sp, step)
                sp.wait_ge(M["y0_set"], EXPERTS)
                sp.wait_ge(M["y1_set"], EXPERTS)
                sp.dma_start(y_of(EXPERTS - 1), yb[1][:]).then_inc(y_out[1], 16)
                for s in range(2):
                    sp.wait_ge(y_out[s], 16 * (EXPERTS // 2))
                sp.wait_ge(R["zeroed"], 16)

                def further(j):
                    e = sp.value_load(ovexp_i[0:1, bass.ds(j, 1)], min_val=0, max_val=EXPERTS - 1)
                    sp.dma_start(wg[0][:], one_of(wgv, e)).then_inc(O["w_landed"], 16)
                    sp.dma_start(wu[0][:], one_of(wuv, e)).then_inc(O["w_landed"], 16)
                    sp.dma_start(wd[0][:], one_of(wdv, e)).then_inc(O["w_landed"], 16)
                    sp.wait_ge(O["y0_set"], j + 1)
                    sp.wait_ge(O["y1_set"], j + 1)
                    sp.dma_start(y_of(j + EXPERTS), yb[0][:]).then_inc(O["y_stored"], 16)
                    sp.wait_ge(O["y_stored"], j * 16 + 16)
                    sp.sem_inc(O["through"], 1)

                further_blocks(sp, further)

            @block.tensor
            def _(pe):
                pe.wait_ge(R["consts"], 1)
                pe.wait_ge(R["both"], 1)
                flat = both[:].rearrange("p t e -> p (t e)")
                nc.tensor.matmul(rank_b[:, 0:NT * EXPERTS], before[:], flat, start=True, stop=True)
                nc.tensor.matmul(rank_b[:, NT * EXPERTS:2 * NT * EXPERTS], E.ones[:], flat, start=True, stop=True).then_inc(R["ranks"], 1)
                pe.wait_ge(R["rowsf"], 1)
                nc.tensor.transpose(rank_b[:, 0:BLOCKS], slot_rows[:], E.ident[0:BLOCKS, 0:BLOCKS]).then_inc(R["turned"], 1)

                def turn_x(x, full):
                    for h in range(2):
                        for c in range(4):
                            last = nc.tensor.transpose(xT_b[h][:, c * P:(c + 1) * P], x[:, (4 * h + c) * P:(4 * h + c + 1) * P], E.ident[:])
                        last.then_inc(full, 1)

                def into_hidden(bank, x, w, full):
                    for d in range(ND):
                        last = nc.tensor.matmul(bank[:], x[:, d, :], w[:, d, :], start=(d == 0), stop=(d == ND - 1))
                    last.then_inc(full, 1)

                def turn_h(full):
                    for c in range(NHC):
                        last = nc.tensor.transpose(hT_b[:, c * P:(c + 1) * P], hid[:, c * P:(c + 1) * P], E.ident[:])
                    last.then_inc(full, 1)

                def down(w, full):
                    for h in range(2):
                        for c in range(NHC):
                            last = nc.tensor.matmul(down_b[h][:], hT[:, c, :], w[:, c, h * HALF:(h + 1) * HALF], start=(c == 0), stop=(c == NHC - 1))
                        last.then_inc(full, 1)

                pe.wait_ge(xg_in[0], 16)
                turn_x(xg[0], M["xT_full"])

                def step(b, s, i):
                    pe.wait_ge(M["xT_set"], 2 * b + 2)
                    pe.wait_ge(wg_in[s], 16 * i + 16)
                    need(pe, M["act_set"], b)
                    into_hidden(gate_b, xT[s], wg[s], M["gate_full"])
                    pe.wait_ge(wu_in[s], 16 * i + 16)
                    need(pe, M["hid_set"], b)
                    into_hidden(up_b, xT[s], wu[s], M["up_full"])
                    if not (isinstance(b, int) and b + 1 >= EXPERTS):
                        pe.wait_ge(xg_in[1 - s], 16 * i + 16 * s + 16)
                        turn_x(xg[1 - s], M["xT_full"])
                    if not (isinstance(b, int) and b == 0):
                        down_of(b - 1, 1 - s, i - (1 - s))
                    pe.wait_ge(M["hid_set"], b + 1)
                    need(pe, M["hT_set"], b)
                    turn_h(M["hT_full"])

                def down_of(b, s, i):
                    pe.wait_ge(M["hT_set"], b + 1)
                    pe.wait_ge(wd_in[s], 16 * i + 16)
                    need(pe, M["y0_set"], b)
                    need(pe, M["y1_set"], b)
                    down(wd[s], M["down_full"])

                blocks_in_turn(pe, step)
                down_of(EXPERTS - 1, 1, EXPERTS // 2 - 1)

                def further(j):
                    pe.wait_ge(O["xg_landed"], j * 16 + 16)
                    turn_x(xg[0], O["xT_full"])
                    pe.wait_ge(O["xT_set"], 2 * j + 2)
                    pe.wait_ge(O["w_landed"], j * 48 + 48)
                    into_hidden(gate_b, xT[0], wg[0], O["gate_full"])
                    into_hidden(up_b, xT[0], wu[0], O["up_full"])
                    pe.wait_ge(O["hid_set"], j + 1)
                    turn_h(O["hT_full"])
                    pe.wait_ge(O["hT_set"], j + 1)
                    down(wd[0], O["down_full"])

                pe.wait_ge(M["y0_set"], EXPERTS)
                pe.wait_ge(M["y1_set"], EXPERTS)
                further_blocks(pe, further)

            @block.gpsimd
            def _(pool):
                own = E.sem("route_pool")
                nc.gpsimd.memset(zero_i[:], 0).then_inc(own, 1)
                nc.gpsimd.memset(zeros[:], 0.0).then_inc(own, 1)
                nc.gpsimd.memset(before[:], 1.0).then_inc(own, 1)
                pool.wait_ge(own, 3)
                nc.gpsimd.affine_select(out=before[:], in_=before[:], compare_op=ALU.is_gt, fill=0.0, base=0,
                                        pattern=[[1, P]], channel_multiplier=-1).then_inc(own, 1)
                nc.gpsimd.iota(iota_j[:], pattern=[[1, EXPERTS]], base=0, channel_multiplier=0,
                               allow_small_or_imprecise_dtypes=True).then_inc(own, 1)
                nc.gpsimd.iota(e128[:], pattern=[[P, EXPERTS]], base=0, channel_multiplier=0,
                               allow_small_or_imprecise_dtypes=True).then_inc(own, 1)
                nc.gpsimd.iota(token_id[:], pattern=[[P, NT]], base=0, channel_multiplier=1).then_inc(own, 1)
                pool.wait_ge(own, 7)
                pool.sem_inc(R["consts"], 1)
                pool.wait_ge(R["cleared"], 16)
                pool.wait_ge(R["slots"], 1)
                for k in range(TOP_K):
                    for t in range(NT):
                        nc.gpsimd.indirect_dma_start(token_of_slot[:, :], bass.IndirectOffsetOnAxis(ap=E.slot[k][:, t:t + 1], axis=0),
                                                     token_id[:, t:t + 1], None).then_inc(R["scattered"], 16)
                pool.wait_ge(R["idx"], 1)
                gather = lambda to, b: nc.gpsimd.indirect_dma_start(to, None, normed[:, :], bass.IndirectOffsetOnAxis(ap=idx[:, b:b + 1], axis=0))
                for b in range(EXPERTS):
                    if b >= 2:
                        pool.wait_ge(M["xT_full"], 2 * (b - 1))
                    gather(xg[b % 2][:], b).then_inc(xg_in[b % 2], 16)
                pool.wait_ge(M["xT_full"], 2 * EXPERTS)
                pool.wait_ge(R["over"], 1)
                filled = pool.value_load(n_over[0:1, 0:1], min_val=0, max_val=OVER)
                for j in range(OVER):
                    with pool.If(filled > j):
                        if j >= 1:
                            pool.wait_ge(O["xT_full"], 2 * j)
                        gather(xg[0][:], EXPERTS + j).then_inc(O["xg_landed"], 16)

            @block.scalar
            def _(act):
                act.wait_ge(R["gsub"], 1)
                nc.scalar.activation(gexp[:], gexp[:], ACT.Exp).then_inc(R["gexp"], 1)
                act.wait_ge(R["ssub"], 1)
                nc.scalar.activation(sexp[:], sexp[:], ACT.Exp).then_inc(R["sexp"], 1)

                def y0(b, s, i):
                    act.wait_ge(M["down_full"], 2 * b + 1)
                    need(act, y_out[s], 16 * i)
                    nc.scalar.copy(yb[s][:, 0:HALF], down_b[0][:]).then_inc(M["y0_set"], 1)

                def step(b, s, i):
                    act.wait_ge(M["gate_full"], b + 1)
                    need(act, M["hid_set"], b)
                    nc.scalar.activation(act_[:], gate_b[:], ACT.Silu).then_inc(M["act_set"], 1)
                    if not (isinstance(b, int) and b == 0):
                        y0(b - 1, 1 - s, i - (1 - s))
                    act.wait_ge(M["hT_full"], b + 1)
                    nc.scalar.copy(hT[:], hT_b.rearrange("p (c n) -> p c n", n=P)).then_inc(M["hT_set"], 1)

                blocks_in_turn(act, step)
                y0(EXPERTS - 1, 1, EXPERTS // 2 - 1)
                act.wait_ge(y_out[0], 16 * (EXPERTS // 2))

                def further(j):
                    act.wait_ge(O["gate_full"], j + 1)
                    nc.scalar.activation(act_[:], gate_b[:], ACT.Silu).then_inc(O["act_set"], 1)
                    act.wait_ge(O["hT_full"], j + 1)
                    nc.scalar.copy(hT[:], hT_b.rearrange("p (c n) -> p c n", n=P)).then_inc(O["hT_set"], 1)
                    act.wait_ge(O["down_full"], 2 * j + 1)
                    nc.scalar.copy(yb[0][:, 0:HALF], down_b[0][:]).then_inc(O["y0_set"], 1)

                further_blocks(act, further)

            @block.vector
            def _(dve):
                link = Chain(E.dve_chain)
                link.n = E.chain_n
                V = nc.vector
                logits = E.logits
                gl = logits[:, :, 0:N_GROUPS]
                el = logits[:, :, N_GROUPS:NR].rearrange("p t (g e) -> p t g e", g=N_GROUPS)
                each = lambda ap, n: ap.rearrange("p (t o) -> p t o", o=1).broadcast_to([P, NT, n])
                over_t = lambda ap, n: ap.rearrange("p (o n) -> p o n", o=1).broadcast_to([P, NT, n])

                def first_max(values, marks, one, n, top):
                    link(dve, V.tensor_reduce(top[:], values, X, ALU.max))
                    link(dve, V.tensor_tensor(marks, values, each(top[:], n), ALU.is_lt))
                    link(dve, V.scalar_tensor_tensor(marks, marks, float(n), over_t(iota_j[:, 0:n], n), ALU.mult, ALU.add))
                    link(dve, V.tensor_reduce(first[:], marks, X, ALU.min))
                    link(dve, V.tensor_tensor(one, over_t(iota_j[:, 0:n], n), each(first[:], n), ALU.is_equal))

                dve.wait_ge(R["consts"], 1)
                link(dve, V.tensor_reduce(best[:], gl, X, ALU.max))
                V.tensor_tensor(gexp[:], gl, each(best[:], N_GROUPS), ALU.subtract).then_inc(R["gsub"], 1)
                dve.wait_ge(R["gexp"], 1)
                first_max(gexp[:], geq[:], gone[:], N_GROUPS, top1)
                link(dve, V.tensor_reduce(den[:], gexp[:], X, ALU.add))
                link(dve, V.reciprocal(den[:], den[:]))
                link(dve, V.tensor_tensor(gprob[:], top1[:], den[:], ALU.mult))
                wide_g = gone[:].rearrange("p t (g o) -> p t g o", o=1).broadcast_to([P, NT, N_GROUPS, PER_GROUP])
                p4 = lambda x: x.rearrange("p t (g e) -> p t g e", g=N_GROUPS)
                link(dve, V.tensor_tensor(p4(pick[:]), el, wide_g, ALU.mult))
                link(dve, V.tensor_reduce(sel[:], pick[:].rearrange("p t (g e) -> p t e g", g=N_GROUPS), X, ALU.add))
                link(dve, V.tensor_reduce(best[:], sel[:], X, ALU.max))
                V.tensor_tensor(sexp[:], sel[:], each(best[:], PER_GROUP), ALU.subtract).then_inc(R["ssub"], 1)
                dve.wait_ge(R["sexp"], 1)
                first_max(sexp[:], seq[:], one1[:], PER_GROUP, top1)
                link(dve, V.scalar_tensor_tensor(sexp[:], one1[:], -2.0, sexp[:], ALU.mult, ALU.add))
                first_max(sexp[:], seq[:], one2[:], PER_GROUP, top2)
                link(dve, V.tensor_tensor(den[:], top1[:], top2[:], ALU.add))
                link(dve, V.reciprocal(den[:], den[:]))
                link(dve, V.tensor_tensor(den[:], den[:], gprob[:], ALU.mult))
                link(dve, V.tensor_tensor(E.weight[0][:], den[:], top1[:], ALU.mult))
                link(dve, V.tensor_tensor(E.weight[1][:], den[:], top2[:], ALU.mult))
                for one8, one32 in ((one1, one32a), (one2, one32b)):
                    wide_e = one8[:].rearrange("p t (o e) -> p t o e", o=1).broadcast_to([P, NT, N_GROUPS, PER_GROUP])
                    link(dve, V.tensor_tensor(p4(one32[:]), wide_g, wide_e, ALU.mult))
                V.tensor_tensor(both[:], one32a[:], one32b[:], ALU.add).then_inc(R["both"], 1)
                dve.wait_ge(R["ranks"], 1)
                n32 = NT * EXPERTS
                link(dve, V.memset(base[:, 0, :], 0.0))
                for t in range(NT):
                    link(dve, V.tensor_tensor(base[:, t + 1, :], base[:, t, :], rank_b[:, n32 + t * EXPERTS:n32 + (t + 1) * EXPERTS], ALU.add))
                link(dve, V.tensor_tensor(place[:], rank_b[:, 0:n32].rearrange("p (t e) -> p t e", t=NT), base[:, 0:NT, :], ALU.add))
                count = base[:, NT, :]
                link(dve, V.tensor_scalar(nover[:], count, float(P), None, ALU.is_gt))
                for j in range(2, S // P):
                    link(dve, V.scalar_tensor_tensor(nover[:], count, float(j * P), nover[:], ALU.is_gt, ALU.add))
                link(dve, V.tensor_tensor_scan(upto[:], E.ones[:, 0:EXPERTS], nover[:], 0.0, ALU.mult, ALU.add))
                link(dve, V.tensor_tensor(over_at[:], upto[:], nover[:], ALU.subtract))
                link(dve, V.tensor_scalar(over_at[:], over_at[:], float(P), float((EXPERTS - 1) * P), ALU.mult, ALU.add))
                link(dve, V.tensor_tensor(over_at[:], over_at[:], e128[:], ALU.subtract))
                for k, one32 in enumerate((one32a, one32b)):
                    link(dve, V.tensor_tensor(pick[:], one32[:], place[:], ALU.mult))
                    link(dve, V.tensor_reduce(at[:], pick[:], X, ALU.add))
                    link(dve, V.tensor_tensor(pick[:], one32[:], over_t(over_at[:], EXPERTS), ALU.mult))
                    link(dve, V.tensor_reduce(over[:], pick[:], X, ALU.add))
                    link(dve, V.scalar_tensor_tensor(over[:], at[:], float(P), over[:], ALU.is_ge, ALU.mult))
                    link(dve, V.tensor_tensor(at[:], at[:], over[:], ALU.add))
                    link(dve, V.tensor_tensor(pick[:], one32[:], over_t(e128[:], EXPERTS), ALU.mult))
                    link(dve, V.tensor_reduce(over[:], pick[:], X, ALU.add))
                    link(dve, V.tensor_tensor(at[:], at[:], over[:], ALU.add))
                    ins = V.tensor_copy(E.slot[k][:], at[:])
                    if k == 0:
                        link(dve, ins)
                ins.then_inc(R["slots"], 1)
                link(dve, V.tensor_tensor(ovcmp[:], upto[:].rearrange("p (o e) -> p o e", o=1).broadcast_to([P, OVER, EXPERTS]),
                                          iota_j[:, 0:OVER].rearrange("p (j o) -> p j o", o=1).broadcast_to([P, OVER, EXPERTS]), ALU.is_le))
                link(dve, V.tensor_reduce(ovexp[:], ovcmp[:], X, ALU.add))
                link(dve, V.tensor_scalar(ovexp[:], ovexp[:], float(EXPERTS - 1), None, ALU.min))
                link(dve, V.tensor_copy(ovexp_i[:], ovexp[:]))
                V.tensor_copy(n_over[:], upto[:, EXPERTS - 1:EXPERTS]).then_inc(R["over"], 1)
                dve.wait_ge(R["rows"], 16)
                V.tensor_copy(slot_rows[:], slot_rows_i[:]).then_inc(R["rowsf"], 1)
                dve.wait_ge(R["turned"], 1)
                V.tensor_copy(idx[:], rank_b[:, 0:BLOCKS]).then_inc(R["idx"], 1)

                def set_x(to, full, first_full, is_set):
                    for h in range(2):
                        dve.wait_ge(full, first_full + h)
                        for c in range(4):
                            k = 4 * h + c
                            last = V.tensor_scalar(to[:, k, :], xT_b[h][:, c * P:(c + 1) * P], scale[:, k:k + 1], shift[:, k:k + 1], ALU.mult, ALU.add)
                        last.then_inc(is_set, 1)

                set_x(xT[0], M["xT_full"], 1, M["xT_set"])

                def y1(b, s, i):
                    dve.wait_ge(M["down_full"], 2 * b + 2)
                    need(dve, y_out[s], 16 * i)
                    V.tensor_copy(yb[s][:, HALF:D], down_b[1][:]).then_inc(M["y1_set"], 1)

                def step(b, s, i):
                    dve.wait_ge(M["up_full"], b + 1)
                    dve.wait_ge(M["act_set"], b + 1)
                    need(dve, M["hT_full"], b)
                    V.tensor_tensor(hid[:], act_[:], up_b[:], ALU.mult).then_inc(M["hid_set"], 1)
                    if not (isinstance(b, int) and b + 1 >= EXPERTS):
                        set_x(xT[1 - s], M["xT_full"], 2 * b + 3, M["xT_set"])
                    if not (isinstance(b, int) and b == 0):
                        y1(b - 1, 1 - s, i - (1 - s))

                blocks_in_turn(dve, step)
                y1(EXPERTS - 1, 1, EXPERTS // 2 - 1)
                dve.wait_ge(y_out[0], 16 * (EXPERTS // 2))

                def further(j):
                    set_x(xT[0], O["xT_full"], 2 * j + 1, O["xT_set"])
                    dve.wait_ge(O["up_full"], j + 1)
                    dve.wait_ge(O["act_set"], j + 1)
                    V.tensor_tensor(hid[:], act_[:], up_b[:], ALU.mult).then_inc(O["hid_set"], 1)
                    dve.wait_ge(O["down_full"], 2 * j + 2)
                    V.tensor_copy(yb[0][:, HALF:D], down_b[1][:]).then_inc(O["y1_set"], 1)

                further_blocks(dve, further)
                E.chain_n = link.n


def stage_combine(nc, E, A, rows_in, y_slots):
    with ExitStack() as st:
        sb = lambda name, shape, dt=F32: E.sb(name, shape, dt, ctx=st)
        N = 3
        y = [[sb(f"cy{k}_{i}", [P, D]) for i in range(N)] for k in range(TOP_K)]
        x = [sb(f"cx{i}", [P, D]) for i in range(N)]
        sq = sb("c_sq", [P, D])
        gate, gain = sb("gate2", [P, D]), sb("final_gain", [P, D])
        ss, dev, inv = (sb(n, [P, NT]) for n in ("c_ss", "c_dev", "c_inv"))
        rows_landed = E.sem("c_rows")
        x_in, y_in = ([E.sem(f"{n}{i}") for i in range(N)] for n in ("cx_landed", "cy_landed"))
        weighted, summed, scaled, sq_set, dev_set, ready = (E.sem("c_" + n) for n in ("weighted", "summed", "scaled", "sq_set", "dev_set", "ready"))
        with nc.Block() as block:

            @block.sync
            def _(sp):
                sp.dma_start(gate[:], E.gates[:, D:2 * D]).then_inc(rows_landed, 16)
                sp.dma_start(gain[:], A["final_norm_g_2"].rearrange("(o d) -> o d", o=1).broadcast_to([P, D])).then_inc(rows_landed, 16)

                def load(t):
                    sp.dma_start(x[t % N][:], rows_in[t * P:(t + 1) * P, :]).then_inc(x_in[t % N], 16)

                for t in range(N):
                    load(t)
                for t in range(NT):
                    sp.wait_ge(ready, t + 1)
                    sp.dma_start(A["out"][0, t * P:(t + 1) * P, :], x[t % N][:]).then_inc(E.out_stored, 16)
                    if t + N < NT:
                        sp.wait_ge(E.out_stored, 16 * (t + 1))
                        load(t + N)
                sp.wait_ge(E.out_stored, 16 * NT)

            @block.gpsimd
            def _(pool):
                for t in range(NT):
                    if t >= N:
                        pool.wait_ge(summed, t - N + 1)
                    for k in range(TOP_K):
                        nc.gpsimd.indirect_dma_start(y[k][t % N][:], None, y_slots[:, :],
                                                     bass.IndirectOffsetOnAxis(ap=E.slot[k][:, t:t + 1], axis=0)).then_inc(y_in[t % N], 16)

            @block.scalar
            def _(act):
                for t in range(NT + 1):
                    if t < NT:
                        act.wait_ge(y_in[t % N], 32 * (t // N + 1))
                        nc.scalar.activation(y[0][t % N][:], y[0][t % N][:], ACT.Copy, scale=E.weight[0][:, t:t + 1]).then_inc(weighted, 1)
                    if t >= 1:
                        act.wait_ge(scaled, t)
                        nc.scalar.activation(sq[:], x[(t - 1) % N][:], ACT.Square, accum_out=ss[:, t - 1:t]).then_inc(sq_set, 1)
                        act.wait_ge(sq_set, t)
                        nc.scalar.activation(dev[:, t - 1:t], ss[:, t - 1:t], ACT.Sqrt, bias=E.eps_rms[:], scale=1.0 / D).then_inc(dev_set, 1)

            @block.vector
            def _(dve):
                link = Chain(E.dve_chain)
                link.n = E.chain_n
                V = nc.vector
                dve.wait_ge(rows_landed, 32)
                for t in range(NT + 1):
                    if t < NT:
                        y0, y1, xt = y[0][t % N][:], y[1][t % N][:], x[t % N][:]
                        dve.wait_ge(weighted, t + 1)
                        link(dve, V.scalar_tensor_tensor(y0, y1, E.weight[1][:, t:t + 1], y0, ALU.mult, ALU.add))
                        link(dve, V.tensor_tensor(y0, y0, gate[:], ALU.mult))
                        dve.wait_ge(x_in[t % N], 16 * (t // N + 1))
                        V.tensor_tensor(xt, xt, y0, ALU.add).then_inc(scaled, 1)
                        dve.wait_ge(scaled, t + 1)
                        dve.sem_inc(summed, 1)
                    if t >= 1:
                        b = slice(t - 1, t)
                        dve.wait_ge(dev_set, t)
                        link(dve, V.reciprocal(inv[:, b], dev[:, b]))
                        V.scalar_tensor_tensor(x[(t - 1) % N][:], x[(t - 1) % N][:], inv[:, b], gain[:], ALU.mult, ALU.mult).then_inc(ready, 1)
                E.chain_n = link.n


def build_program(nc, A):
    with ExitStack() as ctx:
        E = Env(nc, ctx)
        E.psum = ctx.enter_context(nc.psum_tensor("psum", [P, 8 * HALF], F32))
        E.banks = [E.psum[:, i * HALF:(i + 1) * HALF] for i in range(8)]
        E.dve_chain = E.sem("dve_chain")
        E.chain_n = 0
        E.out_stored = E.sem("out_stored")
        E.ncum_rows = nc.dram_tensor("ncum_rows", (FOX_HEADS, S), F32, kind="Internal").ap()
        x1_rows = nc.dram_tensor("x1_rows", (S, D), F32, kind="Internal").ap()
        x2_rows = nc.dram_tensor("x2_rows", (S, D), F32, kind="Internal").ap()
        x3_rows = nc.dram_tensor("x3_rows", (S, D), F32, kind="Internal").ap()
        n3_rows = nc.dram_tensor("n3_rows", (S, D), F32, kind="Internal").ap()
        token_of_slot = nc.dram_tensor("token_of_slot", (SLOTS, 1), I32, kind="Internal").ap()
        y_slots = nc.dram_tensor("y_slots", (SLOTS, D), F32, kind="Internal").ap()
        x0_rows = A["x"].rearrange("o t d -> (o t) d")
        E.ident = E.sb("ident", [P, P])
        E.ones = E.sb("ones", [P, P])
        E.eps_ln = E.sb("eps_ln", [P, 1])
        E.eps_rms = E.sb("eps_rms", [P, 1])
        E.eps_gn = E.sb("eps_gn", [P, 1])
        E.mod = E.sb("mod", [P, 6 * ND])
        E.causal = E.sb("causal", [P, P])
        E.icount = E.sb("icount", [P, len(POOL_WINDOWS), PAD])
        E.pool_scale = E.sb("pool_scale", [P, ND])
        E.b_forget = E.sb("b_forget_col", [FOX_HEADS, 1])
        E.gates = nc.dram_tensor("gate_rows_dram", (P, 2 * D), F32, kind="Internal").ap()
        E.v_dram, E.yi_dram = (nc.dram_tensor(x, (P, NT, RW), F32, kind="Internal").ap() for x in ("v_rows", "yi_rows"))
        E.mt_dram, E.n_dram, E.qt_dram = (nc.dram_tensor(x, (P, NPAIR * S), F32, kind="Internal").ap() for x in ("mt", "n", "qt"))
        E.n_small, E.n_masks = 12, 1
        far = lambda name, st: E.sb(name, [P, ND, S], ctx=st, side="right")
        halves = lambda name, st: [E.sb(name + n, [P, ND, S], F32R, ctx=st) for n in ("_hi", "_lo")]
        with ExitStack() as first:
            E.yT = E.sb("yT", [P, NY, S], ctx=first)
            with ExitStack() as memory:
                E.memT = E.sb("memT", [P, ND, N_MEM], ctx=memory)
                E.mkT = E.sb("mkT", [P, MEM_HEADS, N_MEM], ctx=memory)
                E.mv = E.sb("mv", [P, NM, HALF], ctx=memory)
                with ExitStack() as whole:
                    E.xT = far("x0T", whole)
                    E.run(stage_constants, A)
                    split = ExitStack()
                    E.x_hi, E.x_lo = halves("x0", split)
                    E.run(stage_memory_kv, A, 0, split_x=True)
                with split:
                    E.run(stage_layer0, A)
                whole = ExitStack()
                E.xT = far("x1T", whole)
                E.run(stage_out, A, 0, x0_rows, x1_rows)
                E.run(stage_forget, A)
                E.run(stage_memory_kv, A, 1)
                E.run(stage_memory_heads, A, 1)
            with ExitStack() as split:
                with whole:
                    E.x_hi, E.x_lo = halves("x1", split)
                    E.run(stage_split_x, A)
                E.run(stage_fox, A)
            E.xT = far("hT", ctx)
            E.run(stage_out, A, 1, x1_rows, x2_rows, modulate=True)
        E.logits = E.sb("logits", [P, NT, N_GROUPS + EXPERTS])
        with ExitStack() as second:
            E.bonus = E.sb("bonus", [P, NT, 2 * NPAIR], ctx=second)
            E.carry = E.sb("carry", [P, NPAIR, NC], ctx=second)
            E.ident2 = E.sb("ident2", [P, HD], ctx=second)
            E.xg = E.sb("xg", [GATE_LORA, S], ctx=second)
            E.hT = E.xT
            E.run(stage_rwkv_pairs, A)
            E.run(stage_mix, A, x2_rows, x3_rows, n3_rows)
        with ExitStack() as third:
            E.slot = [E.sb(f"slot{k}", [P, NT], I32, ctx=third) for k in range(TOP_K)]
            E.weight = [E.sb(f"weight{k}", [P, NT], ctx=third) for k in range(TOP_K)]
            E.run(stage_experts, A, n3_rows, token_of_slot, y_slots)
            E.run(stage_combine, A, x3_rows, y_slots)


COLUMNS = ("pool_scale", "c_2", "ada_b_2", "norm1_g_2", "norm2_g_2", "rwkv_w0_2", "rwkv_a0_2", "rwkv_k_k_2", "rwkv_k_a_2", "rwkv_r_k_2")


def kernel(**inputs):
    import numpy as _np
    import concourse.bacc as _bacc
    from concourse import mybir as _mybir
    from concourse.bass_utils import run_bass_kernel_spmd as _run

    nc = _bacc.Bacc("TRN2", target_bir_lowering=False, num_devices=1)
    arrays, A = {}, {}
    for name in COLUMNS:
        if name in inputs:
            inputs[name + "_cols"] = _np.asarray(inputs[name]).reshape(-1, P).T
    mu = _np.asarray(inputs["rwkv_mu_2"]).reshape(-1)
    inputs["mu_main_cols"] = mu[:3 * RW].reshape(-1, P).T
    inputs["mu_w_col"], inputs["mu_a_col"], inputs["mu_g_col"] = (
        mu[a:b].reshape(-1, 1) for a, b in ((3 * RW, 3 * RW + LORA), (3 * RW + LORA, 3 * RW + 2 * LORA), (3 * RW + 2 * LORA, None)))
    inputs["gmlp_bs_cols"] = _np.asarray(inputs["gmlp_bs_2"])[0].T
    for name, a in inputs.items():
        a = _np.ascontiguousarray(a)
        arrays[f"in_{name}"] = a
        A[name] = nc.dram_tensor(f"in_{name}", a.shape, _mybir.dt.from_np(a.dtype), kind="ExternalInput").ap()
    A["out"] = nc.dram_tensor("result", (1, S, D), F32, kind="ExternalOutput").ap()
    build_program(nc, A)
    r = _run(nc, [arrays], core_ids=[0])
    return r.results[0]["result"]
```

```python
import math
from contextlib import ExitStack

import concourse.bass as bass
from concourse import mybir

F32 = mybir.dt.float32
F32R = mybir.dt.float32r
BF16 = mybir.dt.bfloat16
I32 = mybir.dt.int32
U32 = mybir.dt.uint32
ALU = mybir.AluOpType
ACT = mybir.ActivationFunctionType
X = mybir.AxisListType.X

P = 128
D = 1024
S = 1024
NT = S // P
ND = D // P
HALF = 512
NH = S // HALF
DEPTH = 2
ALPHA = (2 * DEPTH) ** 0.25
LN_EPS = 1e-5
RMS_EPS = 1e-6
GN_EPS = 64e-5
N_MEM = 256
NM = N_MEM // P
MEM_HEADS = 4
MEM_SCALE = 128.0 ** -0.5
NY = ND + MEM_HEADS
GATE0 = NY
POOL_WINDOWS = (2, 4, 8, 16)
PAD = 16
FOX_HEADS = 16
FOX_SCALE = 64.0 ** -0.5
MASKED = -1.0e30


class Ring:

    def __init__(self, banks, full, free):
        self.banks, self.full, self.free = banks, full, free
        self.n, self.at = 0, {}

    def take(self, key):
        self.at[key] = self.n
        self.n += 1
        before = self.n - len(self.banks)
        return self.banks[self.at[key] % len(self.banks)], (before if before > 0 else None)

    def nth(self, key):
        return self.at[key] + 1

    def bank(self, key):
        return self.banks[self.at[key] % len(self.banks)]


class Chain:

    def __init__(self, sem):
        self.sem, self.n = sem, 0

    def __call__(self, eng, ins):
        ins.then_inc(self.sem, 1)
        self.n += 1
        eng.wait_ge(self.sem, self.n)


class Env:

    def __init__(self, nc, ctx):
        self.nc, self.ctx = nc, ctx
        self.of_stage = None

    def sem(self, name):
        if self.of_stage is None:
            return self.ctx.enter_context(self.nc.semaphore(name))
        self.of_stage.append(self.nc.alloc_semaphore(name=name))
        return self.of_stage[-1]

    def run(self, stage, *args, **options):
        self.of_stage = []
        stage(self.nc, self, *args, **options)
        self.nc.clear_and_free_semaphores(self.of_stage)
        self.nc.all_engine_barrier()
        self.of_stage = None

    def sb(self, name, shape, dt=F32, ctx=None, **options):
        return (ctx or self.ctx).enter_context(self.nc.sbuf_tensor(name, shape, dt, **options))


def wait(eng, sem, value):
    if value is not None and value > 0:
        eng.wait_ge(sem, value)


class SplitX:

    def __init__(self, nc, E, name):
        self.nc, self.E = nc, E
        self.hi_set = E.sem(name + "_x_hi_set")

    def round(self, act):
        for d in range(ND):
            self.nc.scalar.copy(self.E.x_hi[:, d, :], self.E.xT[:, d, :]).then_inc(self.hi_set, 1)

    def rest(self, dve):
        E = self.E
        for d in range(ND):
            dve.wait_ge(self.hi_set, d + 1)
            self.nc.vector.tensor_tensor(E.x_lo[:, d, :], E.xT[:, d, :], E.x_hi[:, d, :].bitcast(F32), ALU.subtract)


class SplitProducts:

    def __init__(self, nc, E, name, st, used):
        self.nc, self.E, self.used = nc, E, used
        self.slots = [E.sb(f"{name}_{i}", [P, ND, P], ctx=st) for i in range(2)]
        self.landed = [E.sem(f"{name}_landed{i}") for i in range(2)]
        self.hi, self.lo = ([E.sb(f"{name}_{x}{i}", [P, ND, P], F32R, ctx=st) for i in range(2)] for x in ("hi", "lo"))
        self.hi_set, self.split = E.sem(name + "_hi_set"), E.sem(name + "_split")

    def load(self, sp, n, src):
        if n >= 2:
            sp.wait_ge(self.split, n - 1)
        sp.dma_start(self.slots[n % 2][:], src).then_inc(self.landed[n % 2], 16)

    def split_weights(self, pool, end, start=0):
        for n in range(start, end):
            b = n % 2
            if n >= 2:
                self.used(pool, n - 2)
            pool.wait_ge(self.landed[b], 16 * (n // 2 + 1))
            self.nc.gpsimd.tensor_copy(self.hi[b][:], self.slots[b][:]).then_inc(self.hi_set, 1)
            pool.wait_ge(self.hi_set, n + 1)
            self.nc.gpsimd.tensor_tensor(self.lo[b][:], self.slots[b][:], self.hi[b][:].bitcast(F32), ALU.subtract).then_inc(self.split, 1)

    def project(self, pe, bank, n, hf):
        E, cols = self.E, slice(hf * HALF, (hf + 1) * HALF)
        pe.wait_ge(self.split, n + 1)
        hi, lo = self.hi[n % 2], self.lo[n % 2]
        for d in range(ND):
            self.nc.tensor.matmul(bank[:], hi[:, d, :], E.x_hi[:, d, cols], start=(d == 0), stop=False)
            self.nc.tensor.matmul(bank[:], hi[:, d, :], E.x_lo[:, d, cols], start=False, stop=False)
            last = self.nc.tensor.matmul(bank[:], lo[:, d, :], E.x_hi[:, d, cols], start=False, stop=(d == ND - 1))
        return last


def stage_constants(nc, E, A):
    with ExitStack() as st:
        mem_rows = E.sb("mem_rows", [P, NM, D], ctx=st)
        x_rows = E.sb("x_rows", [P, NT, D], ctx=st)
        x_landed = E.sem("x_landed")
        x_landed2 = E.sem("x_landed2")
        mem_landed = E.sem("mem_landed")
        id_set = E.sem("id_set")
        turned = Ring(E.banks[0:4], E.sem("turn_full"), E.sem("turn_free"))
        turned2 = Ring(E.banks[4:8], E.sem("turn2_full"), E.sem("turn2_free"))
        small_landed = E.sem("small_landed")
        const_set = E.sem("const_set")
        groups = [("mem", m, h) for m in range(NM) for h in range(2)]
        groups += [("x", t, h) for t in range(NT) for h in range(2)]

        with nc.Block() as block:

            @block.sync
            def _(sp):
                sp.dma_start(mem_rows[:], A["mem"].rearrange("o (m p) d -> p (o m) d", p=P)).then_inc(mem_landed, 16)
                xv = A["x"].rearrange("o (t p) d -> p (o t) d", p=P)
                sp.dma_start(x_rows[:, 0:4, :], xv[:, 0:4, :]).then_inc(x_landed, 16)
                sp.dma_start(x_rows[:, 4:8, :], xv[:, 4:8, :]).then_inc(x_landed2, 16)
                sp.dma_start(E.pool_scale[:], A["pool_scale_cols"]).then_inc(small_landed, 16)
                sp.dma_start(E.b_forget[:], A["b_forget"].rearrange("(h o) -> h o", o=1)).then_inc(small_landed, 16)
                wv = A["w_mem_kv"][0].rearrange("(c p) n -> p c n", p=P)
                for i in range(2):
                    sp.dma_start(E.kv_w[i][:], wv[:, :, i * HALF:(i + 1) * HALF]).then_inc(E.kv_landed[i], 16)
                sp.wait_ge(small_landed, 32)

            @block.gpsimd
            def _(pool):
                nc.gpsimd.memset(E.ident[:], 0.0).then_inc(id_set, 1)
                nc.gpsimd.memset(E.causal[:], 0.0).then_inc(id_set, 1)
                pool.wait_ge(id_set, 2)
                nc.gpsimd.affine_select(out=E.ident[:], in_=E.ident[:], compare_op=ALU.not_equal, fill=1.0, base=0,
                                        pattern=[[-1, P]], channel_multiplier=1).then_inc(id_set, 1)
                nc.gpsimd.affine_select(out=E.causal[:], in_=E.causal[:], compare_op=ALU.is_ge, fill=MASKED, base=0,
                                        pattern=[[-1, P]], channel_multiplier=1).then_inc(id_set, 1)
                for g, w in enumerate(POOL_WINDOWS):
                    nc.gpsimd.iota(E.icount[:, g, :], pattern=[[1, PAD]], base=1, channel_multiplier=0,
                                   allow_small_or_imprecise_dtypes=True).then_inc(const_set, 1)

            @block.tensor
            def _(pe):
                pe.wait_ge(id_set, 4)
                for n, (what, t, h) in enumerate(groups):
                    if what == "mem" and n == 0:
                        pe.wait_ge(mem_landed, 16)
                    if what == "x" and h == 0 and t == 0:
                        pe.wait_ge(x_landed, 16)
                    if what == "x" and h == 0 and t == 4:
                        pe.wait_ge(x_landed2, 16)
                    ring = turned if n % 2 == 0 else turned2
                    bank, free = ring.take(n)
                    wait(pe, ring.free, free)
                    rows = mem_rows if what == "mem" else x_rows
                    for c in range(4):
                        last = nc.tensor.transpose(bank[:, c * P:(c + 1) * P], rows[:, t, (4 * h + c) * P:(4 * h + c + 1) * P], E.ident[:])
                    last.then_inc(ring.full, 1)

            def evacuate(eng, copy, ring, parity):
                for n, (what, t, h) in enumerate(groups):
                    if n % 2 != parity:
                        continue
                    eng.wait_ge(ring.full, ring.nth(n))
                    to = E.memT if what == "mem" else E.xT
                    copy(to[:, 4 * h:4 * h + 4, t * P:(t + 1) * P],
                         ring.bank(n).rearrange("p (c n) -> p c n", c=4)).then_inc(ring.free, 1)

            @block.scalar
            def _(act):
                evacuate(act, nc.scalar.copy, turned, 0)

            @block.vector
            def _(dve):
                link = Chain(E.dve_chain)
                link.n = E.chain_n
                dve.wait_ge(const_set, len(POOL_WINDOWS))
                for g, w in enumerate(POOL_WINDOWS):
                    link(dve, nc.vector.tensor_scalar(E.icount[:, g, :], E.icount[:, g, :], float(w), None, ALU.min))
                link(dve, nc.vector.reciprocal(E.icount[:], E.icount[:]))
                link(dve, nc.vector.memset(E.ones[:], 1.0))
                link(dve, nc.vector.memset(E.eps_ln[:], LN_EPS))
                link(dve, nc.vector.memset(E.eps_rms[:], RMS_EPS))
                link(dve, nc.vector.memset(E.eps_gn[:], GN_EPS))
                evacuate(dve, nc.vector.tensor_copy, turned2, 1)
                E.chain_n = link.n


def stage_memory_kv(nc, E, A):
    with ExitStack() as st:
        halves, landed = E.kv_w, E.kv_landed
        ring = Ring(E.banks, E.sem("mkv_full"), E.sem("mkv_free"))
        split = SplitX(nc, E, "kv")
        with nc.Block() as block:

            @block.tensor
            def _(pe):
                pe.wait_ge(landed[0], 16)
                for h in range(MEM_HEADS):
                    bank, _ = ring.take(("k", h))
                    for c in range(ND):
                        last = nc.tensor.matmul(bank[:, 0:N_MEM], halves[0][:, c, h * P:(h + 1) * P], E.memT[:, c, :],
                                                start=(c == 0), stop=(c == ND - 1))
                    last.then_inc(ring.full, 1)
                pe.wait_ge(landed[1], 16)
                for m in range(NM):
                    bank, _ = ring.take(("v", m))
                    for c in range(ND):
                        last = nc.tensor.matmul(bank[:], E.memT[:, c, m * P:(m + 1) * P], halves[1][:, c, :],
                                                start=(c == 0), stop=(c == ND - 1))
                    last.then_inc(ring.full, 1)

            @block.scalar
            def _(act):
                split.round(act)
                for h in range(MEM_HEADS):
                    act.wait_ge(ring.full, ring.nth(("k", h)))
                    nc.scalar.copy(E.mkT[:, h, :], ring.bank(("k", h))[:, 0:N_MEM])
                for m in range(NM):
                    act.wait_ge(ring.full, ring.nth(("v", m)))
                    nc.scalar.copy(E.mv[:, m, :], ring.bank(("v", m))[:])

            @block.vector
            def _(dve):
                split.rest(dve)


def stage_split_x(nc, E, A):
    split = SplitX(nc, E, "x")
    with nc.Block() as block:

        @block.scalar
        def _(act):
            split.round(act)

        @block.vector
        def _(dve):
            split.rest(dve)


class MemoryAttention:

    def __init__(self, nc, E, layer, ringA, ringD, st):
        self.nc, self.E, self.ringA, self.ringD = nc, E, ringA, ringD
        n = f"{layer}"
        self.probs = E.sb("mem_probs" + n, [P, NT, N_MEM], ctx=st)
        self.probsT = E.sb("mem_probsT" + n, [P, NM, S], ctx=st)
        self.top = E.sb("mem_top" + n, [P, NT], ctx=st)
        self.bias = E.sb("mem_bias" + n, [P, NT], ctx=st)
        self.total = E.sb("mem_total" + n, [P, NT], ctx=st)
        self.inv = E.sb("mem_inv" + n, [P, NT], ctx=st)
        self.bias_set = E.sem("mem_bias_set" + n)
        self.scaled = E.sem("mem_scaled" + n)

    def scores(self, pe, h, qT):
        nc, ring = self.nc, self.ringA
        for tp in range(NT // 2):
            bank, free = ring.take(("s", h, tp))
            wait(pe, ring.free, free)
            for j in range(2):
                t = 2 * tp + j
                last = nc.tensor.matmul(bank[:, j * N_MEM:(j + 1) * N_MEM], qT[:, t * P:(t + 1) * P], self.E.mkT[:, h, :],
                                        start=True, stop=True)
            last.then_inc(ring.full, 1)

    def turn(self, pe, h):
        nc, ring = self.nc, self.ringA
        for tp in range(NT // 2):
            bank, free = ring.take(("t", h, tp))
            wait(pe, ring.free, free)
            pe.wait_ge(self.scaled, h * (NT // 2) + tp + 1)
            for m in range(NM):
                for j in range(2):
                    last = nc.tensor.transpose(bank[:, (2 * m + j) * P:(2 * m + j + 1) * P],
                                               self.probs[:, 2 * tp + j, m * P:(m + 1) * P], self.E.ident[:])
            last.then_inc(ring.full, 1)

    def values(self, pe, h):
        nc, ring = self.nc, self.ringD
        pe.wait_ge(self.ringA.free, self.ringA.nth(("t", h, NT // 2 - 1)))
        for hf in range(NH):
            bank, free = ring.take(("o", h, hf))
            wait(pe, ring.free, free)
            for m in range(NM):
                last = nc.tensor.matmul(bank[:], self.E.mv[:, m, h * P:(h + 1) * P], self.probsT[:, m, hf * HALF:(hf + 1) * HALF],
                                        start=(m == 0), stop=(m == NM - 1))
            last.then_inc(ring.full, 1)

    def maxima(self, dve, link, h):
        nc, ring = self.nc, self.ringA
        for tp in range(NT // 2):
            dve.wait_ge(ring.full, ring.nth(("s", h, tp)))
            tt = slice(2 * tp, 2 * tp + 2)
            if h > 0:
                dve.wait_ge(ring.free, ring.nth(("s", h - 1, tp)))
            link(dve, nc.vector.tensor_reduce(self.top[:, tt], ring.bank(("s", h, tp)).rearrange("p (j n) -> p j n", j=2), X, ALU.max))
            nc.vector.tensor_scalar(self.bias[:, tt], self.top[:, tt], -MEM_SCALE, None, ALU.mult).then_inc(self.bias_set, 1)

    def normalise(self, dve, link, h):
        nc = self.nc
        for tp in range(NT // 2):
            dve.wait_ge(self.ringA.free, self.ringA.nth(("s", h, tp)))
            tt = slice(2 * tp, 2 * tp + 2)
            link(dve, nc.vector.reciprocal(self.inv[:, tt], self.total[:, tt]))
            nc.vector.tensor_scalar(self.probs[:, 2 * tp, :], self.probs[:, 2 * tp, :], self.inv[:, 2 * tp:2 * tp + 1], None, ALU.mult)
            nc.vector.tensor_scalar(self.probs[:, 2 * tp + 1, :], self.probs[:, 2 * tp + 1, :], self.inv[:, 2 * tp + 1:2 * tp + 2], None,
                                    ALU.mult).then_inc(self.scaled, 1)

    def gate(self, dve, h):
        nc, ring = self.nc, self.ringD
        for hf in range(NH):
            dve.wait_ge(ring.full, ring.nth(("o", h, hf)))
            cols = slice(hf * HALF, (hf + 1) * HALF)
            nc.vector.tensor_tensor(self.E.yT[:, ND + h, cols], ring.bank(("o", h, hf))[:], self.E.yT[:, ND + h, cols], ALU.mult).then_inc(ring.free, 1)

    def exps(self, act, h):
        nc, ring = self.nc, self.ringA
        for tp in range(NT // 2):
            act.wait_ge(self.bias_set, h * (NT // 2) + tp + 1)
            if h > 0:
                act.wait_ge(ring.full, ring.nth(("t", h - 1, tp)))
            for j in range(2):
                t = 2 * tp + j
                last = nc.scalar.activation(self.probs[:, t, :], ring.bank(("s", h, tp))[:, j * N_MEM:(j + 1) * N_MEM], ACT.Exp,
                                            bias=self.bias[:, t:t + 1], scale=MEM_SCALE, accum_out=self.total[:, t:t + 1])
            last.then_inc(ring.free, 1)

    def evacuate(self, act, h):
        nc, ring = self.nc, self.ringA
        for tp in range(NT // 2):
            act.wait_ge(ring.full, ring.nth(("t", h, tp)))
            if h > 0 and tp == 0:
                act.wait_ge(self.ringD.full, self.ringD.nth(("o", h - 1, NH - 1)))
            nc.scalar.copy(self.probsT[:, :, tp * 2 * P:(tp + 1) * 2 * P],
                           ring.bank(("t", h, tp)).rearrange("p (m n) -> p m n", m=NM)).then_inc(ring.free, 1)


def stage_layer0(nc, E, A):
    with ExitStack() as st:
        pool_w = [E.sb(f"pool_w{i}", [P, 2, 256], ctx=st) for i in range(2)]
        pool_w_landed = [E.sem(f"pool_w_landed{i}") for i in range(2)]
        uT = [E.sb(f"uT{c}", [P, PAD + S], ctx=st) for c in range(2)]
        qT = E.sb("qT0", [P, S], ctx=st)
        sums = [E.sb(f"sums{c}", [P, PAD + S], ctx=st) for c in range(2)]
        pm = [E.sb(f"pm{c}", [P, S], ctx=st) for c in range(2)]
        edge = E.sb("edge", [P, PAD], ctx=st)
        ringA = Ring(E.banks[0:4], E.sem("l0A_full"), E.sem("l0A_free"))
        ringD = Ring(E.banks[4:8], E.sem("l0D_full"), E.sem("l0D_free"))
        pm_set = E.sem("pm_set")
        attn = MemoryAttention(nc, E, 0, ringA, ringD, st)
        win = A["w_in"][0].rearrange("(c p) n -> p c n", p=P)
        G = len(POOL_WINDOWS)
        order = []
        for g in range(G):
            order += [("u", 0, 2 * g), ("u", 1, 2 * g + 1), ("g", 0, GATE0 + 2 * g), ("g", 1, GATE0 + 2 * g + 1),
                      ("q", 0, ND + g), ("m", 0, GATE0 + ND + g)]

        def used(eng, n):
            kind, c, _ = order[n]
            ring = ringD if kind in "uq" else ringA
            eng.wait_ge(ring.full, ring.nth((kind, n // 6, c, NH - 1)))

        split = SplitProducts(nc, E, "w0", st, used)

        def evacuate_dve(dve, g):
            for kind, c in (("u", 0), ("u", 1), ("q", 0)):
                for hf in range(NH):
                    key = (kind, g, c, hf)
                    dve.wait_ge(ringD.full, ringD.nth(key))
                    if kind == "u":
                        to = uT[c][:, PAD + hf * HALF:PAD + (hf + 1) * HALF]
                    else:
                        if g > 0 and hf == 0:
                            dve.wait_ge(ringA.full, ringA.nth(("s", g - 1, NT // 2 - 1)))
                        to = qT[:, hf * HALF:(hf + 1) * HALF]
                    nc.vector.tensor_copy(to, ringD.bank(key)[:]).then_inc(ringD.free, 1)

        with nc.Block() as block:

            @block.tensor
            def _(pe):
                def project(g):
                    for kind, c, col in order[6 * g:6 * g + 6]:
                        n = 6 * g + (("u", "u", "g", "g", "q", "m").index(kind) + (c if kind in "ug" else 0))
                        ring = ringD if kind in "uq" else ringA
                        for hf in range(NH):
                            bank, free = ring.take((kind, g, c, hf))
                            wait(pe, ring.free, free)
                            split.project(pe, bank, n, hf).then_inc(ring.full, 1)

                project(0)
                for g in range(G):
                    pe.wait_ge(ringD.free, ringD.nth(("q", g, 0, 1)))
                    attn.scores(pe, g, qT)
                    if g + 1 < G:
                        project(g + 1)
                    attn.turn(pe, g)
                    attn.values(pe, g)
                    pe.wait_ge(pm_set, 2 * (g + 1))
                    pe.wait_ge(pool_w_landed[g % 2], 16 * (g // 2 + 1))
                    for c in range(2):
                        for hf in range(NH):
                            bank, free = ringD.take(("mix", g, c, hf))
                            wait(pe, ringD.free, free)
                            for k in range(2):
                                last = nc.tensor.matmul(bank[:], pool_w[g % 2][:, k, c * P:(c + 1) * P], pm[k][:, hf * HALF:(hf + 1) * HALF],
                                                        start=(k == 0), stop=(k == 1))
                            last.then_inc(ringD.full, 1)

            @block.sync
            def _(sp):
                for n, (kind, c, col) in enumerate(order):
                    split.load(sp, n, win[:, :, col * P:(col + 1) * P])
                    if n % 6 == 1:
                        g = n // 6
                        if g > 1:
                            sp.wait_ge(ringD.full, ringD.nth(("mix", g - 2, 1, NH - 1)))
                        sp.dma_start(pool_w[g % 2][:], A["pool_w"][0, g].rearrange("(k p) d -> p k d", p=P)).then_inc(pool_w_landed[g % 2], 16)

            @block.gpsimd
            def _(pool):
                split.split_weights(pool, len(order))

            @block.scalar
            def _(act):
                def gates(g):
                    for kind, c in (("g", 0), ("g", 1), ("m", 0)):
                        for hf in range(NH):
                            key = (kind, g, c, hf)
                            act.wait_ge(ringA.full, ringA.nth(key))
                            to = E.yT[:, 2 * g + c if kind == "g" else ND + g, :]
                            nc.scalar.activation(to[:, hf * HALF:(hf + 1) * HALF], ringA.bank(key)[:], ACT.Silu).then_inc(ringA.free, 1)

                gates(0)
                for g in range(G):
                    attn.exps(act, g)
                    if g + 1 < G:
                        gates(g + 1)
                    attn.evacuate(act, g)

            @block.vector
            def _(dve):
                link = Chain(E.dve_chain)
                link.n = E.chain_n
                for c in range(2):
                    link(dve, nc.vector.memset(uT[c][:, 0:PAD], 0.0))
                    link(dve, nc.vector.memset(sums[c][:, 0:PAD], 0.0))

                def pool_mean(g, c):
                    u = uT[c]
                    before, at = u, 0
                    step = 1
                    while step < POOL_WINDOWS[g]:
                        to = sums[at]
                        link(dve, nc.vector.tensor_tensor(to[:, PAD:PAD + S], before[:, PAD:PAD + S], before[:, PAD - step:PAD + S - step], ALU.add))
                        before, at, step = to, 1 - at, 2 * step
                    if g > 0 and c == 0:
                        dve.wait_ge(ringD.full, ringD.nth(("mix", g - 1, 1, NH - 1)))
                    nc.vector.scalar_tensor_tensor(pm[c][:, PAD:S], before[:, 2 * PAD:PAD + S], 1.0 / POOL_WINDOWS[g], u[:, 2 * PAD:PAD + S],
                                                   ALU.mult, ALU.subtract)
                    link(dve, nc.vector.tensor_tensor(edge[:], before[:, PAD:2 * PAD], E.icount[:, g, :], ALU.mult))
                    link(dve, nc.vector.tensor_tensor(pm[c][:, 0:PAD], edge[:], u[:, PAD:2 * PAD], ALU.subtract))
                    dve.sem_inc(pm_set, 1)

                evacuate_dve(dve, 0)
                for g in range(G):
                    attn.maxima(dve, link, g)
                    attn.normalise(dve, link, g)
                    dve.wait_ge(ringD.free, ringD.nth(("u", g, 1, NH - 1)))
                    pool_mean(g, 0)
                    pool_mean(g, 1)
                    if g + 1 < G:
                        evacuate_dve(dve, g + 1)
                    dve.wait_ge(ringA.free, ringA.nth(("m", g, 0, NH - 1)))
                    attn.gate(dve, g)
                    for c in range(2):
                        for hf in range(NH):
                            key = ("mix", g, c, hf)
                            cols = slice(hf * HALF, (hf + 1) * HALF)
                            dve.wait_ge(ringD.full, ringD.nth(key))
                            dve.wait_ge(ringA.free, ringA.nth(("g", g, c, hf)))
                            nc.vector.scalar_tensor_tensor(E.yT[:, 2 * g + c, cols], ringD.bank(key)[:], E.pool_scale[:, 2 * g + c:2 * g + c + 1],
                                                           E.yT[:, 2 * g + c, cols], ALU.mult, ALU.mult).then_inc(ringD.free, 1)
                E.chain_n = link.n


class NormTurn:

    def __init__(self, nc, E, name, ring, st, rows_set, to, scale, shift):
        self.nc, self.E, self.ring, self.rows_set, self.to, self.scale, self.shift = nc, E, ring, rows_set, to, scale, shift
        self.rows = [E.sb(f"{name}_rows{i}", [P, D], ctx=st) for i in range(2)]
        self.ssq, self.dev, self.inv = (E.sb(f"{name}_{x}", [P, 2], ctx=st) for x in ("ssq", "dev", "inv"))
        self.sq_set, self.dev_set, self.xn_set = (E.sem(f"{name}_{x}") for x in ("sq_set", "dev_set", "xn_set"))
        self.stored = None

    def square(self, act, x, t):
        nc, b = self.nc, slice(t % 2, t % 2 + 1)
        act.wait_ge(self.rows_set, t + 1)
        if t >= 2:
            act.wait_ge(self.ring.full, self.ring.nth(("t", t - 2, 1)))
            if self.stored is not None:
                act.wait_ge(self.stored[t % 2], 16 * (t // 2))
        nc.scalar.activation(self.rows[t % 2][:], x, ACT.Square, accum_out=self.ssq[:, b]).then_inc(self.sq_set, 1)
        act.wait_ge(self.sq_set, t + 1)
        nc.scalar.activation(self.dev[:, b], self.ssq[:, b], ACT.Sqrt, bias=self.E.eps_rms[:], scale=1.0 / D).then_inc(self.dev_set, 1)

    def normalise(self, dve, link, x, t):
        nc, b = self.nc, slice(t % 2, t % 2 + 1)
        dve.wait_ge(self.dev_set, t + 1)
        link(dve, nc.vector.reciprocal(self.inv[:, b], self.dev[:, b]))
        nc.vector.tensor_scalar(self.rows[t % 2][:], x, self.inv[:, b], None, ALU.mult).then_inc(self.xn_set, 1)

    def turn(self, pe, t):
        nc, ring = self.nc, self.ring
        pe.wait_ge(self.xn_set, t + 1)
        for h in range(2):
            bank, free = ring.take(("t", t, h))
            wait(pe, ring.free, free)
            for c in range(4):
                last = nc.tensor.transpose(bank[:, c * P:(c + 1) * P], self.rows[t % 2][:, (4 * h + c) * P:(4 * h + c + 1) * P], self.E.ident[:])
            last.then_inc(ring.full, 1)

    def evacuate(self, act, t):
        nc, ring = self.nc, self.ring
        for h in range(2):
            act.wait_ge(ring.full, ring.nth(("t", t, h)))
            for k in range(4):
                c = 4 * h + k
                last = nc.scalar.activation(self.to[:, c, t * P:(t + 1) * P], ring.bank(("t", t, h))[:, k * P:(k + 1) * P], ACT.Identity,
                                            bias=self.shift[:, c:c + 1], scale=self.scale[:, c:c + 1])
            last.then_inc(ring.free, 1)


def stage_out(nc, E, A, layer, rows_in, rows_out, modulate=False):
    n = f"{layer}"
    with ExitStack() as st:
        wo = E.sb("wo" + n, [P, NY, D], ctx=st)
        gain = E.sb("ln_gain" + n, [P, D], ctx=st)
        shift = E.sb("ln_shift" + n, [P, D], ctx=st)
        stats = E.sb("ln_stats" + n, [P, 2, 6], ctx=st)
        mv = E.sb("ln_mv" + n, [P, 2], ctx=st)
        dev = E.sb("ln_dev" + n, [P, 1], ctx=st)
        rstd = E.sb("ln_rstd" + n, [P, 1], ctx=st)
        NX = 3
        xs = [E.sb(f"x_tile{n}_{i}", [P, D], ctx=st) for i in range(NX)]
        x_landed = [E.sem(f"x_tile_landed{n}_{i}") for i in range(NX)]
        stored = [E.sem(f"x_stored{n}_{i}") for i in range(NX)]
        wo_landed = [E.sem(f"wo_landed{n}_{i}") for i in range(6)]
        ln_landed = E.sem("ln_landed" + n)
        var_set, dev_set, rows_set = E.sem("var_set" + n), E.sem("dev_set" + n), E.sem("rows_set" + n)
        ringD = Ring(E.banks[0:4], E.sem("outD_full" + n), E.sem("outD_free" + n))
        ringA = Ring(E.banks[4:8], E.sem("outA_full" + n), E.sem("outA_free" + n))
        norm = NormTurn(nc, E, "n1", ringA, st, rows_set, E.xT, E.mod[:, ND:2 * ND], E.mod[:, 0:ND]) if modulate else None
        with nc.Block() as block:

            @block.tensor
            def _(pe):
                def turn(t):
                    if modulate:
                        norm.turn(pe, t)
                        return
                    pe.wait_ge(rows_set, t + 1)
                    for h in range(2):
                        bank, free = ringA.take(("t", t, h))
                        wait(pe, ringA.free, free)
                        for c in range(4):
                            last = nc.tensor.transpose(bank[:, c * P:(c + 1) * P], xs[t % NX][:, (4 * h + c) * P:(4 * h + c + 1) * P], E.ident[:])
                        last.then_inc(ringA.full, 1)

                for t in range(NT):
                    for hf in range(2):
                        bank, free = ringD.take(("y", t, hf))
                        wait(pe, ringD.free, free)
                        for c in range(NY):
                            if t == 0 and hf == 0 and c % 2 == 0:
                                pe.wait_ge(wo_landed[c // 2], 16)
                            last = nc.tensor.matmul(bank[:], E.yT[:, c, t * P:(t + 1) * P], wo[:, c, hf * HALF:(hf + 1) * HALF],
                                                    start=(c == 0), stop=(c == NY - 1))
                        last.then_inc(ringD.full, 1)
                    if t > 0:
                        turn(t - 1)
                turn(NT - 1)

            @block.sync
            def _(sp):
                def load_x(t):
                    if t >= NX:
                        sp.wait_ge(stored[t % NX], 16 * (t // NX))
                        sp.wait_ge(ringA.full, ringA.nth(("t", t - NX, 1)))
                    sp.dma_start(xs[t % NX][:], rows_in[t * P:(t + 1) * P, :]).then_inc(x_landed[t % NX], 16)

                wv = A["w_out"][layer].rearrange("(c p) n -> p c n", p=P)
                for i in range(6):
                    sp.dma_start(wo[:, 2 * i:2 * i + 2, :], wv[:, 2 * i:2 * i + 2, :]).then_inc(wo_landed[i], 16)
                sp.dma_start(gain[:], A["ln_g"][layer:layer + 1, :].broadcast_to([P, D])).then_inc(ln_landed, 16)
                sp.dma_start(shift[:], A["ln_b"][layer:layer + 1, :].broadcast_to([P, D])).then_inc(ln_landed, 16)
                for t in range(NX):
                    load_x(t)
                for t in range(NT):
                    sp.wait_ge(rows_set, t + 1)
                    sp.dma_start(rows_out[t * P:(t + 1) * P, :], xs[t % NX][:]).then_inc(stored[t % NX], 16)
                    if t >= 1 and t - 1 + NX < NT:
                        load_x(t - 1 + NX)
                for i in range(NX):
                    sp.wait_ge(stored[i], 16 * ((NT - 1 - i) // NX + 1))

            @block.scalar
            def _(act):
                def evacuate(t):
                    if modulate:
                        norm.evacuate(act, t)
                        return
                    for h in range(2):
                        act.wait_ge(ringA.full, ringA.nth(("t", t, h)))
                        nc.scalar.copy(E.xT[:, 4 * h:4 * h + 4, t * P:(t + 1) * P],
                                       ringA.bank(("t", t, h)).rearrange("p (c n) -> p c n", c=4)).then_inc(ringA.free, 1)

                for t in range(NT):
                    act.wait_ge(var_set, t + 1)
                    nc.scalar.activation(dev[:], mv[:, 1:2], ACT.Sqrt, bias=E.eps_ln[:]).then_inc(dev_set, 1)
                    if modulate:
                        norm.square(act, xs[t % NX][:], t)
                    if t > 0:
                        evacuate(t - 1)
                evacuate(NT - 1)

            @block.vector
            def _(dve):
                link = Chain(E.dve_chain)
                link.n = E.chain_n
                dve.wait_ge(ln_landed, 32)
                for t in range(NT):
                    xt = xs[t % NX]
                    dve.wait_ge(x_landed[t % NX], 16 * (t // NX + 1))
                    for hf in range(2):
                        cols = slice(hf * HALF, (hf + 1) * HALF)
                        dve.wait_ge(ringD.full, ringD.nth(("y", t, hf)))
                        nc.vector.scalar_tensor_tensor(xt[:, cols], xt[:, cols], ALPHA, ringD.bank(("y", t, hf))[:],
                                                       ALU.mult, ALU.add).then_inc(ringD.free, 1)
                        dve.wait_ge(ringD.free, ringD.nth(("y", t, hf)))
                        link(dve, nc.vector.bn_stats(stats[:, hf, :], xt[:, cols]))
                    nc.vector.bn_aggr(mv[:], stats[:].rearrange("p a b -> p (a b)")).then_inc(var_set, 1)
                    dve.wait_ge(dev_set, t + 1)
                    link(dve, nc.vector.reciprocal(rstd[:], dev[:]))
                    link(dve, nc.vector.tensor_scalar(xt[:], xt[:], mv[:, 0:1], rstd[:], ALU.subtract, ALU.mult))
                    link(dve, nc.vector.tensor_tensor(xt[:], xt[:], gain[:], ALU.mult))
                    nc.vector.tensor_tensor(xt[:], xt[:], shift[:], ALU.add).then_inc(rows_set, 1)
                    if modulate:
                        norm.normalise(dve, link, xt[:], t)
                E.chain_n = link.n


class Forget:

    def __init__(self, nc, E, A, ring, room, st):
        self.nc, self.E, self.A, self.ring = nc, E, A, ring
        self.z, self.e, self.low, self.one = room
        self.wf = E.sb("wf", [P, ND, FOX_HEADS], ctx=st)
        self.landed, self.stored = E.sem("wf_landed"), E.sem("cum_stored")
        self.set = {x: E.sem(f"f_{x}_set") for x in ("logit", "abs", "exp", "log", "ncum")}

    def load(self, sp):
        wf = self.A["w_kv_shared"].rearrange("(c p) n -> p c n", p=P)[:, :, 2 * D:2 * D + FOX_HEADS]
        sp.dma_start(self.wf[:], wf).then_inc(self.landed, 16)

    def store(self, sp):
        sp.wait_ge(self.set["ncum"], 1)
        sp.dma_start(self.E.ncum_rows, self.z).then_inc(self.stored, 16)

    def logits(self, pe):
        pe.wait_ge(self.landed, 16)
        for hf in range(NH):
            bank, _ = self.ring.take(("f", hf))
            for d in range(ND):
                last = self.nc.tensor.matmul(bank[0:FOX_HEADS, :], self.wf[:, d, :], self.E.xT[:, d, hf * HALF:(hf + 1) * HALF],
                                             start=(d == 0), stop=(d == ND - 1))
            last.then_inc(self.ring.full, 1)

    def softplus(self, act):
        nc, e, of = self.nc, self.e, self.set
        act.wait_ge(of["logit"], 1)
        nc.scalar.activation(e, self.z, ACT.Abs).then_inc(of["abs"], 1)
        act.wait_ge(of["abs"], 1)
        nc.scalar.activation(e, e, ACT.Exp, scale=-1.0).then_inc(of["exp"], 1)
        act.wait_ge(of["exp"], 1)
        nc.scalar.activation(e, e, ACT.Ln, bias=self.E.ones[0:FOX_HEADS, 0:1]).then_inc(of["log"], 1)

    def sums(self, dve, link):
        V, ring, of = self.nc.vector, self.ring, self.set
        link(dve, V.memset(self.one, 1.0))
        for hf in range(NH):
            dve.wait_ge(ring.full, ring.nth(("f", hf)))
            V.tensor_scalar(self.z[:, hf * HALF:(hf + 1) * HALF], ring.bank(("f", hf))[0:FOX_HEADS, :], self.E.b_forget[:], None,
                            ALU.add).then_inc(ring.free, 1)
        dve.wait_ge(ring.free, ring.nth(("f", NH - 1)))
        V.tensor_scalar(self.low, self.z, 0.0, None, ALU.min).then_inc(of["logit"], 1)
        dve.wait_ge(of["logit"], 1)
        dve.wait_ge(of["log"], 1)
        link(dve, V.tensor_tensor(self.e, self.e, self.low, ALU.subtract))
        V.tensor_tensor_scan(self.z, self.one, self.e, 0.0, ALU.mult, ALU.add).then_inc(of["ncum"], 1)


def stage_fox(nc, E, A):
    NP = FOX_HEADS // 2
    STEPS = FOX_HEADS * NT
    with ExitStack() as st:
        vT = E.sb("fox_vT", [P, S], ctx=st)
        qT = [E.sb(f"fox_qT{b}", [P, S], ctx=st) for b in range(2)]
        kT = [E.sb(f"fox_kT{b}", [P, S], ctx=st) for b in range(2)]
        v = [E.sb(f"fox_v{b}", [P, NT, P], ctx=st) for b in range(2)]
        ncum = [E.sb(f"ncum{b}", [P, S], ctx=st) for b in range(2)]
        ncum_landed = [E.sem(f"ncum_landed{b}") for b in range(2)]
        probs = [E.sb(f"fox_p{b}", [P, S], ctx=st) for b in range(3)]
        probsT = [E.sb(f"fox_pT{b}", [P, S], ctx=st) for b in range(2)]
        y = [E.sb(f"fox_y{b}", [P, NT, P], ctx=st) for b in range(2)]
        NB = 4
        top = E.sb("fox_top", [P, NB], ctx=st)
        bias = E.sb("fox_bias", [P, NB], ctx=st)
        total = E.sb("fox_total", [P, NB], ctx=st)
        inv = E.sb("fox_inv", [P, NB], ctx=st)
        ident, causal = (E.sb(f"fox_{x}", [P, P], BF16, ctx=st) for x in ("ident", "causal"))
        mask_set = E.sem("fox_mask_set")
        score = Ring([E.psum[:, 0:S], E.psum[:, S:2 * S]], E.sem("score_full"), E.sem("score_free"))
        ringA = Ring(E.banks[4:6], E.sem("foxA_full"), E.sem("foxA_free"))
        ringY = Ring(E.banks[6:8], E.sem("foxY_full"), E.sem("foxY_free"))
        bias_set, exp_done = E.sem("fox_bias_set"), E.sem("fox_exp_done")
        win = A["w_in"][1].rearrange("(c p) n -> p c n", p=P)
        wkv = A["w_kv_shared"].rearrange("(c p) n -> p c n", p=P)
        KINDS = ("q", "k", "v", "g")

        split = SplitProducts(nc, E, "w1", st, lambda eng, n: eng.wait_ge(ringA.full, ringA.nth((KINDS[n % 4], n // 4, 1))))

        def columns(c, kind):
            if kind == "q":
                return win[:, :, c * P:(c + 1) * P]
            if kind == "g":
                return win[:, :, (GATE0 + c) * P:(GATE0 + c + 1) * P]
            return wkv[:, :, c * P + (D if kind == "v" else 0):(c + 1) * P + (D if kind == "v" else 0)]

        def tile_of(n):
            return n % NT

        def groups(i):
            return [(s, min(s + 4, i + 1)) for s in range(0, i + 1, 4)]

        with nc.Block() as block:

            @block.tensor
            def _(pe):
                def project(c, piece):
                    kind, hf = KINDS[piece // 2], piece % 2
                    n = 4 * c + piece // 2
                    if kind == "g":
                        bank, free = ringA.take(("tv", c, hf))
                        wait(pe, ringA.free, free)
                        pe.wait_ge(ringA.free, ringA.nth(("v", c, hf)))
                        for j in range(4):
                            last = nc.tensor.transpose(bank[:, j * P:(j + 1) * P], vT[:, (4 * hf + j) * P:(4 * hf + j + 1) * P], E.ident[:])
                        last.then_inc(ringA.full, 1)
                    bank, free = ringA.take((kind, c, hf))
                    wait(pe, ringA.free, free)
                    split.project(pe, bank, n, hf).then_inc(ringA.full, 1)

                def scores(n):
                    hd, i = n // NT, tile_of(n)
                    c, r = hd // 2, slice((hd % 2) * 64, (hd % 2) * 64 + 64)
                    bank, free = score.take(n)
                    wait(pe, score.free, free)
                    if n % (2 * NT) == 0:
                        pe.wait_ge(ringA.free, ringA.nth(("k", c, 1)))
                    keys = (i + 1) * P
                    for k0 in range(0, keys, HALF):
                        k1 = min(k0 + HALF, keys)
                        nc.tensor.matmul(bank[:, k0:k1], qT[c % 2][r, i * P:(i + 1) * P], kT[c % 2][r, k0:k1],
                                         start=True, stop=True)
                    nc.tensor.matmul(bank[:, keys - P:keys], ident[:], causal[:], start=False, stop=True,
                                     skip_group_check=True).then_inc(score.full, 1)

                def turn(n):
                    i = tile_of(n)
                    pe.wait_ge(exp_done, n + 1)
                    for s0, s1 in groups(i):
                        bank, free = ringA.take(("t", n, s0))
                        wait(pe, ringA.free, free)
                        for s in range(s0, s1):
                            last = nc.tensor.transpose(bank[:, (s - s0) * P:(s - s0 + 1) * P], probs[n % 3][:, s * P:(s + 1) * P], E.ident[:])
                        last.then_inc(ringA.full, 1)

                def values(n):
                    hd, i = n // NT, tile_of(n)
                    c, j = hd // 2, hd % 2
                    bank, free = ringY.take(n)
                    wait(pe, ringY.free, free)
                    pe.wait_ge(ringA.free, ringA.nth(("t", n, groups(i)[-1][0])))
                    pe.wait_ge(ringA.free, ringA.nth(("tv", c, 1)))
                    for s in range(i + 1):
                        last = nc.tensor.matmul(bank[:, 0:64], probsT[n % 2][:, s * P:(s + 1) * P], v[c % 2][:, s, j * 64:(j + 1) * 64],
                                                start=(s == 0), stop=(s == i))
                    last.then_inc(ringY.full, 1)

                def turn_y(c):
                    pe.wait_ge(ringY.free, ringY.nth(2 * NT * (c + 1) - 1))
                    for hf in range(NH):
                        bank, free = ringY.take(("y", c, hf))
                        wait(pe, ringY.free, free)
                        for k in range(4):
                            last = nc.tensor.transpose(bank[:, k * P:(k + 1) * P], y[c % 2][:, 4 * hf + k, :], E.ident[:])
                        last.then_inc(ringY.full, 1)

                for piece in range(8):
                    project(0, piece)
                pe.wait_ge(mask_set, 2)
                for n in range(STEPS + 5):
                    if n < STEPS:
                        scores(n)
                    if n % 2 == 1 and n // (2 * NT) + 1 < NP:
                        project(n // (2 * NT) + 1, (n % (2 * NT)) // 2)
                    if 2 <= n < STEPS + 2:
                        turn(n - 2)
                    if 3 <= n < STEPS + 3:
                        values(n - 3)
                    if n >= 2 * NT + 4 and (n - 4) % (2 * NT) == 0:
                        turn_y((n - 4) // (2 * NT) - 1)

            @block.sync
            def _(sp):
                def load_w(n):
                    split.load(sp, n, columns(n // 4, KINDS[n % 4]))

                def load_ncum(hd):
                    if hd >= 2:
                        sp.wait_ge(score.free, score.nth((hd - 1) * NT - 1))
                    sp.dma_start(ncum[hd % 2][:], E.ncum_rows[hd:hd + 1, :].broadcast_to([P, S])).then_inc(ncum_landed[hd % 2], 16)

                for n in range(4):
                    load_w(n)
                load_ncum(0)
                load_ncum(1)
                hd = 2
                for n in range(4, 4 * NP):
                    load_w(n)
                    while hd < FOX_HEADS and 2 * n >= 4 * hd + 4:
                        load_ncum(hd)
                        hd += 1
                while hd < FOX_HEADS:
                    load_ncum(hd)
                    hd += 1

            @block.gpsimd
            def _(pool):
                split.split_weights(pool, 1)
                nc.gpsimd.tensor_copy(ident[:], E.ident[:]).then_inc(mask_set, 1)
                nc.gpsimd.tensor_copy(causal[:], E.causal[:]).then_inc(mask_set, 1)
                split.split_weights(pool, 4 * NP, 1)

            @block.scalar
            def _(act):
                def evacuate_piece(c, piece):
                    kind, hf = KINDS[piece // 2], piece % 2
                    key = (kind, c, hf)
                    if kind == "g":
                        act.wait_ge(ringA.full, ringA.nth(("tv", c, hf)))
                        if c >= 2 and hf == 0:
                            act.wait_ge(ringY.full, ringY.nth(2 * NT * (c - 1) - 1))
                        nc.scalar.copy(v[c % 2][:, 4 * hf:4 * hf + 4, :], ringA.bank(("tv", c, hf)).rearrange("p (t n) -> p t n", t=4)).then_inc(ringA.free, 1)
                    act.wait_ge(ringA.full, ringA.nth(key))
                    cols = slice(hf * HALF, (hf + 1) * HALF)
                    if c >= 2 and hf == 0 and kind in "qk":
                        act.wait_ge(score.full, score.nth(2 * NT * (c - 1) - 1))
                    bank = ringA.bank(key)
                    if kind == "q":
                        ins = nc.scalar.activation(qT[c % 2][:, cols], bank[:], ACT.Copy, scale=FOX_SCALE)
                    elif kind == "k":
                        ins = nc.scalar.copy(kT[c % 2][:, cols], bank[:])
                    elif kind == "v":
                        ins = nc.scalar.copy(vT[:, cols], bank[:])
                    else:
                        ins = nc.scalar.activation(E.yT[:, c, cols], bank[:], ACT.Silu)
                    ins.then_inc(ringA.free, 1)

                for piece in range(8):
                    evacuate_piece(0, piece)
                for n in range(STEPS + 5):
                    if n < STEPS:
                        keys = (tile_of(n) + 1) * P
                        act.wait_ge(bias_set, n + 1)
                        if n >= NB:
                            act.wait_ge(ringY.free, ringY.nth(n - NB))
                        nc.scalar.activation(probs[n % 3][:, 0:keys], probs[n % 3][:, 0:keys], ACT.Exp, bias=bias[:, n % NB:n % NB + 1],
                                             accum_out=total[:, n % NB:n % NB + 1]).then_inc(exp_done, 1)
                    if n % 2 == 1 and n // (2 * NT) + 1 < NP:
                        evacuate_piece(n // (2 * NT) + 1, (n % (2 * NT)) // 2)
                    if 2 <= n < STEPS + 2:
                        m = n - 2
                        for s0, s1 in groups(tile_of(m)):
                            key = ("t", m, s0)
                            act.wait_ge(ringA.full, ringA.nth(key))
                            if m >= 2 and s0 == 0:
                                act.wait_ge(ringY.full, ringY.nth(m - 2))
                            nc.scalar.copy(probsT[m % 2][:, s0 * P:s1 * P], ringA.bank(key)[:, 0:(s1 - s0) * P]).then_inc(ringA.free, 1)

            @block.vector
            def _(dve):
                link = Chain(E.dve_chain)
                link.n = E.chain_n
                for n in range(STEPS + 5):
                    if n < STEPS:
                        hd, i = n // NT, tile_of(n)
                        keys = (i + 1) * P
                        if n % NT == 0:
                            dve.wait_ge(ncum_landed[hd % 2], 16 * (hd // 2 + 1))
                        if n >= 3:
                            dve.wait_ge(ringA.full, ringA.nth(("t", n - 3, groups(tile_of(n - 3))[-1][0])))
                        if n >= NB:
                            dve.wait_ge(exp_done, n - NB + 1)
                        dve.wait_ge(score.full, score.nth(n))
                        b = slice(n % NB, n % NB + 1)
                        nc.vector.tensor_tensor_reduce(probs[n % 3][:, 0:keys], score.bank(n)[:, 0:keys], ncum[hd % 2][:, 0:keys], 1.0, -3.0e38,
                                                       ALU.add, ALU.max, top[:, b]).then_inc(score.free, 1)
                        dve.wait_ge(score.free, score.nth(n))
                        nc.vector.tensor_scalar(bias[:, b], top[:, b], -1.0, None, ALU.mult).then_inc(bias_set, 1)
                    if 3 <= n < STEPS + 3:
                        m = n - 3
                        hd, i = m // NT, tile_of(m)
                        b = slice(m % NB, m % NB + 1)
                        dve.wait_ge(exp_done, m + 1)
                        link(dve, nc.vector.reciprocal(inv[:, b], total[:, b]))
                        dve.wait_ge(ringY.full, ringY.nth(m))
                        nc.vector.tensor_scalar(y[(hd // 2) % 2][:, i, (hd % 2) * 64:(hd % 2) * 64 + 64], ringY.bank(m)[:, 0:64], inv[:, b], None,
                                                ALU.mult).then_inc(ringY.free, 1)
                    if n >= 2 * NT + 4 and (n - 4) % (2 * NT) == 0:
                        c = (n - 4) // (2 * NT) - 1
                        for hf in range(NH):
                            cols = slice(hf * HALF, (hf + 1) * HALF)
                            dve.wait_ge(ringY.full, ringY.nth(("y", c, hf)))
                            dve.wait_ge(ringA.free, ringA.nth(("g", c, hf)))
                            nc.vector.tensor_tensor(E.yT[:, c, cols], ringY.bank(("y", c, hf))[:], E.yT[:, c, cols], ALU.mult).then_inc(ringY.free, 1)
                E.chain_n = link.n


def stage_memory_and_gates(nc, E, A, layer):
    n = f"{layer}"
    with ExitStack() as st:
        NW = 6
        w = [E.sb(f"wm_{i}", [P, ND, P], ctx=st) for i in range(NW)]
        landed = [E.sem(f"wm_landed{i}") for i in range(NW)]
        qT = [E.sb(f"mem_qT{i}", [P, S], ctx=st) for i in range(2)]
        ringA = Ring(E.banks[0:4], E.sem("mA_full"), E.sem("mA_free"))
        ringD = Ring(E.banks[4:8], E.sem("mD_full"), E.sem("mD_free"))
        attn = MemoryAttention(nc, E, layer, ringA, ringD, st)
        mod = Modulation(nc, E, A, st)
        first = mod.LOADS // 2
        per_head = (mod.LOADS - first) // MEM_HEADS
        mod_banks = (E.banks[0], E.banks[4:8])
        flat = lambda x, dims: x[0:FOX_HEADS].rearrange(dims)
        room = [flat(x, dims)[:, i * S:(i + 1) * S] for x, dims in ((attn.probs, "p t n -> p (t n)"), (attn.probsT, "p m n -> p (m n)")) for i in range(2)]
        forget = Forget(nc, E, A, ringD, room, st)
        order = [("k", h) for h in range(MEM_HEADS)] + [("v", h) for h in range(MEM_HEADS)]
        order += [(kind, h) for h in range(MEM_HEADS) for kind in "qm"]
        wkv = A["w_mem_kv"][layer].rearrange("(c p) n -> p c n", p=P)
        win = A["w_in"][layer].rearrange("(c p) n -> p c n", p=P)
        with nc.Block() as block:

            @block.tensor
            def _(pe):
                def memory(m):
                    kind, h = order[m]
                    pe.wait_ge(landed[m % NW], 16 * (m // NW + 1))
                    bank, free = ringA.take((kind, h))
                    wait(pe, ringA.free, free)
                    for to in range(1 if kind == "k" else NM):
                        for d in range(ND):
                            if kind == "k":
                                last = nc.tensor.matmul(bank[:, 0:N_MEM], w[m % NW][:, d, :], E.memT[:, d, :], start=(d == 0), stop=(d == ND - 1))
                            else:
                                last = nc.tensor.matmul(bank[:, to * P:(to + 1) * P], E.memT[:, d, to * P:(to + 1) * P], w[m % NW][:, d, :],
                                                        start=(d == 0), stop=(d == ND - 1))
                    last.then_inc(ringA.full, 1)

                def project(h):
                    for k, kind in enumerate("qm"):
                        m = 2 * MEM_HEADS + 2 * h + k
                        pe.wait_ge(landed[m % NW], 16 * (m // NW + 1))
                        ring = ringD if kind == "q" else ringA
                        for hf in range(NH):
                            bank, free = ring.take((kind, h, hf))
                            wait(pe, ring.free, free)
                            for d in range(ND):
                                last = nc.tensor.matmul(bank[:], w[m % NW][:, d, :], E.xT[:, d, hf * HALF:(hf + 1) * HALF],
                                                        start=(d == 0), stop=(d == ND - 1))
                            last.then_inc(ring.full, 1)

                forget.logits(pe)
                for m in range(2 * MEM_HEADS):
                    memory(m)
                project(0)
                pe.wait_ge(ringA.free, ringA.nth(("v", MEM_HEADS - 1)))
                for h in range(MEM_HEADS):
                    pe.wait_ge(ringD.free, ringD.nth(("q", h, NH - 1)))
                    attn.scores(pe, h, qT[h % 2])
                    if h + 1 < MEM_HEADS:
                        project(h + 1)
                    attn.turn(pe, h)
                    attn.values(pe, h)
                pe.wait_ge(ringA.free, ringA.nth(("t", MEM_HEADS - 1, NT // 2 - 1)))
                pe.wait_ge(ringD.free, ringD.nth(("o", MEM_HEADS - 1, NH - 1)))
                mod.total(pe, mod_banks)

            @block.sync
            def _(sp):
                forget.load(sp)
                done = 0
                for m, (kind, h) in enumerate(order):
                    if m >= NW:
                        k0, h0 = order[m - NW]
                        ring = ringD if k0 == "q" else ringA
                        sp.wait_ge(ring.full, ring.nth((k0, h0) if k0 in "kv" else (k0, h0, NH - 1)))
                    if kind in "kv":
                        src = wkv[:, :, (h + (MEM_HEADS if kind == "v" else 0)) * P:(h + 1 + (MEM_HEADS if kind == "v" else 0)) * P]
                    else:
                        col = (ND if kind == "q" else GATE0 + ND) + h
                        src = win[:, :, col * P:(col + 1) * P]
                    sp.dma_start(w[m % NW][:], src).then_inc(landed[m % NW], 16)
                    if m == NW - 1:
                        mod.load_small(sp)
                    if m == 2 * MEM_HEADS - 1:
                        forget.store(sp)
                    while m >= NW - 1 and done < (m - NW + 2) * 2:
                        mod.load(sp, done)
                        done += 1
                for m in range(done, mod.LOADS):
                    mod.load(sp, m)
                mod.store(sp)
                sp.wait_ge(forget.stored, 16)

            @block.scalar
            def _(act):
                def gate(h):
                    for hf in range(NH):
                        act.wait_ge(ringA.full, ringA.nth(("m", h, hf)))
                        nc.scalar.activation(E.yT[:, ND + h, hf * HALF:(hf + 1) * HALF], ringA.bank(("m", h, hf))[:], ACT.Silu).then_inc(ringA.free, 1)

                forget.softplus(act)
                for kind, h in order[0:2 * MEM_HEADS]:
                    act.wait_ge(ringA.full, ringA.nth((kind, h)))
                    bank = ringA.bank((kind, h))
                    if kind == "k":
                        nc.scalar.copy(E.mkT[:, h, :], bank[:, 0:N_MEM]).then_inc(ringA.free, 1)
                    else:
                        nc.scalar.copy(E.mv[:, :, h * P:(h + 1) * P], bank[:, 0:NM * P].rearrange("p (m n) -> p m n", m=NM)).then_inc(ringA.free, 1)
                gate(0)
                act.wait_ge(forget.stored, 16)
                for h in range(MEM_HEADS):
                    attn.exps(act, h)
                    if h + 1 < MEM_HEADS:
                        gate(h + 1)
                    attn.evacuate(act, h)

            @block.vector
            def _(dve):
                link = Chain(E.dve_chain)
                link.n = E.chain_n

                def queries(h):
                    for hf in range(NH):
                        dve.wait_ge(ringD.full, ringD.nth(("q", h, hf)))
                        if h >= 2 and hf == 0:
                            dve.wait_ge(ringA.full, ringA.nth(("s", h - 2, NT // 2 - 1)))
                        nc.vector.tensor_copy(qT[h % 2][:, hf * HALF:(hf + 1) * HALF], ringD.bank(("q", h, hf))[:]).then_inc(ringD.free, 1)

                forget.sums(dve, link)
                for m in range(first):
                    mod.accumulate(dve, link, m)
                queries(0)
                for h in range(MEM_HEADS):
                    attn.maxima(dve, link, h)
                    attn.normalise(dve, link, h)
                    for m in range(first + h * per_head, first + (h + 1) * per_head):
                        mod.accumulate(dve, link, m)
                    if h + 1 < MEM_HEADS:
                        queries(h + 1)
                    dve.wait_ge(ringA.free, ringA.nth(("m", h, NH - 1)))
                    attn.gate(dve, h)
                mod.finish(dve, link, mod_banks)
                E.chain_n = link.n


GW = 512
RW = 512
HD = 64
NPAIR = RW // P
C = 64
NC = S // C
LORA, GATE_LORA = 32, 96
DECAY = math.exp(-0.5)
LEVELS = 5
UNITS = 4


class Modulation:
    NG = 6 * D // HALF
    GATES = (4, 5, 10, 11)
    HD_ = ND // 2
    LOADS = 2 * (6 * D // HALF)

    def __init__(self, nc, E, A, st):
        self.nc, self.E, self.A = nc, E, A
        self.w = [E.sb(f"ada_{i}", [P, self.HD_, HALF], ctx=st) for i in range(2)]
        self.landed = [E.sem(f"ada_landed{i}") for i in range(2)]
        self.sum = E.sb("ada_sum", [P, 6 * D], ctx=st)
        self.c_cols = E.sb("c_cols", [P, ND], ctx=st)
        self.b = E.sb("ada_b", [P, 6 * ND], ctx=st)
        self.gain = E.sb("norm_gains", [P, 2 * ND], ctx=st)
        self.gate_b = E.sb("gate_b", [P, 2, D], ctx=st)
        self.small, self.stored = E.sem("ada_small"), E.sem("gates_stored")
        self.summed, self.full, self.rows_set = E.sem("ada_summed"), E.sem("ada_full"), E.sem("gate_rows_set")

    def load_small(self, sp):
        A, gain = self.A, self.gain
        for to, src in ((self.c_cols[:], A["c_2_cols"]), (self.b[:], A["ada_b_2_cols"]),
                        (gain[:, 0:ND], A["norm1_g_2_cols"]), (gain[:, ND:2 * ND], A["norm2_g_2_cols"])):
            sp.dma_start(to, src).then_inc(self.small, 16)
        for i in range(2):
            g0 = (2 + 3 * i) * D
            sp.dma_start(self.gate_b[:, i, :], A["ada_b_2"][0:1, g0:g0 + D].broadcast_to([P, D])).then_inc(self.small, 16)

    def load(self, sp, m):
        g, half = m // 2, m % 2
        if m >= 2:
            sp.wait_ge(self.summed, m - 1)
        wv = self.A["ada_w_2"][0].rearrange("(c p) n -> p c n", p=P)
        sp.dma_start(self.w[half][:], wv[:, half * self.HD_:(half + 1) * self.HD_, g * HALF:(g + 1) * HALF]).then_inc(self.landed[half], 16)

    def store(self, sp):
        sp.wait_ge(self.rows_set, 1)
        for i in range(2):
            g0 = (2 + 3 * i) * D
            sp.dma_start(self.E.gates[:, i * D:(i + 1) * D], self.sum[:, g0:g0 + D]).then_inc(self.stored, 16)
        sp.wait_ge(self.stored, 32)

    def accumulate(self, dve, link, m):
        V, g, half = self.nc.vector, m // 2, m % 2
        to = self.sum[:, g * HALF:(g + 1) * HALF]
        if m == 0:
            dve.wait_ge(self.small, 16 * 6)
        dve.wait_ge(self.landed[half], 16 * (g + 1))
        for k in range(self.HD_):
            d = half * self.HD_ + k
            c = self.c_cols[:, d:d + 1]
            if d == 0:
                ins = V.tensor_scalar(to, self.w[half][:, k, :], c, None, ALU.mult)
            else:
                ins = V.scalar_tensor_tensor(to, self.w[half][:, k, :], c, to, ALU.mult, ALU.add)
            if k < self.HD_ - 1:
                link(dve, ins)
        ins.then_inc(self.summed, 1)
        dve.wait_ge(self.summed, m + 1)

    def finish(self, dve, link, banks):
        V, E = self.nc.vector, self.E
        cols_bank, gate_banks = banks
        dve.wait_ge(self.full, 1)
        for g in range(self.NG):
            if g not in self.GATES:
                link(dve, V.tensor_tensor(E.mod[:, 4 * g:4 * g + 4], cols_bank[:, 4 * g:4 * g + 4], self.b[:, 4 * g:4 * g + 4], ALU.add))
        for k, g in enumerate(self.GATES):
            i, hf = k // 2, g % 2
            ins = V.tensor_tensor(self.sum[:, g * HALF:(g + 1) * HALF], gate_banks[k][:], self.gate_b[:, i, hf * HALF:(hf + 1) * HALF], ALU.add)
        ins.then_inc(self.rows_set, 1)
        for i in range(2):
            m = E.mod[:, (1 + 3 * i) * ND:(2 + 3 * i) * ND]
            link(dve, V.scalar_tensor_tensor(m, m, 1.0, self.gain[:, i * ND:(i + 1) * ND], ALU.add, ALU.mult))

    def total(self, pe, banks):
        nc, E = self.nc, self.E
        cols_bank, gate_banks = banks
        pe.wait_ge(self.summed, self.LOADS)
        for g in range(self.NG):
            if g in self.GATES:
                bank = gate_banks[self.GATES.index(g)]
                last = nc.tensor.matmul(bank[:], E.ones[:], self.sum[:, g * HALF:(g + 1) * HALF], start=True, stop=True)
            else:
                for k in range(4 * g, 4 * g + 4):
                    last = nc.tensor.matmul(cols_bank[:, k:k + 1], self.sum[:, k * P:(k + 1) * P], E.ones[:, 0:1], start=True, stop=True)
        last.then_inc(self.full, 1)


def stage_rwkv_pairs(nc, E, A):
    n0 = 3 * RW
    with ExitStack() as st:
        NW = 3
        w = [E.sb(f"wr_{i}", [P, ND, P], ctx=st) for i in range(NW)]
        w_landed = [E.sem(f"wr_landed{i}") for i in range(NW)]
        wl = E.sb("w_lora", [P, ND, 2 * LORA + GATE_LORA], ctx=st)
        w2 = E.sb("w2", [LORA, RW], ctx=st)
        a2 = E.sb("a2", [LORA, RW], ctx=st)
        small, wl_landed = E.sem("rwkv_small"), E.sem("w_lora_landed")
        cols = E.sb("rwkv_cols", [P, 12 + 4 * 6], ctx=st)
        mu, w0c, a0c, kkc, kac, rkc = (cols[:, 0:12], *(cols[:, 12 + 4 * i:16 + 4 * i] for i in range(5)))
        ka1 = cols[:, 32:36]
        mu_x = [E.sb(f"mu_x{i}", [n, 1], ctx=st) for i, n in enumerate((LORA, LORA, GATE_LORA))]
        xw = E.sb("xw", [LORA, S], ctx=st)
        xa = E.sb("xa", [LORA, S], ctx=st)
        blocksum = E.sb("blocksum", [P, P], ctx=st)
        headsel = E.sb("headsel", [P, 2], ctx=st)
        restart = E.sb("restart", [P, S], ctx=st)
        m_up = E.sb("m_up", [P, P], ctx=st)
        m_upeq = E.sb("m_upeq", [P, P], ctx=st)
        m_low0 = E.sb("m_low0", [P, P], ctx=st)
        m_level = E.sb("m_level", [P, LEVELS + 1, P], ctx=st)
        masks_set = E.sem("masks_set")
        z = E.sb("z", [P, 1 + S], ctx=st)
        r = [E.sb(f"r{i}", [P, S], ctx=st) for i in range(2)]
        k, v, at, bt = (E.sb(x, [P, S], ctx=st) for x in ("k", "v", "at", "bt"))
        lw = E.sb("lw", [P, S], ctx=st)
        cl = E.sb("cl", [P, S], ctx=st)
        e2 = E.sb("e2", [P, S], ctx=st)
        tmp = E.sb("tmp", [P, S], ctx=st)
        rate = E.sb("rate", [P, S], ctx=st)
        ctr = E.sb("ctr", [P, NC], ctx=st)
        tok = {x: E.sb("tok_" + x, [P, NT, P], ctx=st) for x in "abkv"}
        abT, akT, rbT, rkT, Xm, XT, L = (E.sb(x, [P, 4, UNITS * P], ctx=st) for x in ("abT", "akT", "rbT", "rkT", "Xm", "XT", "L"))
        AV = E.sb("AV", [P, 4, UNITS * HD], ctx=st)
        T1, GH = akT, Xm
        spare, spare2 = abT[:].rearrange("p g n -> p (g n)"), L[:].rearrange("p g n -> p (g n)")
        MTs, Ns, QTs = spare[:, 0:S], spare[:, S:2 * S], spare2[:, 0:S]
        Yi = spare2[:, S:2 * S].rearrange("p (t n) -> p t n", t=NT)
        ringA = Ring(E.banks[0:4], E.sem("rwA_full"), E.sem("rwA_free"))
        ringD = Ring(E.banks[4:8], E.sem("rwD_full"), E.sem("rwD_free"))
        S_ = {x: E.sem("rw_" + x) for x in ("shift", "sq", "cc", "front", "level", "exp1", "exp2", "exp3", "lora", "stored", "tanh", "rstore")}
        win = A["w_in_2"][0].rearrange("(c p) n -> p c n", p=P)[:, :, 2 * GW:]
        KIND = "rkv"

        script = [("lora",)]
        front = [("proj", "r"), ("proj", "k"), ("proj", "v"), ("small",), ("sums",)]
        first_front = front[0:2] + front[3:5] + front[2:3]
        script += [(f[0], 0, *f[1:]) for f in first_front]
        for c in range(NPAIR):
            script.append(("turn", c))
            script.append(("A", c))
            script.append(("AV", c))
            for m in range(1, LEVELS + 1):
                script.append(("level", c, m))
                if c + 1 < NPAIR:
                    f = front[m - 1]
                    script.append((f[0], c + 1, *f[1:]))
            script.append(("tail", c))

        def units(g):
            return g // 2, g % 2

        with nc.Block() as block:

            @block.tensor
            def _(pe):
                def take(ring, key):
                    bank, free = ring.take(key)
                    wait(pe, ring.free, free)
                    return bank

                def lora():
                    pe.wait_ge(wl_landed, 16)
                    for i, (lo, n) in enumerate(((0, LORA), (LORA, LORA), (2 * LORA, GATE_LORA))):
                        for hf in range(NH):
                            bank = take(ringA, ("lora", i, hf))
                            for d in range(ND):
                                last = nc.tensor.matmul(bank[0:n, :], wl[:, d, lo:lo + n], E.hT[:, d, hf * HALF:(hf + 1) * HALF],
                                                        start=(d == 0), stop=(d == ND - 1))
                            last.then_inc(ringA.full, 1)

                def proj(c, kind):
                    m = 3 * c + KIND.index(kind)
                    pe.wait_ge(w_landed[m % NW], 16 * (m // NW + 1))
                    for hf in range(NH):
                        bank = take(ringA, (kind, c, hf))
                        for d in range(ND):
                            last = nc.tensor.matmul(bank[:], w[m % NW][:, d, :], E.hT[:, d, hf * HALF:(hf + 1) * HALF],
                                                    start=(d == 0), stop=(d == ND - 1))
                        last.then_inc(ringA.full, 1)

                def small_(c):
                    pe.wait_ge(S_["lora"], 2)
                    pe.wait_ge(S_["tanh"], 1)
                    pe.wait_ge(small, 16 * E.n_small)
                    for name, m, x in (("w", w2, xw), ("a", a2, xa)):
                        for hf in range(NH):
                            bank = take(ringA, (name, c, hf))
                            nc.tensor.matmul(bank[:], m[:, c * P:(c + 1) * P], x[:, hf * HALF:(hf + 1) * HALF],
                                             start=True, stop=True).then_inc(ringA.full, 1)

                def sums(c):
                    if c == 0:
                        pe.wait_ge(masks_set, E.n_masks)
                    pe.wait_ge(S_["sq"], c + 1)
                    for hf in range(NH):
                        bank = take(ringA, ("n", c, hf))
                        nc.tensor.matmul(bank[:], blocksum[:], tmp[:, hf * HALF:(hf + 1) * HALF], start=True, stop=True).then_inc(ringA.full, 1)

                def turn(c):
                    for x, src in (("v", v), ("k", k), ("b", bt), ("a", at)):
                        if x == "v":
                            pe.wait_ge(S_["shift"], 3 * c + 3)
                        if x == "k":
                            pe.wait_ge(S_["front"], c + 1)
                        for hf in range(NH):
                            bank = take(ringA, ("t" + x, c, hf))
                            for j in range(4):
                                t = 4 * hf + j
                                last = nc.tensor.transpose(bank[:, j * P:(j + 1) * P], src[:, t * P:(t + 1) * P], E.ident[:])
                            last.then_inc(ringA.full, 1)
                    bank = take(ringA, ("bonus", c))
                    for t in range(NT):
                        last = nc.tensor.matmul(bank[:, 2 * t:2 * t + 2], rate[:, t * P:(t + 1) * P], headsel[:], start=True, stop=True)
                    last.then_inc(ringA.full, 1)

                def a_part(c):
                    aT, bT, kT, rT = at, bt, k, r[c % 2]
                    for g in range(4):
                        j, th = units(g)
                        rows = slice(j * HD, (j + 1) * HD)
                        for name, left, right in (("ab", bT, aT), ("X", aT, bT), ("ak", kT, aT), ("rb", bT, rT), ("rk", kT, rT)):
                            bank = take(ringD, (name, c, g))
                            for u in range(UNITS):
                                t = slice((4 * th + u) * P, (4 * th + u + 1) * P)
                                last = nc.tensor.matmul(bank[:, u * P:(u + 1) * P], left[rows, t], right[rows, t], start=True, stop=True)
                            last.then_inc(ringD.full, 1)

                def level(c, m):
                    for g in range(4):
                        pe.wait_ge(S_["level"], 4 * (LEVELS * c + m - 1) + g + 1)
                        pe.wait_ge(ringD.free, ringD.nth(("X", c, g) if m == 1 else ("dXT", c, m - 1, g)))
                        bank = take(ringA, ("T1", c, m, g))
                        for u in range(UNITS):
                            cu = slice(u * P, (u + 1) * P)
                            last = nc.tensor.matmul(bank[:, cu], L[:, g, cu], Xm[:, g, cu], start=True, stop=True)
                        last.then_inc(ringA.full, 1)
                    for g in range(4):
                        pe.wait_ge(ringA.free, ringA.nth(("T1", c, m, g)))
                        if m < LEVELS:
                            bank = take(ringD, ("dX", c, m, g))
                            for u in range(UNITS):
                                cu = slice(u * P, (u + 1) * P)
                                last = nc.tensor.matmul(bank[:, cu], XT[:, g, cu], T1[:, g, cu], start=True, stop=True)
                            last.then_inc(ringD.full, 1)
                        bank = take(ringD, ("dXT", c, m, g))
                        for u in range(UNITS):
                            cu = slice(u * P, (u + 1) * P)
                            last = nc.tensor.matmul(bank[:, cu], T1[:, g, cu], XT[:, g, cu], start=True, stop=True)
                        last.then_inc(ringD.full, 1)

                def av(c):
                    pe.wait_ge(ringA.free, ringA.nth(("ta", c, NH - 1)))
                    for g in range(4):
                        j, th = units(g)
                        hcols = slice(j * HD, (j + 1) * HD)
                        bank = take(ringA, ("AV", c, g))
                        pe.wait_ge(ringD.free, ringD.nth(("ak", c, g)))
                        for u in range(UNITS):
                            last = nc.tensor.matmul(bank[:, u * HD:(u + 1) * HD], akT[:, g, u * P:(u + 1) * P], tok["v"][:, 4 * th + u, hcols],
                                                    start=True, stop=True)
                        last.then_inc(ringA.full, 1)

                def tail(c):
                    for g in range(4):
                        j, th = units(g)
                        hcols = slice(j * HD, (j + 1) * HD)
                        bank = take(ringA, ("GH", c, g))
                        pe.wait_ge(ringA.free, ringA.nth(("AV", c, g)))
                        pe.wait_ge(ringD.free, ringD.nth(("dXT", c, LEVELS, g)))
                        for u in range(UNITS):
                            wT = XT[:, g, u * P:(u + 1) * P]
                            nc.tensor.matmul(bank[:, u * P:u * P + HD], wT, tok["a"][:, 4 * th + u, hcols], start=True, stop=True)
                            last = nc.tensor.matmul(bank[:, u * P + HD:(u + 1) * P], wT, AV[:, g, u * HD:(u + 1) * HD], start=True, stop=True)
                        last.then_inc(ringA.full, 1)
                    pe.wait_ge(ringA.free, ringA.nth(("GH", c, 3)))
                    for q in range(2):
                        rows = slice(q * C, (q + 1) * C)
                        bank = take(ringD, ("MT", c, q))
                        for t in range(NT):
                            for j in range(2):
                                g, u, o = 2 * j + t // 4, t % 4, slice(j * HD, (j + 1) * HD)
                                last = nc.tensor.matmul(bank[o, t * HD:(t + 1) * HD], GH[rows, g, u * P:u * P + HD], tok["b"][rows, t, o],
                                                        start=True, stop=True)
                        last.then_inc(ringD.full, 1)
                    for q in range(2):
                        rows = slice(q * C, (q + 1) * C)
                        bank = take(ringD, ("N", c, q))
                        for t in range(NT):
                            for j in range(2):
                                g, u, o = 2 * j + t // 4, t % 4, slice(j * HD, (j + 1) * HD)
                                to = bank[o, t * HD:(t + 1) * HD]
                                nc.tensor.matmul(to, tok["b"][rows, t, o], GH[rows, g, u * P + HD:(u + 1) * P], start=True, stop=False)
                                last = nc.tensor.matmul(to, tok["k"][rows, t, o], tok["v"][rows, t, o], start=False, stop=True)
                        last.then_inc(ringD.full, 1)
                    for th in range(2):
                        bank = take(ringD, ("Q", c, th))
                        for u in range(UNITS):
                            for j in range(2):
                                g = 2 * j + th
                                last = nc.tensor.matmul(bank[j * HD:(j + 1) * HD, u * P:(u + 1) * P], GH[:, g, u * P:u * P + HD],
                                                        rbT[:, g, u * P:(u + 1) * P], start=True, stop=True)
                        last.then_inc(ringD.full, 1)
                    for th in range(2):
                        bank = take(ringA, ("Yi", c, th))
                        for u in range(UNITS):
                            t = 4 * th + u
                            for j in range(2):
                                g = 2 * j + th
                                to = bank[:, u * P + j * HD:u * P + (j + 1) * HD]
                                nc.tensor.matmul(to, rbT[:, g, u * P:(u + 1) * P], GH[:, g, u * P + HD:(u + 1) * P], start=True, stop=False)
                                last = nc.tensor.matmul(to, rkT[:, g, u * P:(u + 1) * P], tok["v"][:, t, j * HD:(j + 1) * HD], start=False, stop=True)
                        last.then_inc(ringA.full, 1)

                steps = {"lora": lora, "proj": proj, "small": small_, "sums": sums, "turn": turn, "A": a_part, "AV": av, "level": level, "tail": tail}
                for name, *args in script:
                    steps[name](*args)

            @block.sync
            def _(sp):
                n = 0
                sp.dma_start(wl[:], win[:, :, n0:n0 + 2 * LORA + GATE_LORA]).then_inc(wl_landed, 16)
                for to, src in ((w2[:], A["rwkv_w2_2"][0]), (a2[:], A["rwkv_a2_2"][0]),
                                (mu, A["mu_main_cols"]), (mu_x[0][:], A["mu_w_col"]), (mu_x[1][:], A["mu_a_col"]), (mu_x[2][:], A["mu_g_col"]),
                                (w0c, A["rwkv_w0_2_cols"]), (a0c, A["rwkv_a0_2_cols"]), (kkc, A["rwkv_k_k_2_cols"]),
                                (kac, A["rwkv_k_a_2_cols"]), (rkc, A["rwkv_r_k_2_cols"])):
                    sp.dma_start(to, src).then_inc(small, 16)
                    n += 1
                assert n == E.n_small

                def load(m):
                    if m >= NW:
                        sp.wait_ge(ringA.full, ringA.nth((KIND[(m - NW) % 3], (m - NW) // 3, 1)))
                    col = (m % 3) * RW + (m // 3) * P
                    sp.dma_start(w[m % NW][:], win[:, :, col:col + P]).then_inc(w_landed[m % NW], 16)

                for m in range(NW):
                    load(m)
                for c in range(NPAIR):
                    sp.wait_ge(ringA.free, ringA.nth(("tv", c, 1)))
                    sp.dma_start(E.v_dram[:, :, c * P:(c + 1) * P], tok["v"][:]).then_inc(S_["rstore"], 16)
                    for m in range(NW + 3 * c, min(NW + 3 * c + 3, 3 * NPAIR)):
                        load(m)
                    sp.wait_ge(ringD.free, ringD.nth(("Q", c, 1)))
                    sp.wait_ge(ringA.free, ringA.nth(("Yi", c, 1)))
                    for to, src in ((E.mt_dram, MTs), (E.n_dram, Ns), (E.qt_dram, QTs)):
                        sp.dma_start(to[:, c * S:(c + 1) * S], src).then_inc(S_["stored"], 16)
                    sp.dma_start(E.yi_dram[:, :, c * P:(c + 1) * P], Yi).then_inc(S_["stored"], 16)
                sp.wait_ge(S_["stored"], 64 * NPAIR)
                sp.wait_ge(S_["rstore"], 16 * NPAIR)

            @block.gpsimd
            def _(pool):
                ready = E.sem("pool_masks")
                count = 0

                def done(ins):
                    nonlocal count
                    ins.then_inc(ready, 1)
                    count += 1
                    pool.wait_ge(ready, count)

                def keep(ap, pattern, op, base, mult):
                    done(nc.gpsimd.affine_select(out=ap, in_=ap, compare_op=op, fill=0.0, base=base, pattern=pattern, channel_multiplier=mult))

                def blocks(ap, size):
                    v3 = ap.rearrange("p (b n) -> p b n", n=size)
                    keep(v3, [[-size, P // size], [0, size]], ALU.is_ge, 0, 1)
                    keep(v3, [[size, P // size], [0, size]], ALU.is_ge, size - 1, -1)

                for ap in (blocksum[:], m_up[:], m_upeq[:], m_low0[:], m_level[:]):
                    done(nc.gpsimd.memset(ap, 1.0))
                blocks(blocksum[:], HD)
                blocks(m_up[:], C)
                keep(m_up[:], [[1, P]], ALU.is_gt, 0, -1)
                blocks(m_upeq[:], C)
                keep(m_upeq[:], [[1, P]], ALU.is_ge, 0, -1)
                blocks(m_low0[:], 2)
                keep(m_low0[:], [[-1, P]], ALU.is_gt, 0, 1)
                for m in range(0, LEVELS + 1):
                    half = 2 ** m
                    ap = m_level[:, m, :]
                    blocks(ap, 2 * half)
                    v3 = ap.rearrange("p (b n) -> p b n", n=2 * half)
                    keep(v3, [[0, P // (2 * half)], [1, 2 * half]], ALU.is_ge, -half, 0)
                    keep(v3, [[2 * half, P // (2 * half)], [0, 2 * half]], ALU.is_ge, half - 1, -1)
                done(nc.gpsimd.memset(restart[:], 1.0))
                keep(restart[:].rearrange("p (b n) -> p b n", n=C), [[0, NC], [1, C]], ALU.is_gt, 0, 0)
                done(nc.gpsimd.memset(headsel[:], 1.0))
                keep(headsel[:, 0:1], [[0, 1]], ALU.is_ge, HD - 1, -1)
                keep(headsel[:, 1:2], [[0, 1]], ALU.is_ge, -HD, 1)
                pool.sem_inc(masks_set, E.n_masks)
                for c in range(NPAIR):
                    for m in range(1, LEVELS + 1):
                        for g in range(4):
                            if m == 1:
                                pool.wait_ge(ringD.free, ringD.nth(("ab", c, g)))
                                if c > 0:
                                    pool.wait_ge(S_["stored"], 64 * c)
                            else:
                                pool.wait_ge(ringA.full, ringA.nth(("T1", c, m - 1, g)))
                            nc.gpsimd.tensor_tensor(L[:, g, :].rearrange("p (u n) -> p u n", u=UNITS), abT[:, g, :].rearrange("p (u n) -> p u n", u=UNITS),
                                                    m_level[:, m:m + 1, :].broadcast_to([P, UNITS, P]), ALU.mult).then_inc(S_["level"], 1)

            @block.scalar
            def _(act):
                def got(key):
                    act.wait_ge(ringA.full, ringA.nth(key))
                    return ringA.bank(key)

                def lora():
                    for i, n in enumerate((LORA, LORA, GATE_LORA)):
                        for hf in range(NH):
                            bank = got(("lora", i, hf))
                            if i > 0 and hf == 0:
                                act.wait_ge(S_["lora"], i)
                            nc.scalar.copy(z[0:n, 1 + hf * HALF:1 + (hf + 1) * HALF], bank[0:n, :]).then_inc(ringA.free, 1)
                    act.wait_ge(S_["lora"], 1)
                    nc.scalar.activation(xw[:], xw[:], ACT.Tanh).then_inc(S_["tanh"], 1)
                    act.wait_ge(S_["lora"], 3)
                    nc.scalar.activation(E.xg[:], E.xg[:], ACT.Sigmoid)

                def proj(c, kind):
                    m = 3 * c + KIND.index(kind)
                    for hf in range(NH):
                        bank = got((kind, c, hf))
                        if hf == 0 and m > 0:
                            act.wait_ge(S_["shift"], m)
                        nc.scalar.copy(z[:, 1 + hf * HALF:1 + (hf + 1) * HALF], bank[:]).then_inc(ringA.free, 1)

                def small_(c):
                    for name, to, bias in (("w", lw, w0c), ("a", rate, a0c)):
                        for hf in range(NH):
                            bank = got((name, c, hf))
                            if c > 0 and hf == 0:
                                if name == "w":
                                    act.wait_ge(S_["front"], c)
                                else:
                                    act.wait_ge(ringA.full, ringA.nth(("bonus", c - 1)))
                            nc.scalar.activation(to[:, hf * HALF:(hf + 1) * HALF], bank[:], ACT.Sigmoid, bias=bias[:, c:c + 1]).then_inc(ringA.free, 1)
                    act.wait_ge(S_["shift"], 3 * c + 2)
                    if c > 0:
                        act.wait_ge(S_["front"], c)
                    nc.scalar.activation(tmp[:], k[:], ACT.Square, scale=kkc[:, c:c + 1]).then_inc(S_["sq"], 1)

                def sums(c):
                    for hf in range(NH):
                        bank = got(("n", c, hf))
                        if hf == 0:
                            act.wait_ge(ringA.full, ringA.nth(("n", c, 1)))
                        nc.scalar.activation(tmp[:, hf * HALF:(hf + 1) * HALF], bank[:], ACT.Sqrt).then_inc(ringA.free, 1)
                    act.wait_ge(S_["cc"], c + 1)
                    nc.scalar.activation(e2[:], cl[:], ACT.Exp, scale=-1.0).then_inc(S_["exp1"], 1)
                    nc.scalar.activation(cl[:], cl[:], ACT.Exp).then_inc(S_["exp2"], 1)
                    nc.scalar.activation(E.carry[:, c, :], E.carry[:, c, :], ACT.Exp)
                    nc.scalar.activation(lw[:], lw[:], ACT.Exp).then_inc(S_["exp3"], 1)

                def turn(c):
                    for x in "vkba":
                        for hf in range(NH):
                            bank = got(("t" + x, c, hf))
                            if x == "v" and hf == 0 and c > 0:
                                act.wait_ge(S_["rstore"], 16 * c)
                            nc.scalar.copy(tok[x][:, 4 * hf:4 * hf + 4, :], bank.rearrange("p (t n) -> p t n", t=4)).then_inc(ringA.free, 1)
                    bank = got(("bonus", c))
                    nc.scalar.copy(E.bonus[:, :, 2 * c:2 * c + 2], bank[:, 0:2 * NT].rearrange("p (t j) -> p t j", t=NT)).then_inc(ringA.free, 1)

                def a_part(c):
                    pass

                def av(c):
                    for g in range(4):
                        bank = got(("AV", c, g))
                        nc.scalar.copy(AV[:, g, :], bank[:, 0:UNITS * HD]).then_inc(ringA.free, 1)

                def level(c, m):
                    for g in range(4):
                        bank = got(("T1", c, m, g))
                        if not (c == 0 and m == 1):
                            before = (c, m - 1) if m > 1 else (c - 1, LEVELS)
                            act.wait_ge(ringD.full, ringD.nth(("dXT", before[0], before[1], g)))
                        nc.scalar.copy(T1[:, g, :], bank[:]).then_inc(ringA.free, 1)

                def tail(c):
                    for g in range(4):
                        bank = got(("GH", c, g))
                        nc.scalar.copy(GH[:, g, :], bank[:]).then_inc(ringA.free, 1)
                    for th in range(2):
                        bank = got(("Yi", c, th))
                        nc.scalar.copy(Yi[:, 4 * th:4 * th + 4, :], bank.rearrange("p (t n) -> p t n", t=4)).then_inc(ringA.free, 1)

                steps = {"lora": lora, "proj": proj, "small": small_, "sums": sums, "turn": turn, "A": a_part, "AV": av, "level": level, "tail": tail}
                for name, *args in script:
                    steps[name](*args)

            @block.vector
            def _(dve):
                link = Chain(E.dve_chain)
                link.n = E.chain_n
                def mixed(dst, n, m, free_sem):
                    link(dve, nc.vector.tensor_tensor(dst, z[0:n, 0:S], z[0:n, 1:1 + S], ALU.subtract))
                    nc.vector.scalar_tensor_tensor(dst, dst, m, z[0:n, 1:1 + S], ALU.mult, ALU.add).then_inc(free_sem, 1)

                def lora():
                    for i, (n, dst) in enumerate(((LORA, xw[:]), (LORA, xa[:]), (GATE_LORA, E.xg[:]))):
                        dve.wait_ge(ringA.free, ringA.nth(("lora", i, 1)))
                        mixed(dst, n, mu_x[i][:], S_["lora"])

                def proj(c, kind):
                    i = KIND.index(kind)
                    dve.wait_ge(ringA.free, ringA.nth((kind, c, 1)))
                    dst = {"r": r[c % 2], "k": k, "v": v}[kind]
                    if kind == "v" and c > 0:
                        dve.wait_ge(ringA.full, ringA.nth(("tv", c - 1, 1)))
                    if c >= 2 and kind == "r":
                        dve.wait_ge(ringD.free, ringD.nth(("Q", c - 2, 1)))
                    if c >= 1 and kind == "k":
                        dve.wait_ge(ringD.full, ringD.nth(("rk", c - 1, 3)))
                        dve.wait_ge(ringA.full, ringA.nth(("tk", c - 1, 1)))
                    mixed(dst[:], P, mu[:, i * 4 + c:i * 4 + c + 1], S_["shift"])

                def small_(c):
                    V = nc.vector
                    dve.wait_ge(S_["shift"], 3 * c + 2)
                    dve.wait_ge(ringA.free, ringA.nth(("w", c, 1)))
                    if c == 0:
                        dve.wait_ge(masks_set, E.n_masks)
                    link(dve, V.tensor_scalar(lw[:], lw[:], -DECAY, None, ALU.mult))
                    link(dve, V.tensor_tensor_scan(cl[:], restart[:], lw[:], 0.0, ALU.mult, ALU.add))
                    cl3 = cl[:].rearrange("p (c n) -> p c n", n=C)
                    link(dve, V.tensor_copy(ctr[:].rearrange("p (c o) -> p c o", o=1), cl3[:, :, C // 2 - 1:C // 2]))
                    carry = E.carry[:, c, :]
                    link(dve, V.tensor_tensor(carry.rearrange("p (c o) -> p c o", o=1), cl3[:, :, C - 1:C], ctr[:].rearrange("p (c o) -> p c o", o=1), ALU.subtract))
                    link(dve, V.tensor_tensor(carry[:, 0:NC - 1], carry[:, 0:NC - 1], ctr[:, 1:NC], ALU.add))
                    link(dve, V.tensor_tensor(cl3, cl3, ctr[:].rearrange("p (c o) -> p c o", o=1).broadcast_to([P, NC, C]), ALU.subtract))
                    V.tensor_tensor(lw[:], cl[:], lw[:], ALU.subtract).then_inc(S_["cc"], 1)

                def sums(c):
                    V = nc.vector
                    K, R = k, r[c % 2]
                    if c >= 1:
                        dve.wait_ge(ringD.full, ringD.nth(("rk", c - 1, 3)))
                        dve.wait_ge(ringA.full, ringA.nth(("ta", c - 1, 1)))
                    dve.wait_ge(ringA.free, ringA.nth(("n", c, 1)))
                    link(dve, V.tensor_scalar(tmp[:], tmp[:], 1e-12, None, ALU.max))
                    link(dve, V.reciprocal(tmp[:], tmp[:]))
                    link(dve, V.scalar_tensor_tensor(at[:], K[:], kkc[:, c:c + 1], tmp[:], ALU.mult, ALU.mult))
                    link(dve, V.tensor_tensor(bt[:], at[:], rate[:], ALU.mult))
                    link(dve, V.tensor_scalar(rate[:], rate[:], kac[:, c:c + 1], ka1[:, c:c + 1], ALU.mult, ALU.add))
                    link(dve, V.tensor_tensor(K[:], K[:], rate[:], ALU.mult))
                    link(dve, V.scalar_tensor_tensor(rate[:], R[:], rkc[:, c:c + 1], K[:], ALU.mult, ALU.mult))
                    dve.wait_ge(S_["exp1"], c + 1)
                    link(dve, V.tensor_tensor(K[:], K[:], e2[:], ALU.mult))
                    link(dve, V.tensor_tensor(bt[:], bt[:], e2[:], ALU.mult))
                    dve.wait_ge(S_["exp2"], c + 1)
                    link(dve, V.tensor_tensor(R[:], R[:], cl[:], ALU.mult))
                    dve.wait_ge(S_["exp3"], c + 1)
                    V.scalar_tensor_tensor(at[:], at[:], -1.0, lw[:], ALU.mult, ALU.mult).then_inc(S_["front"], 1)

                def turn(c):
                    pass

                def av(c):
                    pass

                def a_part(c):
                    V = nc.vector
                    if c > 0:
                        dve.wait_ge(ringA.full, ringA.nth(("Yi", c - 1, 1)))
                        dve.wait_ge(S_["stored"], 64 * c)
                    wide = lambda m: m.rearrange("p (o n) -> p o n", o=1).broadcast_to([P, UNITS, P])
                    u3 = lambda x: x.rearrange("p (u n) -> p u n", u=UNITS)
                    for g in range(4):
                        for name, to, m in (("ab", abT, m_up), ("X", Xm, m_low0), ("ak", akT, m_up), ("rb", rbT, m_upeq), ("rk", rkT, m_upeq)):
                            key = (name, c, g)
                            dve.wait_ge(ringD.full, ringD.nth(key))
                            if name != "X":
                                V.tensor_tensor(u3(to[:, g, :]), u3(ringD.bank(key)), wide(m[:]), ALU.mult).then_inc(ringD.free, 1)
                                if name == "ab":
                                    dve.wait_ge(ringD.free, ringD.nth(key))
                                    link(dve, V.tensor_tensor(u3(XT[:, g, :]), u3(abT[:, g, :]), m_level[:, 0:1, :].broadcast_to([P, UNITS, P]), ALU.mult))
                                    link(dve, V.tensor_tensor(u3(XT[:, g, :]), u3(XT[:, g, :]), wide(E.ident[:]), ALU.add))
                            else:
                                link(dve, V.tensor_tensor(u3(Xm[:, g, :]), u3(ringD.bank(key)), wide(m[:]), ALU.mult))
                                V.tensor_tensor(u3(Xm[:, g, :]), u3(Xm[:, g, :]), wide(E.ident[:]), ALU.add).then_inc(ringD.free, 1)

                def level(c, m):
                    V = nc.vector
                    for g in range(4):
                        if m < LEVELS:
                            key = ("dX", c, m, g)
                            dve.wait_ge(ringD.full, ringD.nth(key))
                            V.tensor_tensor(Xm[:, g, :], Xm[:, g, :], ringD.bank(key)[:], ALU.add).then_inc(ringD.free, 1)
                        key = ("dXT", c, m, g)
                        dve.wait_ge(ringD.full, ringD.nth(key))
                        V.tensor_tensor(XT[:, g, :], XT[:, g, :], ringD.bank(key)[:], ALU.add).then_inc(ringD.free, 1)

                def tail(c):
                    V = nc.vector
                    dve.wait_ge(S_["level"], 4 * LEVELS * (c + 1))
                    chunk = lambda to, q: to.rearrange("p (t q n) -> p t q n", q=2, n=HD)[:, :, q, :]
                    for q in range(2):
                        dve.wait_ge(ringD.full, ringD.nth(("MT", c, q)))
                        V.tensor_tensor(chunk(MTs, q), ringD.bank(("MT", c, q)).rearrange("p (t n) -> p t n", n=HD),
                                        E.ident2[:].rearrange("p (o n) -> p o n", o=1).broadcast_to([P, NT, HD]), ALU.add).then_inc(ringD.free, 1)
                    for q in range(2):
                        dve.wait_ge(ringD.full, ringD.nth(("N", c, q)))
                        V.tensor_copy(chunk(Ns, q), ringD.bank(("N", c, q)).rearrange("p (t n) -> p t n", n=HD)).then_inc(ringD.free, 1)
                    for th in range(2):
                        cols4 = slice(th * HALF, (th + 1) * HALF)
                        dve.wait_ge(ringD.full, ringD.nth(("Q", c, th)))
                        V.tensor_tensor(QTs[:, cols4], ringD.bank(("Q", c, th))[:], r[c % 2][:, cols4], ALU.add).then_inc(ringD.free, 1)

                link(dve, nc.vector.memset(z[:, 0:1], 0.0))
                dve.wait_ge(small, 16 * E.n_small)
                link(dve, nc.vector.tensor_scalar(ka1, kac, -1.0, 1.0, ALU.mult, ALU.add))
                link(dve, nc.vector.tensor_copy(E.ident2[0:HD, :], E.ident[0:HD, 0:HD]))
                link(dve, nc.vector.tensor_copy(E.ident2[HD:P, :], E.ident[HD:P, HD:P]))
                steps = {"lora": lora, "proj": proj, "small": small_, "sums": sums, "turn": turn, "A": a_part, "AV": av, "level": level, "tail": tail}
                for name, *args in script:
                    steps[name](*args)
                E.chain_n = link.n


N_GROUPS, PER_GROUP = 4, 8
EXPERTS = N_GROUPS * PER_GROUP
TOP_K = 2
EH = 512
ASSIGNED = S * TOP_K
OVER = (ASSIGNED - 1) // P
BLOCKS = EXPERTS + OVER
SLOTS = BLOCKS * P


def stage_mix(nc, E, A, rows_in, rows_out, normed_out, y_slots):
    ZW = 256
    H = GW // HD
    NR = N_GROUPS + EXPERTS
    with ExitStack() as st:
        sb = lambda name, shape, dt=F32: E.sb(name, shape, dt, ctx=st)
        w_uv, w_o = sb("w_uv", [P, ND, 2 * GW]), sb("w_o", [P, ND, D])
        ws, wsT = sb("ws", [P, H, P]), sb("wsT", [P, H, P])
        bs = sb("bs", [P, H])
        ln_w, ln_b, gn_w, gn_b = (sb(x, [P, 512]) for x in ("gln_w", "gln_b", "gn_w", "gn_b"))
        g2 = sb("g2", [GATE_LORA, RW])
        gate = sb("gate1", [P, D])
        rw, rb = sb("rw", [P, ND, NR]), sb("rb", [P, NR])
        STREAMS = ("mt", "n", "qt", "yi", "v")
        stream = {x: [sb(f"s_{x}{i}", [P, 512]) for i in range(2)] for x in STREAMS}
        landed = {x: [E.sem(f"s_{x}_landed{i}") for i in range(2)] for x in STREAMS}
        T = [sb(f"T{i}", [P, NPAIR * HD]) for i in range(5)]
        u = [sb(f"gu{i}", [P, GW]) for i in range(2)]
        vg = sb("vg", [P, GW])
        vn = [sb(f"vn{i}", [P, GW]) for i in range(2)]
        y = [sb(f"y{i}", [P, D]) for i in range(2)]
        sq = sb("gn_sq", [P, RW])
        yT = [sb(f"y2T{i}", [P, ND, P]) for i in range(2)]
        NX = 2
        xs = [sb(f"x2_{i}", [P, D]) for i in range(NX)]
        h2T = [sb(f"h2T{i}", [P, ND, P]) for i in range(2)]
        stats, mv_ = sb("g_stats", [P, 6]), sb("g_mv", [P, 2])
        gdev, grstd = sb("g_dev", [P, 1]), sb("g_rstd", [P, 1])
        s1, s2, dev8, inv8 = (sb(x, [P, H]) for x in ("gn_s1", "gn_s2", "gn_dev", "gn_inv"))
        small = E.sem("mix_small")
        zeros, zeros_set, zeroed = sb("zeros", [P, ZW]), E.sem("zeros_set"), E.sem("slots_zeroed")
        w_landed = {x: E.sem("mix_" + x) for x in ("u", "v", "o", "ws", "row")}
        x_landed = [E.sem(f"x2_landed{i}") for i in range(NX)]
        x_stored = [E.sem(f"x2_stored{i}") for i in range(NX)]
        n_stored = [E.sem(f"n2_stored{i}") for i in range(2)]
        sems = {x: E.sem("mix_" + x) for x in ("tril", "var", "dev", "vn", "T", "ya", "yb", "s2", "sq", "yc", "dev8", "rows")}
        ringA = Ring(E.banks[0:4], E.sem("mixA_full"), E.sem("mixA_free"))
        ringD = Ring(E.banks[4:8], E.sem("mixD_full"), E.sem("mixD_free"))

        class Slot:
            def __getitem__(self, at):
                _, c, cols = at
                t = cols.start // P
                return h2T[t % 2][:, c, :]

        norm = NormTurn(nc, E, "n2", ringA, st, sems["rows"], Slot(), E.mod[:, 4 * ND:5 * ND], E.mod[:, 3 * ND:4 * ND])
        norm.stored = n_stored
        win = A["w_in_2"][0].rearrange("(c p) n -> p c n", p=P)

        with nc.Block() as block:

            @block.tensor
            def _(pe):
                def take(ring, key):
                    bank, free = ring.take(key)
                    wait(pe, ring.free, free)
                    return bank

                def uv(t, i):
                    bank = take(ringA, ("u" if i == 0 else "v", t))
                    for d in range(ND):
                        last = nc.tensor.matmul(bank[:], E.hT[:, d, t * P:(t + 1) * P], w_uv[:, d, i * GW:(i + 1) * GW],
                                                start=(d == 0), stop=(d == ND - 1))
                    last.then_inc(ringA.full, 1)

                def chain(c):
                    if c == 0 or c >= NC - 1:
                        return
                    t, q = c // 2, c % 2
                    if q == 0 or c == 1:
                        pe.wait_ge(landed["mt"][t % 2], 16 * (t // 2 + 1))
                    pe.wait_ge(sems["T"], c + 1)
                    bank = take(ringD, ("T", c))
                    for p in range(NPAIR):
                        for j in range(2):
                            rows = slice(j * HD, (j + 1) * HD)
                            last = nc.tensor.matmul(bank[rows, p * HD:(p + 1) * HD], stream["mt"][t % 2][rows, p * P + q * HD:p * P + (q + 1) * HD],
                                                    T[c % 5][rows, p * HD:(p + 1) * HD], start=True, stop=True)
                    last.then_inc(ringD.full, 1)

                def mix(t):
                    pe.wait_ge(sems["vn"], t + 1)
                    bank = take(ringD, ("mix", t))
                    for h in range(H):
                        last = nc.tensor.matmul(bank[:, h * HD:(h + 1) * HD], wsT[:, h, :], vn[t % 2][:, h * HD:(h + 1) * HD], start=True, stop=True)
                    last.then_inc(ringD.full, 1)

                def rwkv_rows(t):
                    pe.wait_ge(landed["qt"][t % 2], 16 * (t // 2 + 1))
                    pe.wait_ge(sems["T"], min(2 * t + 2, NC))
                    for j in range(2):
                        bank = take(ringD, ("y", t, j))
                        rows = slice(j * HD, (j + 1) * HD)
                        for q in range(2):
                            for p in range(NPAIR):
                                last = nc.tensor.matmul(bank[q * C:(q + 1) * C, p * HD:(p + 1) * HD],
                                                        stream["qt"][t % 2][rows, p * P + q * C:p * P + (q + 1) * C],
                                                        T[(2 * t + q) % 5][rows, p * HD:(p + 1) * HD], start=True, stop=True)
                        last.then_inc(ringD.full, 1)
                    bank = take(ringD, ("g", t))
                    nc.tensor.matmul(bank[:], E.xg[:, t * P:(t + 1) * P], g2[:], start=True, stop=True).then_inc(ringD.full, 1)

                def turn(t):
                    pe.wait_ge(sems["ya"], t + 1)
                    pe.wait_ge(sems["yb"], t + 1)
                    for h in range(2):
                        bank = take(ringA, ("yT", t, h))
                        for k in range(4):
                            last = nc.tensor.transpose(bank[:, k * P:(k + 1) * P], y[t % 2][:, (4 * h + k) * P:(4 * h + k + 1) * P], E.ident[:])
                        last.then_inc(ringA.full, 1)

                def out(t):
                    pe.wait_ge(ringA.free, ringA.nth(("yT", t, 1)))
                    for hf in range(2):
                        bank = take(ringD, ("o", t, hf))
                        for d in range(ND):
                            last = nc.tensor.matmul(bank[:], yT[t % 2][:, d, :], w_o[:, d, hf * HALF:(hf + 1) * HALF],
                                                    start=(d == 0), stop=(d == ND - 1))
                        last.then_inc(ringD.full, 1)

                def router(t):
                    pe.wait_ge(ringA.free, ringA.nth(("t", t, 1)))
                    bank = take(ringD, ("r", t))
                    for d in range(ND):
                        last = nc.tensor.matmul(bank[:, 0:NR], h2T[t % 2][:, d, :], rw[:, d, :], start=(d == 0), stop=(d == ND - 1))
                    last.then_inc(ringD.full, 1)

                pe.wait_ge(sems["tril"], 1)
                for h in range(2):
                    bank = take(ringA, ("ws", h))
                    for k in range(4):
                        last = nc.tensor.transpose(bank[:, k * P:(k + 1) * P], ws[:, 4 * h + k, :], E.ident[:])
                    last.then_inc(ringA.full, 1)
                pe.wait_ge(small, 16 * 6)
                for t in range(NT + 5):
                    if t < NT:
                        if t == 0:
                            pe.wait_ge(w_landed["u"], 16)
                        uv(t, 0)
                        chain(2 * t)
                        if t == 0:
                            pe.wait_ge(w_landed["v"], 16)
                        uv(t, 1)
                        chain(2 * t + 1)
                    if 1 <= t <= NT:
                        mix(t - 1)
                        rwkv_rows(t - 1)
                    if 2 <= t <= NT + 1:
                        turn(t - 2)
                    if 3 <= t <= NT + 2:
                        if t == 3:
                            pe.wait_ge(w_landed["o"], 16)
                        out(t - 3)
                    if 4 <= t <= NT + 3:
                        norm.turn(pe, t - 4)
                    if 5 <= t:
                        router(t - 5)

            @block.sync
            def _(sp):
                sp.dma_start(ws[:], A["gmlp_ws_2"][0].rearrange("h t s -> t h s")).then_inc(w_landed["ws"], 16)
                sp.dma_start(w_uv[:, :, 0:GW], win[:, :, 0:GW]).then_inc(w_landed["u"], 16)
                sp.dma_start(bs[:], A["gmlp_bs_cols"]).then_inc(small, 16)
                sp.dma_start(g2[:], A["rwkv_g2_2"][0]).then_inc(small, 16)
                sp.dma_start(rw[:, :, 0:N_GROUPS], A["router_group_w_2"][0].rearrange("(c p) n -> p c n", p=P)).then_inc(small, 16)
                sp.dma_start(rw[:, :, N_GROUPS:NR], A["router_expert_w_2"][0].rearrange("(c p) n -> p c n", p=P)).then_inc(small, 16)
                sp.dma_start(rb[:, 0:N_GROUPS], A["router_group_b_2"].broadcast_to([P, N_GROUPS])).then_inc(small, 16)
                sp.dma_start(rb[:, N_GROUPS:NR], A["router_expert_b_2"].broadcast_to([P, EXPERTS])).then_inc(small, 16)
                sp.dma_start(w_uv[:, :, GW:2 * GW], win[:, :, GW:2 * GW]).then_inc(w_landed["v"], 16)
                for to, name in ((ln_w, "gmlp_ln_w_2"), (ln_b, "gmlp_ln_b_2"), (gn_w, "rwkv_gn_w_2"), (gn_b, "rwkv_gn_b_2")):
                    sp.dma_start(to[:], A[name].broadcast_to([P, 512])).then_inc(w_landed["row"], 16)
                sp.dma_start(gate[:], E.gates[:, 0:D]).then_inc(w_landed["row"], 16)

                def load(x, t):
                    to = stream[x][t % 2]
                    if t >= 2:
                        if x == "mt":
                            sp.wait_ge(ringD.full, ringD.nth(("T", 2 * t - 3)))
                        elif x == "n":
                            sp.wait_ge(sems["T"], 2 * t - 1)
                        elif x == "qt":
                            sp.wait_ge(ringD.full, ringD.nth(("y", t - 2, 1)))
                        else:
                            sp.wait_ge(sems["yb"], t - 1)
                    if x in ("yi", "v"):
                        src = {"yi": E.yi_dram, "v": E.v_dram}[x][:, t, :]
                        sp.dma_start(to[:], src).then_inc(landed[x][t % 2], 16)
                    else:
                        src = {"mt": E.mt_dram, "n": E.n_dram, "qt": E.qt_dram}[x].rearrange("p (c n) -> p c n", c=NPAIR)[:, :, t * P:(t + 1) * P]
                        sp.dma_start(to[:].rearrange("p (c n) -> p c n", c=NPAIR), src).then_inc(landed[x][t % 2], 16)

                def load_x(t):
                    if t >= NX:
                        sp.wait_ge(x_stored[t % NX], 16 * (t // NX))
                        sp.wait_ge(norm.xn_set, t - NX + 1)
                    sp.dma_start(xs[t % NX][:], rows_in[t * P:(t + 1) * P, :]).then_inc(x_landed[t % NX], 16)

                def store(t):
                    sp.wait_ge(sems["rows"], t + 1)
                    sp.dma_start(rows_out[t * P:(t + 1) * P, :], xs[t % NX][:]).then_inc(x_stored[t % NX], 16)
                    sp.wait_ge(norm.xn_set, t + 1)
                    sp.dma_start(normed_out[t * P:(t + 1) * P, :], norm.rows[t % 2][:]).then_inc(n_stored[t % 2], 16)

                for t in range(2):
                    for x in STREAMS:
                        load(x, t)
                    load_x(t)
                sp.dma_start(w_o[:], A["w_out_2"][0].rearrange("(c p) n -> p c n", p=P)).then_inc(w_landed["o"], 16)
                sp.wait_ge(zeros_set, 1)
                further = y_slots[EXPERTS * P:SLOTS, :].rearrange("(p b) d -> p (b d)", p=P).rearrange("p (k n) -> p k n", n=ZW)
                sp.dma_start(further, zeros[:].rearrange("p (o n) -> p o n", o=1).broadcast_to([P, OVER * D // ZW, ZW])).then_inc(zeroed, 16)
                for t in range(1, NT + 5):
                    if t + 1 < NT and t >= 1:
                        for x in STREAMS:
                            load(x, t + 1)
                    if 4 <= t < NT + 4:
                        store(t - 4)
                        if t - 4 + NX < NT:
                            load_x(t - 4 + NX)
                sp.wait_ge(zeroed, 16)
                for i in range(2):
                    sp.wait_ge(x_stored[i], 16 * (NT // 2))
                    sp.wait_ge(n_stored[i], 16 * (NT // 2))

            @block.gpsimd
            def _(pool):
                nc.gpsimd.memset(zeros[:], 0.0).then_inc(zeros_set, 1)
                pool.wait_ge(w_landed["ws"], 16)
                nc.gpsimd.affine_select(out=ws[:], in_=ws[:], compare_op=ALU.is_ge, fill=0.0, base=0,
                                        pattern=[[0, H], [-1, P]], channel_multiplier=1).then_inc(sems["tril"], 1)

            @block.scalar
            def _(act):
                def got(key):
                    act.wait_ge(ringA.full, ringA.nth(key))
                    return ringA.bank(key)

                for h in range(2):
                    nc.scalar.copy(wsT[:, 4 * h:4 * h + 4, :], got(("ws", h)).rearrange("p (h n) -> p h n", h=4)).then_inc(ringA.free, 1)
                for t in range(NT + 5):
                    if t < NT:
                        if t >= 2:
                            act.wait_ge(sems["ya"], t - 1)
                        nc.scalar.activation(u[t % 2][:], got(("u", t))[:], ACT.Gelu_apprx_tanh).then_inc(ringA.free, 1)
                        if t >= 1:
                            act.wait_ge(sems["vn"], t)
                        nc.scalar.activation(vg[:], got(("v", t))[:], ACT.Gelu_apprx_tanh).then_inc(ringA.free, 1)
                        act.wait_ge(sems["var"], t + 1)
                        nc.scalar.activation(gdev[:], mv_[:, 1:2], ACT.Sqrt, bias=E.eps_ln[:]).then_inc(sems["dev"], 1)
                    if 1 <= t <= NT:
                        act.wait_ge(sems["yc"], t)
                        nc.scalar.activation(sq[:], y[(t - 1) % 2][:, GW:D], ACT.Square).then_inc(sems["sq"], 1)
                        act.wait_ge(sems["s2"], t)
                        nc.scalar.activation(dev8[:], s2[:], ACT.Sqrt, bias=E.eps_gn[:], scale=1.0 / HD).then_inc(sems["dev8"], 1)
                    if 2 <= t <= NT + 1:
                        for h in range(2):
                            bank = got(("yT", t - 2, h))
                            if t >= 4 and h == 0:
                                act.wait_ge(ringD.full, ringD.nth(("o", t - 4, 1)))
                            nc.scalar.copy(yT[(t - 2) % 2][:, 4 * h:4 * h + 4, :], bank.rearrange("p (c n) -> p c n", c=4)).then_inc(ringA.free, 1)
                    if 4 <= t <= NT + 3:
                        norm.square(act, xs[(t - 4) % NX][:], t - 4)
                        if t >= 6:
                            act.wait_ge(ringD.full, ringD.nth(("r", t - 6)))
                        norm.evacuate(act, t - 4)

            @block.vector
            def _(dve):
                link = Chain(E.dve_chain)
                link.n = E.chain_n
                V = nc.vector
                heads = lambda ap: ap.rearrange("p (h n) -> p h n", n=HD)
                each = lambda ap, n: ap.rearrange("p (h o) -> p h o", o=1).broadcast_to([P, n, HD])

                def got(key):
                    dve.wait_ge(ringD.full, ringD.nth(key))
                    return ringD.bank(key)

                def step(c):
                    if c >= NC - 1:
                        return
                    t, q = c // 2, c % 2
                    if q == 0:
                        dve.wait_ge(landed["n"][t % 2], 16 * (t // 2 + 1))
                    part = stream["n"][t % 2][:].rearrange("p (c n) -> p c n", c=NPAIR)[:, :, q * HD:(q + 1) * HD]
                    to = heads(T[(c + 1) % 5][:])
                    F = E.carry[:, :, c:c + 1].broadcast_to([P, NPAIR, HD])
                    if c >= 4:
                        dve.wait_ge(ringD.full, ringD.nth(("y", (c - 4) // 2, 1)))
                    if c == 0:
                        V.tensor_tensor(to, part, F, ALU.mult).then_inc(sems["T"], 1)
                        return
                    link(dve, V.tensor_tensor(to, heads(got(("T", c))[:, 0:NPAIR * HD]), part, ALU.add))
                    dve.sem_inc(ringD.free, 1)
                    V.tensor_tensor(to, to, F, ALU.mult).then_inc(sems["T"], 1)

                def gmlp_norm(t):
                    dve.wait_ge(ringA.free, ringA.nth(("v", t)))
                    link(dve, V.bn_stats(stats[:], vg[:]))
                    V.bn_aggr(mv_[:], stats[:]).then_inc(sems["var"], 1)
                    dve.wait_ge(sems["dev"], t + 1)
                    link(dve, V.reciprocal(grstd[:], gdev[:]))
                    if t >= 2:
                        dve.wait_ge(ringD.full, ringD.nth(("mix", t - 2)))
                    to = vn[t % 2]
                    link(dve, V.tensor_scalar(to[:], vg[:], mv_[:, 0:1], grstd[:], ALU.subtract, ALU.mult))
                    link(dve, V.tensor_tensor(to[:], to[:], ln_w[:], ALU.mult))
                    V.tensor_tensor(to[:], to[:], ln_b[:], ALU.add).then_inc(sems["vn"], 1)

                def gmlp_rows(t):
                    if t >= 2:
                        dve.wait_ge(ringA.full, ringA.nth(("yT", t - 2, 1)))
                    to = y[t % 2][:, 0:GW]
                    V.tensor_tensor(heads(to), heads(got(("mix", t))), each(bs[:], H), ALU.add).then_inc(ringD.free, 1)
                    dve.wait_ge(ringD.free, ringD.nth(("mix", t)))
                    V.tensor_tensor(to, to, u[t % 2][:], ALU.mult).then_inc(sems["ya"], 1)

                def rwkv_rows(t):
                    yr = y[t % 2][:, GW:D]
                    dve.wait_ge(landed["yi"][t % 2], 16 * (t // 2 + 1))
                    dve.wait_ge(landed["v"][t % 2], 16 * (t // 2 + 1))
                    for j in range(2):
                        head = lambda ap: ap.rearrange("p (c j n) -> p c j n", j=2, n=HD)[:, :, j, :]
                        V.tensor_tensor(head(yr), heads(got(("y", t, j))[:, 0:NPAIR * HD]), head(stream["yi"][t % 2][:]), ALU.add).then_inc(ringD.free, 1)
                    dve.wait_ge(ringD.free, ringD.nth(("y", t, 1)))
                    link(dve, V.tensor_reduce(s1[:], heads(yr), X, ALU.add))
                    link(dve, V.tensor_scalar(s1[:], s1[:], 1.0 / HD, None, ALU.mult))
                    V.tensor_tensor(heads(yr), heads(yr), each(s1[:], H), ALU.subtract).then_inc(sems["yc"], 1)
                    dve.wait_ge(sems["sq"], t + 1)
                    V.tensor_reduce(s2[:], heads(sq[:]), X, ALU.add).then_inc(sems["s2"], 1)
                    vr = stream["v"][t % 2][:]
                    link(dve, V.tensor_tensor(heads(vr), heads(vr), each(E.bonus[:, t, :], H), ALU.mult))
                    dve.wait_ge(sems["dev8"], t + 1)
                    link(dve, V.reciprocal(inv8[:], dev8[:]))
                    link(dve, V.tensor_tensor(heads(yr), heads(yr), each(inv8[:], H), ALU.mult))
                    link(dve, V.tensor_tensor(yr, yr, gn_w[:], ALU.mult))
                    link(dve, V.tensor_tensor(vr, vr, gn_b[:], ALU.add))
                    link(dve, V.tensor_tensor(yr, yr, vr, ALU.add))
                    V.tensor_tensor(yr, yr, got(("g", t))[:], ALU.mult).then_inc(ringD.free, 1)
                    dve.wait_ge(ringD.free, ringD.nth(("g", t)))
                    dve.sem_inc(sems["yb"], 1)

                def residual(t):
                    x = xs[t % NX]
                    dve.wait_ge(x_landed[t % NX], 16 * (t // NX + 1))
                    for hf in range(2):
                        cols = slice(hf * HALF, (hf + 1) * HALF)
                        bank = got(("o", t, hf))
                        link(dve, V.tensor_tensor(sq2[:], bank[:], gate[:, cols], ALU.mult))
                        dve.sem_inc(ringD.free, 1)
                        ins = V.tensor_tensor(x[:, cols], x[:, cols], sq2[:], ALU.add)
                        if hf == 0:
                            link(dve, ins)
                    ins.then_inc(sems["rows"], 1)

                sq2 = sb("res_tmp", [P, HALF])
                dve.wait_ge(w_landed["row"], 16 * 5)
                dve.wait_ge(small, 16 * 6)
                V.memset(T[0][:], 0.0).then_inc(sems["T"], 1)
                for t in range(NT + 5):
                    if t < NT:
                        step(2 * t)
                        gmlp_norm(t)
                        step(2 * t + 1)
                    if 1 <= t <= NT:
                        gmlp_rows(t - 1)
                        rwkv_rows(t - 1)
                    if 4 <= t <= NT + 3:
                        norm.normalise(dve, link, xs[(t - 4) % NX][:], t - 4)
                    if 3 <= t <= NT + 2:
                        residual(t - 3)
                    if 5 <= t:
                        V.tensor_tensor(E.logits[:, t - 5, :], got(("r", t - 5))[:, 0:NR], rb[:], ALU.add).then_inc(ringD.free, 1)
                link(dve, V.memset(s1[:], 0.0))
                E.chain_n = link.n


NHC = EH // P


UP_PIECES, DOWN_PIECES = ("g0", "g1", "u0", "u1"), ("d0", "d1")
PIECES = UP_PIECES + DOWN_PIECES


def stage_experts(nc, E, A, normed, y_slots):
    NR = N_GROUPS + EXPERTS
    with ExitStack() as st:
        sb = lambda name, shape, dt=F32: E.sb(name, shape, dt, ctx=st)
        routes = ("gexp", "geq", "gone")
        gexp, geq, gone = (sb(x, [P, NT, N_GROUPS]) for x in routes)
        sel, sexp, seq, one1, one2 = (sb(x, [P, NT, PER_GROUP]) for x in ("sel", "sexp", "seq", "one1", "one2"))
        best, gprob, first, top1, top2, over, at, den = (sb(x, [P, NT]) for x in ("best", "gprob", "first", "top1", "top2", "over", "at_", "den"))
        both, pick, one32a, one32b, place = (sb(x, [P, NT, EXPERTS]) for x in ("both", "pick", "one32a", "one32b", "place"))
        base = sb("rank_base", [P, NT + 1, EXPERTS])
        nover, upto, over_at, e128 = (sb(x, [P, EXPERTS]) for x in ("nover", "upto", "over_at", "e128"))
        ovcmp, ovexp = sb("ovcmp", [P, OVER + 1, EXPERTS]), sb("ovexp", [P, OVER + 1])
        iota_j = sb("iota_j", [P, P])
        before = sb("before", [P, P])
        token_id = sb("token_id", [P, NT])
        part_i, part, block_i, block_f = sb("part_i", [P, NT], I32), sb("part", [P, NT]), sb("block_i", [P, NT], I32), sb("block_f", [P, NT])
        at_block = [sb(f"at_block{k}", [P, NT, BLOCKS]) for k in range(TOP_K)]
        idx = sb("idx", [P, BLOCKS], I32)
        ovexp_i, n_over = sb("ovexp_i", [P, OVER + 1], I32), sb("n_over", [P, 1], I32)
        PIECE = ND * EH // 2
        land = {x: sb("land_" + x, [P, PIECE]) for x in PIECES}
        w_hi, w_lo = ({x: sb(f"{h}_{x}", [P, PIECE], F32R) for x in PIECES} for h in ("hi", "lo"))
        xg = [sb(f"xg{i}", [P, D]) for i in range(2)]
        xm = sb("e_xm", [P, ND, P])
        x_hi, x_lo = (sb("e_" + x, [P, ND, P], F32R) for x in ("x_hi", "x_lo"))
        act_, hid = sb("e_act", [P, EH]), sb("e_hid", [P, EH])
        h_hi, h_lo = (sb("e_" + x, [P, NHC, P], F32R) for x in ("h_hi", "h_lo"))
        yb = [sb(f"yb{i}", [P, D]) for i in range(2)]
        at_part = [x[:].rearrange("p (t n) -> p t n", t=NT) for x in yb]

        R = {x: E.sem("route_" + x) for x in ("consts", "gsub", "gexp", "ssub", "sexp", "both", "ranks", "places", "table", "idx", "over")}
        two = lambda name: [E.sem(f"{name}{i}") for i in range(2)]
        xg_in, y_out = (two(x) for x in ("xg_landed", "y_stored"))
        landed, hi_set, lo_set = ({x: E.sem(f"{n}_{x}") for x in PIECES} for n in ("landed", "hi_set", "lo_set"))
        steps = ("xT_full", "xm_set", "x_hi_set", "x_lo_set", "gate_full", "up_full", "act_set", "hid_set", "hT_full", "h_hi_set", "h_lo_set",
                 "down_full", "y_set")
        M = {x: E.sem("moe_" + x) for x in steps}
        O = {x: E.sem("over_" + x) for x in steps + ("hi_set", "lo_set", "xg_landed", "y_stored", "through")}
        gate_b, up_b, xT_b, hT_b, down_b, rank_b = E.banks[0], E.banks[1], E.banks[2:4], E.banks[4], E.banks[5:7], E.banks[7]
        down_rows = E.psum[:, 5 * HALF:7 * HALF]
        gate, gate_landed = sb("gate2", [P, D]), E.sem("gate2_landed")
        scale, shift = E.mod[:, 4 * ND:5 * ND], E.mod[:, 3 * ND:4 * ND]
        views = {x: A[n][0].rearrange("e (c p) n -> e p c n", p=P) for x, n in (("g", "moe_w_gate_2"), ("u", "moe_w_up_2"), ("d", "moe_w_down_2"))}
        yv = y_slots.rearrange("(b p) d -> b p d", p=P)

        def piece_of(x, e):
            n = (NHC if x[0] == "d" else ND) // 2
            half = int(x[1])
            return views[x[0]][bass.ds(e, 1), :, half * n:(half + 1) * n, :].rearrange("o p c n -> p (o c) n")

        def chunks(ap, x):
            return ap.rearrange("p (c n) -> p c n", n=D if x[0] == "d" else EH)

        y_of = lambda b: yv[bass.ds(b, 1)].rearrange("o p d -> p (o d)")

        def need(eng, sem, value):
            if not isinstance(value, int) or value > 0:
                eng.wait_ge(sem, value)

        def blocks_in_turn(eng, step):
            for b in range(4):
                step(b, b % 2)
            with eng.Fori(2, EXPERTS // 2 - 1) as i:
                for s in range(2):
                    step(i * 2 + s, s)
            for b in range(EXPERTS - 2, EXPERTS):
                step(b, b % 2)

        sp_filled = []

        def further_blocks(eng, step, count=None):
            eng.wait_ge(R["over"], 1)
            filled = eng.value_load(n_over[0:1, 0:1], min_val=0, max_val=OVER)
            if count is not None:
                count.append(filled)
            with eng.Fori(0, OVER) as j:
                with eng.If(filled > j):
                    step(j)

        with nc.Block() as block:

            @block.sync
            def _(sp):
                def load(x, b):
                    need(sp, lo_set[x], b)
                    sp.dma_start(chunks(land[x][:], x), piece_of(x, b)).then_inc(landed[x], 16)

                for x in PIECES:
                    load(x, 0)
                sp.dma_start(gate[:], E.gates[:, D:2 * D]).then_inc(gate_landed, 16)
                for x in UP_PIECES:
                    load(x, 1)

                def step(b, s):
                    last = isinstance(b, int) and b + 2 >= EXPERTS
                    if not last:
                        for x in UP_PIECES:
                            load(x, b + 2)
                    if not (isinstance(b, int) and b + 1 >= EXPERTS):
                        for x in DOWN_PIECES:
                            load(x, b + 1)
                    if not (isinstance(b, int) and b == 0):
                        sp.wait_ge(M["y_set"], b)
                        sp.dma_start(y_of(b - 1), yb[1 - s][:]).then_inc(y_out[1 - s], 16)

                def load_further(j):
                    e = sp.value_load(ovexp_i[0:1, bass.ds(j, 1)], min_val=0, max_val=EXPERTS - 1)
                    for x in PIECES:
                        if isinstance(j, int):
                            sp.wait_ge(lo_set[x], EXPERTS)
                        sp.dma_start(chunks(land[x][:], x), piece_of(x, e)).then_inc(landed[x], 16)

                blocks_in_turn(sp, step)
                sp.wait_ge(R["over"], 1)
                load_further(0)
                sp.wait_ge(M["y_set"], EXPERTS)
                sp.dma_start(y_of(EXPERTS - 1), yb[1][:]).then_inc(y_out[1], 16)
                for s in range(2):
                    sp.wait_ge(y_out[s], 16 * (EXPERTS // 2))
                for x in PIECES:
                    sp.wait_ge(landed[x], 16 * (EXPERTS + 1))

                def further(j):
                    sp.wait_ge(O["y_set"], j + 1)
                    sp.dma_start(y_of(j + EXPERTS), yb[0][:]).then_inc(O["y_stored"], 16)
                    sp.wait_ge(O["y_stored"], j * 16 + 16)
                    sp.sem_inc(O["through"], 1)
                    with sp.If(sp_filled[0] > j + 1):
                        load_further(j + 1)

                further_blocks(sp, further, sp_filled)

            @block.tensor
            def _(pe):
                pe.wait_ge(R["consts"], 1)
                pe.wait_ge(R["both"], 1)
                flat = both[:].rearrange("p t e -> p (t e)")
                nc.tensor.matmul(rank_b[:, 0:NT * EXPERTS], before[:], flat, start=True, stop=True)
                nc.tensor.matmul(rank_b[:, NT * EXPERTS:2 * NT * EXPERTS], E.ones[:], flat, start=True, stop=True).then_inc(R["ranks"], 1)
                pe.wait_ge(R["places"], 1)
                for n in range(TOP_K * NT):
                    k, t = n // NT, n % NT
                    last = nc.tensor.matmul(rank_b[:, 0:BLOCKS], at_part[k][:, t, :], at_block[k][:, t, :], start=(n == 0), stop=(n == TOP_K * NT - 1))
                last.then_inc(R["table"], 1)

                def turn_x(x, full):
                    for h in range(2):
                        for c in range(4):
                            last = nc.tensor.transpose(xT_b[h][:, c * P:(c + 1) * P], x[:, (4 * h + c) * P:(4 * h + c + 1) * P], E.ident[:])
                        last.then_inc(full, 1)

                def three(bank, hi_t, lo_t, hi_w, lo_w, start, stop):
                    nc.tensor.matmul(bank, hi_t, hi_w, start=start, stop=False)
                    nc.tensor.matmul(bank, lo_t, hi_w, start=False, stop=False)
                    return nc.tensor.matmul(bank, hi_t, lo_w, start=False, stop=stop)

                def into_hidden(bank, pieces, full, ready):
                    for n, x in enumerate(pieces):
                        ready(x)
                        for k in range(ND // 2):
                            d = n * ND // 2 + k
                            last = three(bank[:], x_hi[:, d, :], x_lo[:, d, :], chunks(w_hi[x][:], x)[:, k, :], chunks(w_lo[x][:], x)[:, k, :],
                                         d == 0, d == ND - 1)
                    last.then_inc(full, 1)

                def turn_h(full):
                    for c in range(NHC):
                        last = nc.tensor.transpose(hT_b[:, c * P:(c + 1) * P], hid[:, c * P:(c + 1) * P], E.ident[:])
                    last.then_inc(full, 1)

                def down(full, ready):
                    for n, x in enumerate(DOWN_PIECES):
                        ready(x)
                        for h in range(2):
                            cols = slice(h * HALF, (h + 1) * HALF)
                            for k in range(NHC // 2):
                                c = n * NHC // 2 + k
                                last = three(down_b[h][:], h_hi[:, c, :], h_lo[:, c, :], chunks(w_hi[x][:], x)[:, k, cols], chunks(w_lo[x][:], x)[:, k, cols],
                                             c == 0, c == NHC - 1)
                            if n == 1:
                                last.then_inc(full, 1)

                pe.wait_ge(xg_in[0], 16)
                turn_x(xg[0], M["xT_full"])

                def step(b, s):
                    ready = lambda x: pe.wait_ge(lo_set[x], b + 1)
                    pe.wait_ge(M["x_lo_set"], b + 1)
                    need(pe, M["act_set"], b)
                    into_hidden(gate_b, UP_PIECES[0:2], M["gate_full"], ready)
                    need(pe, M["hid_set"], b)
                    into_hidden(up_b, UP_PIECES[2:4], M["up_full"], ready)
                    if not (isinstance(b, int) and b + 1 >= EXPERTS):
                        pe.wait_ge(xg_in[1 - s], (b + 1 - (1 - s)) * 8 + 16)
                        turn_x(xg[1 - s], M["xT_full"])
                    if not (isinstance(b, int) and b == 0):
                        down_of(b - 1)
                    pe.wait_ge(M["hid_set"], b + 1)
                    turn_h(M["hT_full"])

                def down_of(b):
                    pe.wait_ge(M["h_lo_set"], b + 1)
                    need(pe, M["y_set"], b)
                    down(M["down_full"], lambda x: pe.wait_ge(lo_set[x], b + 1))

                blocks_in_turn(pe, step)
                down_of(EXPERTS - 1)

                def further(j):
                    split = lambda x: pe.wait_ge(O["lo_set"], j * len(PIECES) + PIECES.index(x) + 1)
                    pe.wait_ge(O["xg_landed"], j * 16 + 16)
                    turn_x(xg[0], O["xT_full"])
                    pe.wait_ge(O["x_lo_set"], j + 1)
                    into_hidden(gate_b, UP_PIECES[0:2], O["gate_full"], split)
                    into_hidden(up_b, UP_PIECES[2:4], O["up_full"], split)
                    pe.wait_ge(O["hid_set"], j + 1)
                    turn_h(O["hT_full"])
                    pe.wait_ge(O["h_lo_set"], j + 1)
                    down(O["down_full"], split)

                pe.wait_ge(M["y_set"], EXPERTS)
                further_blocks(pe, further)

            @block.gpsimd
            def _(pool):
                own = E.sem("route_pool")
                nc.gpsimd.memset(before[:], 1.0).then_inc(own, 1)
                pool.wait_ge(own, 1)
                nc.gpsimd.affine_select(out=before[:], in_=before[:], compare_op=ALU.is_gt, fill=0.0, base=0,
                                        pattern=[[1, P]], channel_multiplier=-1).then_inc(own, 1)
                nc.gpsimd.iota(iota_j[:], pattern=[[1, P]], base=0, channel_multiplier=0,
                               allow_small_or_imprecise_dtypes=True).then_inc(own, 1)
                nc.gpsimd.iota(e128[:], pattern=[[P, EXPERTS]], base=0, channel_multiplier=0,
                               allow_small_or_imprecise_dtypes=True).then_inc(own, 1)
                nc.gpsimd.iota(token_id[:], pattern=[[P, NT]], base=0, channel_multiplier=1,
                               allow_small_or_imprecise_dtypes=True).then_inc(own, 1)
                pool.wait_ge(own, 5)
                pool.sem_inc(R["consts"], 1)
                pool.wait_ge(R["idx"], 1)
                gather = lambda to, b: nc.gpsimd.indirect_dma_start(to, None, normed[:, :], bass.IndirectOffsetOnAxis(ap=idx[:, b:b + 1], axis=0))
                for b in range(EXPERTS + 1):
                    if b < EXPERTS:
                        if b >= 2:
                            pool.wait_ge(M["xT_full"], 2 * (b - 1))
                        gather(xg[b % 2][:], b).then_inc(xg_in[b % 2], 16)
                    if b >= 1:
                        pool.wait_ge(hi_set["u1"], b)
                        nc.gpsimd.tensor_tensor(w_lo["u1"][:], land["u1"][:], w_hi["u1"][:].bitcast(F32), ALU.subtract).then_inc(lo_set["u1"], 1)
                pool.wait_ge(M["xT_full"], 2 * EXPERTS)
                pool.wait_ge(R["over"], 1)
                filled = pool.value_load(n_over[0:1, 0:1], min_val=0, max_val=OVER)
                for j in range(OVER):
                    with pool.If(filled > j):
                        if j >= 1:
                            pool.wait_ge(O["xT_full"], 2 * j)
                        gather(xg[0][:], EXPERTS + j).then_inc(O["xg_landed"], 16)

            @block.scalar
            def _(act):
                act.wait_ge(R["gsub"], 1)
                nc.scalar.activation(gexp[:], gexp[:], ACT.Exp).then_inc(R["gexp"], 1)
                act.wait_ge(R["ssub"], 1)
                nc.scalar.activation(sexp[:], sexp[:], ACT.Exp).then_inc(R["sexp"], 1)

                free = {x: M["gate_full"] if x[0] == "g" else M["up_full"] for x in UP_PIECES}

                def hi(x, b):
                    if x in free:
                        need(act, free[x], b)
                    else:
                        need(act, M["down_full"], b * 2)
                    act.wait_ge(landed[x], b * 16 + 16)
                    nc.scalar.copy(w_hi[x][:], land[x][:]).then_inc(hi_set[x], 1)

                def hi_x(b):
                    act.wait_ge(M["xm_set"], b + 1)
                    nc.scalar.copy(x_hi[:], xm[:]).then_inc(M["x_hi_set"], 1)

                for x in UP_PIECES:
                    hi(x, 0)
                hi_x(0)

                def step(b, s):
                    more = not (isinstance(b, int) and b + 1 >= EXPERTS)
                    act.wait_ge(M["gate_full"], b + 1)
                    need(act, M["hid_set"], b)
                    nc.scalar.activation(act_[:], gate_b[:], ACT.Silu).then_inc(M["act_set"], 1)
                    if more:
                        hi("g0", b + 1)
                        hi("g1", b + 1)
                        hi_x(b + 1)
                        hi("u0", b + 1)
                        hi("u1", b + 1)
                    hi("d0", b)
                    hi("d1", b)
                    act.wait_ge(M["hT_full"], b + 1)
                    nc.scalar.copy(h_hi[:], hT_b.rearrange("p (c n) -> p c n", n=P)).then_inc(M["h_hi_set"], 1)

                blocks_in_turn(act, step)

                def further(j):
                    for n, x in enumerate(PIECES):
                        act.wait_ge(landed[x], j * 16 + 16 * (EXPERTS + 1))
                        nc.scalar.copy(w_hi[x][:], land[x][:]).then_inc(O["hi_set"], 1)
                    act.wait_ge(O["xm_set"], j + 1)
                    nc.scalar.copy(x_hi[:], xm[:]).then_inc(O["x_hi_set"], 1)
                    act.wait_ge(O["gate_full"], j + 1)
                    nc.scalar.activation(act_[:], gate_b[:], ACT.Silu).then_inc(O["act_set"], 1)
                    act.wait_ge(O["hT_full"], j + 1)
                    nc.scalar.copy(h_hi[:], hT_b.rearrange("p (c n) -> p c n", n=P)).then_inc(O["h_hi_set"], 1)

                act.wait_ge(M["down_full"], 2 * EXPERTS)
                further_blocks(act, further)

            @block.vector
            def _(dve):
                link = Chain(E.dve_chain)
                link.n = E.chain_n
                V = nc.vector
                logits = E.logits
                gl = logits[:, :, 0:N_GROUPS]
                el = logits[:, :, N_GROUPS:NR].rearrange("p t (g e) -> p t g e", g=N_GROUPS)
                each = lambda ap, n: ap.rearrange("p (t o) -> p t o", o=1).broadcast_to([P, NT, n])
                over_t = lambda ap, n: ap.rearrange("p (o n) -> p o n", o=1).broadcast_to([P, NT, n])

                def first_max(values, marks, one, n, top):
                    link(dve, V.tensor_reduce(top[:], values, X, ALU.max))
                    link(dve, V.tensor_tensor(marks, values, each(top[:], n), ALU.is_lt))
                    link(dve, V.scalar_tensor_tensor(marks, marks, float(n), over_t(iota_j[:, 0:n], n), ALU.mult, ALU.add))
                    link(dve, V.tensor_reduce(first[:], marks, X, ALU.min))
                    link(dve, V.tensor_tensor(one, over_t(iota_j[:, 0:n], n), each(first[:], n), ALU.is_equal))

                dve.wait_ge(R["consts"], 1)
                link(dve, V.tensor_reduce(best[:], gl, X, ALU.max))
                V.tensor_tensor(gexp[:], gl, each(best[:], N_GROUPS), ALU.subtract).then_inc(R["gsub"], 1)
                dve.wait_ge(R["gexp"], 1)
                first_max(gexp[:], geq[:], gone[:], N_GROUPS, top1)
                link(dve, V.tensor_reduce(den[:], gexp[:], X, ALU.add))
                link(dve, V.reciprocal(den[:], den[:]))
                link(dve, V.tensor_tensor(gprob[:], top1[:], den[:], ALU.mult))
                wide_g = gone[:].rearrange("p t (g o) -> p t g o", o=1).broadcast_to([P, NT, N_GROUPS, PER_GROUP])
                p4 = lambda x: x.rearrange("p t (g e) -> p t g e", g=N_GROUPS)
                link(dve, V.tensor_tensor(p4(pick[:]), el, wide_g, ALU.mult))
                link(dve, V.tensor_reduce(sel[:], pick[:].rearrange("p t (g e) -> p t e g", g=N_GROUPS), X, ALU.add))
                link(dve, V.tensor_reduce(best[:], sel[:], X, ALU.max))
                V.tensor_tensor(sexp[:], sel[:], each(best[:], PER_GROUP), ALU.subtract).then_inc(R["ssub"], 1)
                dve.wait_ge(R["sexp"], 1)
                first_max(sexp[:], seq[:], one1[:], PER_GROUP, top1)
                link(dve, V.scalar_tensor_tensor(sexp[:], one1[:], -2.0, sexp[:], ALU.mult, ALU.add))
                first_max(sexp[:], seq[:], one2[:], PER_GROUP, top2)
                link(dve, V.tensor_tensor(den[:], top1[:], top2[:], ALU.add))
                link(dve, V.reciprocal(den[:], den[:]))
                link(dve, V.tensor_tensor(den[:], den[:], gprob[:], ALU.mult))
                link(dve, V.tensor_tensor(E.weight[0][:], den[:], top1[:], ALU.mult))
                link(dve, V.tensor_tensor(E.weight[1][:], den[:], top2[:], ALU.mult))
                for one8, one32 in ((one1, one32a), (one2, one32b)):
                    wide_e = one8[:].rearrange("p t (o e) -> p t o e", o=1).broadcast_to([P, NT, N_GROUPS, PER_GROUP])
                    link(dve, V.tensor_tensor(p4(one32[:]), wide_g, wide_e, ALU.mult))
                V.tensor_tensor(both[:], one32a[:], one32b[:], ALU.add).then_inc(R["both"], 1)
                dve.wait_ge(R["ranks"], 1)
                n32 = NT * EXPERTS
                link(dve, V.memset(base[:, 0, :], 0.0))
                for t in range(NT):
                    link(dve, V.tensor_tensor(base[:, t + 1, :], base[:, t, :], rank_b[:, n32 + t * EXPERTS:n32 + (t + 1) * EXPERTS], ALU.add))
                link(dve, V.tensor_tensor(place[:], rank_b[:, 0:n32].rearrange("p (t e) -> p t e", t=NT), base[:, 0:NT, :], ALU.add))
                count = base[:, NT, :]
                link(dve, V.tensor_scalar(nover[:], count, float(P), None, ALU.is_gt))
                for j in range(2, S // P):
                    link(dve, V.scalar_tensor_tensor(nover[:], count, float(j * P), nover[:], ALU.is_gt, ALU.add))
                link(dve, V.tensor_tensor_scan(upto[:], E.ones[:, 0:EXPERTS], nover[:], 0.0, ALU.mult, ALU.add))
                link(dve, V.tensor_tensor(over_at[:], upto[:], nover[:], ALU.subtract))
                link(dve, V.tensor_scalar(over_at[:], over_at[:], float(P), float((EXPERTS - 1) * P), ALU.mult, ALU.add))
                link(dve, V.tensor_tensor(over_at[:], over_at[:], e128[:], ALU.subtract))
                for k, one32 in enumerate((one32a, one32b)):
                    link(dve, V.tensor_tensor(pick[:], one32[:], place[:], ALU.mult))
                    link(dve, V.tensor_reduce(at[:], pick[:], X, ALU.add))
                    link(dve, V.tensor_tensor(pick[:], one32[:], over_t(over_at[:], EXPERTS), ALU.mult))
                    link(dve, V.tensor_reduce(over[:], pick[:], X, ALU.add))
                    link(dve, V.scalar_tensor_tensor(over[:], at[:], float(P), over[:], ALU.is_ge, ALU.mult))
                    link(dve, V.tensor_tensor(at[:], at[:], over[:], ALU.add))
                    link(dve, V.tensor_tensor(pick[:], one32[:], over_t(e128[:], EXPERTS), ALU.mult))
                    link(dve, V.tensor_reduce(over[:], pick[:], X, ALU.add))
                    link(dve, V.tensor_tensor(at[:], at[:], over[:], ALU.add))
                    link(dve, V.tensor_copy(E.slot[k][:], at[:]))
                    V.tensor_scalar(part_i[:], E.slot[k][:], P - 1, None, ALU.bitwise_and)
                    link(dve, V.tensor_scalar(block_i[:], E.slot[k][:], P.bit_length() - 1, None, ALU.logical_shift_right))
                    V.tensor_copy(part[:], part_i[:])
                    link(dve, V.tensor_copy(block_f[:], block_i[:]))
                    V.tensor_tensor(at_part[k], over_t(iota_j[:], P), each(part[:], P), ALU.is_equal)
                    link(dve, V.tensor_tensor(at_block[k][:], over_t(iota_j[:, 0:BLOCKS], BLOCKS), each(block_f[:], BLOCKS), ALU.is_equal))
                    ins = V.tensor_tensor(at_block[k][:], at_block[k][:], each(token_id[:], BLOCKS), ALU.mult)
                    if k == 0:
                        link(dve, ins)
                ins.then_inc(R["places"], 1)
                dve.wait_ge(R["table"], 1)
                V.tensor_copy(idx[:], rank_b[:, 0:BLOCKS]).then_inc(R["idx"], 1)
                link(dve, V.tensor_tensor(ovcmp[:], upto[:].rearrange("p (o e) -> p o e", o=1).broadcast_to([P, OVER + 1, EXPERTS]),
                                          iota_j[:, 0:OVER + 1].rearrange("p (j o) -> p j o", o=1).broadcast_to([P, OVER + 1, EXPERTS]), ALU.is_le))
                link(dve, V.tensor_reduce(ovexp[:], ovcmp[:], X, ALU.add))
                link(dve, V.tensor_scalar(ovexp[:], ovexp[:], float(EXPERTS - 1), None, ALU.min))
                link(dve, V.tensor_copy(ovexp_i[:], ovexp[:]))
                V.tensor_copy(n_over[:], upto[:, EXPERTS - 1:EXPERTS]).then_inc(R["over"], 1)

                def lo(x, b):
                    dve.wait_ge(hi_set[x], b + 1)
                    V.tensor_tensor(w_lo[x][:], land[x][:], w_hi[x][:].bitcast(F32), ALU.subtract).then_inc(lo_set[x], 1)

                def modulate(m, b):
                    for h in range(2):
                        dve.wait_ge(m["xT_full"], b * 2 + h + 1)
                        for c in range(4):
                            k = 4 * h + c
                            last = V.tensor_scalar(xm[:, k, :], xT_b[h][:, c * P:(c + 1) * P], scale[:, k:k + 1], shift[:, k:k + 1], ALU.mult, ALU.add)
                    last.then_inc(m["xm_set"], 1)
                    dve.wait_ge(m["x_hi_set"], b + 1)
                    V.tensor_tensor(x_lo[:], xm[:], x_hi[:].bitcast(F32), ALU.subtract).then_inc(m["x_lo_set"], 1)

                def lo_h(m, b):
                    dve.wait_ge(m["h_hi_set"], b + 1)
                    V.tensor_tensor(h_lo[:], hT_b.rearrange("p (c n) -> p c n", n=P), h_hi[:].bitcast(F32), ALU.subtract).then_inc(m["h_lo_set"], 1)

                def results(m, b, s):
                    dve.wait_ge(m["down_full"], b * 2 + 2)
                    if m is M:
                        need(dve, y_out[s], (b - s) * 8)
                    V.tensor_tensor(yb[s][:], down_rows, gate[:], ALU.mult).then_inc(m["y_set"], 1)

                dve.wait_ge(gate_landed, 16)
                for x in UP_PIECES[0:3]:
                    lo(x, 0)
                modulate(M, 0)

                def step(b, s):
                    more = not (isinstance(b, int) and b + 1 >= EXPERTS)
                    if more:
                        lo("g0", b + 1)
                        lo("g1", b + 1)
                    dve.wait_ge(M["up_full"], b + 1)
                    dve.wait_ge(M["act_set"], b + 1)
                    need(dve, M["hT_full"], b)
                    V.tensor_tensor(hid[:], act_[:], up_b[:], ALU.mult).then_inc(M["hid_set"], 1)
                    if more:
                        modulate(M, b + 1)
                        lo("u0", b + 1)
                    if not (isinstance(b, int) and b == 0):
                        results(M, b - 1, 1 - s)
                    lo("d0", b)
                    lo("d1", b)
                    lo_h(M, b)

                blocks_in_turn(dve, step)
                results(M, EXPERTS - 1, 1)
                dve.wait_ge(y_out[0], 16 * (EXPERTS // 2))

                def further(j):
                    for n, x in enumerate(PIECES):
                        dve.wait_ge(O["hi_set"], j * len(PIECES) + n + 1)
                        V.tensor_tensor(w_lo[x][:], land[x][:], w_hi[x][:].bitcast(F32), ALU.subtract).then_inc(O["lo_set"], 1)
                    modulate(O, j)
                    dve.wait_ge(O["up_full"], j + 1)
                    dve.wait_ge(O["act_set"], j + 1)
                    V.tensor_tensor(hid[:], act_[:], up_b[:], ALU.mult).then_inc(O["hid_set"], 1)
                    lo_h(O, j)
                    results(O, j, 0)

                further_blocks(dve, further)
                E.chain_n = link.n


def stage_combine(nc, E, A, rows_in, y_slots):
    with ExitStack() as st:
        sb = lambda name, shape, dt=F32: E.sb(name, shape, dt, ctx=st)
        N = 3
        y = [[sb(f"cy{k}_{i}", [P, D]) for i in range(N)] for k in range(TOP_K)]
        x = [sb(f"cx{i}", [P, D]) for i in range(N)]
        sq = sb("c_sq", [P, D])
        gain = sb("final_gain", [P, D])
        ss, dev, inv = (sb(n, [P, NT]) for n in ("c_ss", "c_dev", "c_inv"))
        rows_landed = E.sem("c_rows")
        x_in, y_in = ([E.sem(f"{n}{i}") for i in range(N)] for n in ("cx_landed", "cy_landed"))
        weighted, summed, scaled, sq_set, dev_set, ready = (E.sem("c_" + n) for n in ("weighted", "summed", "scaled", "sq_set", "dev_set", "ready"))
        with nc.Block() as block:

            @block.sync
            def _(sp):
                sp.dma_start(gain[:], A["final_norm_g_2"].rearrange("(o d) -> o d", o=1).broadcast_to([P, D])).then_inc(rows_landed, 16)

                def load(t):
                    sp.dma_start(x[t % N][:], rows_in[t * P:(t + 1) * P, :]).then_inc(x_in[t % N], 16)

                for t in range(N):
                    load(t)
                for t in range(NT):
                    sp.wait_ge(ready, t + 1)
                    sp.dma_start(A["out"][0, t * P:(t + 1) * P, :], x[t % N][:]).then_inc(E.out_stored, 16)
                    if t + N < NT:
                        sp.wait_ge(E.out_stored, 16 * (t + 1))
                        load(t + N)
                sp.wait_ge(E.out_stored, 16 * NT)

            @block.gpsimd
            def _(pool):
                for t in range(NT):
                    if t >= N:
                        pool.wait_ge(summed, t - N + 1)
                    for k in range(TOP_K):
                        nc.gpsimd.indirect_dma_start(y[k][t % N][:], None, y_slots[:, :],
                                                     bass.IndirectOffsetOnAxis(ap=E.slot[k][:, t:t + 1], axis=0)).then_inc(y_in[t % N], 16)

            @block.scalar
            def _(act):
                for t in range(NT + 1):
                    if t < NT:
                        act.wait_ge(y_in[t % N], 32 * (t // N + 1))
                        nc.scalar.activation(y[0][t % N][:], y[0][t % N][:], ACT.Copy, scale=E.weight[0][:, t:t + 1]).then_inc(weighted, 1)
                    if t >= 1:
                        act.wait_ge(scaled, t)
                        nc.scalar.activation(sq[:], x[(t - 1) % N][:], ACT.Square, accum_out=ss[:, t - 1:t]).then_inc(sq_set, 1)
                        act.wait_ge(sq_set, t)
                        nc.scalar.activation(dev[:, t - 1:t], ss[:, t - 1:t], ACT.Sqrt, bias=E.eps_rms[:], scale=1.0 / D).then_inc(dev_set, 1)

            @block.vector
            def _(dve):
                link = Chain(E.dve_chain)
                link.n = E.chain_n
                V = nc.vector
                dve.wait_ge(rows_landed, 16)
                for t in range(NT + 1):
                    if t < NT:
                        y0, y1, xt = y[0][t % N][:], y[1][t % N][:], x[t % N][:]
                        dve.wait_ge(weighted, t + 1)
                        link(dve, V.scalar_tensor_tensor(y0, y1, E.weight[1][:, t:t + 1], y0, ALU.mult, ALU.add))
                        dve.wait_ge(x_in[t % N], 16 * (t // N + 1))
                        V.tensor_tensor(xt, xt, y0, ALU.add).then_inc(scaled, 1)
                        dve.wait_ge(scaled, t + 1)
                        dve.sem_inc(summed, 1)
                    if t >= 1:
                        b = slice(t - 1, t)
                        dve.wait_ge(dev_set, t)
                        link(dve, V.reciprocal(inv[:, b], dev[:, b]))
                        V.scalar_tensor_tensor(x[(t - 1) % N][:], x[(t - 1) % N][:], inv[:, b], gain[:], ALU.mult, ALU.mult).then_inc(ready, 1)
                E.chain_n = link.n


def build_program(nc, A):
    with ExitStack() as ctx:
        E = Env(nc, ctx)
        E.psum = ctx.enter_context(nc.psum_tensor("psum", [P, 8 * HALF], F32))
        E.banks = [E.psum[:, i * HALF:(i + 1) * HALF] for i in range(8)]
        E.dve_chain = E.sem("dve_chain")
        E.chain_n = 0
        E.kv_landed = [E.sem(f"mkv_landed{i}") for i in range(2)]
        E.out_stored = E.sem("out_stored")
        E.ncum_rows = nc.dram_tensor("ncum_rows", (FOX_HEADS, S), F32, kind="Internal").ap()
        x1_rows = nc.dram_tensor("x1_rows", (S, D), F32, kind="Internal").ap()
        x2_rows = nc.dram_tensor("x2_rows", (S, D), F32, kind="Internal").ap()
        x3_rows = nc.dram_tensor("x3_rows", (S, D), F32, kind="Internal").ap()
        n3_rows = nc.dram_tensor("n3_rows", (S, D), F32, kind="Internal").ap()
        y_slots = nc.dram_tensor("y_slots", (SLOTS, D), F32, kind="Internal").ap()
        x0_rows = A["x"].rearrange("o t d -> (o t) d")
        E.ident = E.sb("ident", [P, P])
        E.ones = E.sb("ones", [P, P])
        E.eps_ln = E.sb("eps_ln", [P, 1])
        E.eps_rms = E.sb("eps_rms", [P, 1])
        E.eps_gn = E.sb("eps_gn", [P, 1])
        E.mod = E.sb("mod", [P, 6 * ND])
        E.causal = E.sb("causal", [P, P])
        E.icount = E.sb("icount", [P, len(POOL_WINDOWS), PAD])
        E.pool_scale = E.sb("pool_scale", [P, ND])
        E.b_forget = E.sb("b_forget_col", [FOX_HEADS, 1])
        E.gates = nc.dram_tensor("gate_rows_dram", (P, 2 * D), F32, kind="Internal").ap()
        E.v_dram, E.yi_dram = (nc.dram_tensor(x, (P, NT, RW), F32, kind="Internal").ap() for x in ("v_rows", "yi_rows"))
        E.mt_dram, E.n_dram, E.qt_dram = (nc.dram_tensor(x, (P, NPAIR * S), F32, kind="Internal").ap() for x in ("mt", "n", "qt"))
        E.n_small, E.n_masks = 11, 1
        far = lambda name, st: E.sb(name, [P, ND, S], ctx=st, side="right")
        halves = lambda name, st: [E.sb(name + n, [P, ND, S], F32R, ctx=st) for n in ("_hi", "_lo")]
        with ExitStack() as first:
            E.yT = E.sb("yT", [P, NY, S], ctx=first)
            with ExitStack() as memory:
                E.memT = E.sb("memT", [P, ND, N_MEM], ctx=memory)
                E.mkT = E.sb("mkT", [P, MEM_HEADS, N_MEM], ctx=memory)
                E.mv = E.sb("mv", [P, NM, HALF], ctx=memory)
                with ExitStack() as whole:
                    E.xT = far("x0T", whole)
                    kv = ExitStack()
                    E.kv_w = [E.sb(f"mkv_w{i}", [P, ND, HALF], ctx=kv, side="right") for i in range(2)]
                    E.run(stage_constants, A)
                    split = ExitStack()
                    E.x_hi, E.x_lo = halves("x0", split)
                    E.run(stage_memory_kv, A)
                    kv.close()
                with split:
                    E.run(stage_layer0, A)
                whole = ExitStack()
                E.xT = far("x1T", whole)
                E.run(stage_out, A, 0, x0_rows, x1_rows)
                E.run(stage_memory_and_gates, A, 1)
            with ExitStack() as split:
                with whole:
                    E.x_hi, E.x_lo = halves("x1", split)
                    E.run(stage_split_x, A)
                E.run(stage_fox, A)
            modulated = ExitStack()
            E.xT = far("hT", modulated)
            E.run(stage_out, A, 1, x1_rows, x2_rows, modulate=True)
        E.logits = E.sb("logits", [P, NT, N_GROUPS + EXPERTS])
        with ExitStack() as second:
            E.bonus = E.sb("bonus", [P, NT, 2 * NPAIR], ctx=second)
            E.carry = E.sb("carry", [P, NPAIR, NC], ctx=second)
            E.ident2 = E.sb("ident2", [P, HD], ctx=second)
            E.xg = E.sb("xg", [GATE_LORA, S], ctx=second)
            E.hT = E.xT
            E.run(stage_rwkv_pairs, A)
            E.run(stage_mix, A, x2_rows, x3_rows, n3_rows, y_slots)
        modulated.close()
        with ExitStack() as third:
            E.slot = [E.sb(f"slot{k}", [P, NT], I32, ctx=third) for k in range(TOP_K)]
            E.weight = [E.sb(f"weight{k}", [P, NT], ctx=third) for k in range(TOP_K)]
            E.run(stage_experts, A, n3_rows, y_slots)
            E.run(stage_combine, A, x3_rows, y_slots)


COLUMNS = ("pool_scale", "c_2", "ada_b_2", "norm1_g_2", "norm2_g_2", "rwkv_w0_2", "rwkv_a0_2", "rwkv_k_k_2", "rwkv_k_a_2", "rwkv_r_k_2")


def kernel(**inputs):
    import numpy as _np
    import concourse.bacc as _bacc
    from concourse import mybir as _mybir
    from concourse.bass_utils import run_bass_kernel_spmd as _run

    nc = _bacc.Bacc("TRN2", target_bir_lowering=False, num_devices=1)
    arrays, A = {}, {}
    for name in COLUMNS:
        if name in inputs:
            inputs[name + "_cols"] = _np.asarray(inputs[name]).reshape(-1, P).T
    mu = _np.asarray(inputs["rwkv_mu_2"]).reshape(-1)
    inputs["mu_main_cols"] = mu[:3 * RW].reshape(-1, P).T
    inputs["mu_w_col"], inputs["mu_a_col"], inputs["mu_g_col"] = (
        mu[a:b].reshape(-1, 1) for a, b in ((3 * RW, 3 * RW + LORA), (3 * RW + LORA, 3 * RW + 2 * LORA), (3 * RW + 2 * LORA, None)))
    inputs["gmlp_bs_cols"] = _np.asarray(inputs["gmlp_bs_2"])[0].T
    for name, a in inputs.items():
        a = _np.ascontiguousarray(a)
        arrays[f"in_{name}"] = a
        A[name] = nc.dram_tensor(f"in_{name}", a.shape, _mybir.dt.from_np(a.dtype), kind="ExternalInput").ap()
    A["out"] = nc.dram_tensor("result", (1, S, D), F32, kind="ExternalOutput").ap()
    build_program(nc, A)
    r = _run(nc, [arrays], core_ids=[0])
    return r.results[0]["result"]
```
